# Optimizing a Trainium2 kernel written in Bass

```python
import math, functools
import jax, jax.numpy as jnp
from jax import lax
import numpy as np

D_MODEL = 1024
BATCH = 1
SEQ = 512
DEPTH = 2
DEC_BATCH = 8
DEC_SEQ = 1
PAST_LEN = 4096
PAGE_SIZE = 128

D_MIX = D_MODEL
D_A = D_MIX // 4
A_BLOCKS = 4
A_BLK = D_A // A_BLOCKS
CONV_W = 4
RGLRU_C = 8.0
B_HEADS = 4
B_DK = D_MIX // 16
B_DV = B_DK
D_B = B_HEADS * B_DK
C_HEADS = 4
C_DK = D_MIX // 8
C_DV = C_DK
D_C = C_HEADS * C_DK
PROJ_WIDTHS = (D_A, D_A, D_B, D_B, D_B, D_B, D_C, D_C, D_C, D_C)
D_IN = D_A * 2 + D_B * 4 + D_C * 4
B_CHUNK = 64
C_CHUNK = 128
ROPE_BASE = 10000.0
N_EXPERTS = 16
N_GROUPS = 4
EXP_PER_GROUP = N_EXPERTS // N_GROUPS
TOP_K = 2
D_EXPERT = D_MODEL // 2
LN_EPS = 1e-5
RMS_EPS = 1e-6
GN_EPS = 1e-6
F_TINY = 1e-30
ALPHA = (2 * DEPTH) ** 0.25
BETA = (8 * DEPTH) ** -0.25

kernel_name = "hybrid_rglru_hgrn2_retention_moe_step"

def _split_points():
    pts, acc = [], 0
    for w in PROJ_WIDTHS[:-1]:
        acc += w
        pts.append(acc)
    return pts

def _layernorm(x, g, b):
    xf = x.astype(jnp.float32)
    mu = xf.mean(-1, keepdims=True)
    var = jnp.square(xf - mu).mean(-1, keepdims=True)
    return ((xf - mu) * lax.rsqrt(var + LN_EPS) * g + b).astype(x.dtype)

def _linear_combine(c1, c2):
    a1, b1 = c1
    a2, b2 = c2
    return a1 * a2, a2 * b1 + b2

def _chunked_scan(step, S0, xs, chunk):
    Bn, T = xs[0].shape[:2]
    ch = chunk if T % chunk == 0 else T
    n = T // ch
    xs_c = tuple(jnp.moveaxis(a.reshape((Bn, n, ch) + a.shape[2:]), 1, 0) for a in xs)
    S, out = lax.scan(lambda S, c: step(S, *c), S0, xs_c)
    out = jnp.moveaxis(out, 0, 1).reshape((Bn, T) + out.shape[3:])
    return out, S

def _rotary(x, pos):
    half = x.shape[-1] // 2
    inv = ROPE_BASE ** (-jnp.arange(half, dtype=jnp.float32) / half)
    ang = pos.astype(jnp.float32)[:, None] * inv[None]
    cos = jnp.cos(ang)[None, :, None, :]
    sin = jnp.sin(ang)[None, :, None, :]
    x1, x2 = x[..., :half], x[..., half:]
    return jnp.concatenate([x1 * cos - x2 * sin, x2 * cos + x1 * sin], axis=-1)

def _rglru_mixer(xa, ga, conv0, h0, conv_w, conv_b, w_r, b_r, w_i, b_i, lam):
    f32 = jnp.float32
    Bn, T, _ = xa.shape
    xp = jnp.concatenate([conv0.astype(xa.dtype), xa], axis=1)
    u = conv_b + xp[:, 0:T] * conv_w[0]
    for j in range(1, CONV_W):
        u = u + xp[:, j:j + T] * conv_w[j]
    conv_new = xp[:, T:]
    ub = u.reshape(Bn, T, A_BLOCKS, A_BLK)
    r = jax.nn.sigmoid(jnp.einsum('btgi,gij->btgj', ub, w_r) + b_r).reshape(Bn, T, D_A).astype(f32)
    i = jax.nn.sigmoid(jnp.einsum('btgi,gij->btgj', ub, w_i) + b_i).reshape(Bn, T, D_A).astype(f32)
    log_a = RGLRU_C * r * jax.nn.log_sigmoid(lam.astype(f32))
    a = jnp.exp(log_a)
    bterm = jnp.sqrt(jnp.maximum(-jnp.expm1(2.0 * log_a), 0.0)) * (i * u.astype(f32))
    bterm = bterm.at[:, 0].add(a[:, 0] * h0.astype(f32))
    _, h = lax.associative_scan(_linear_combine, (a, bterm), axis=1)
    ya = (h * jax.nn.gelu(ga.astype(f32))).astype(xa.dtype)
    return ya, h[:, -1], conv_new

def _hgrn2_chunk(S, q, logf, k, v):
    L = q.shape[1]
    b = jnp.cumsum(logf, axis=1)
    causal = jnp.tril(jnp.ones((L, L), dtype=bool))[None, :, :, None, None]
    diff = b[:, :, None] - b[:, None, :]
    decay = jnp.where(causal, jnp.exp(jnp.where(causal, diff, 0.0)), 0.0)
    scores = jnp.sum(q[:, :, None] * k[:, None] * decay, axis=-1)
    o = jnp.einsum('btsh,bshv->bthv', scores, v) + jnp.einsum('bthk,bhkv->bthv', q * jnp.exp(b), S)
    bL = b[:, -1]
    S_new = jnp.exp(bL)[..., None] * S + jnp.einsum('bshk,bshv->bhkv', k * jnp.exp(bL[:, None] - b), v)
    return S_new, o

def _hgrn2_mixer(qb, fb, vb, gb, S0, lb, norm_g):
    f32 = jnp.float32
    Bn, T, _ = qb.shape
    shp = (Bn, T, B_HEADS, B_DK)
    fl = fb.astype(f32)
    q = jax.nn.silu(qb.astype(f32)).reshape(shp)
    f = lb + (1.0 - lb) * jax.nn.sigmoid(fl)
    logf = jnp.log(jnp.maximum(f, F_TINY)).reshape(shp)
    k = ((1.0 - lb) * jax.nn.sigmoid(-fl)).reshape(shp)
    v = vb.astype(f32).reshape(Bn, T, B_HEADS, B_DV)
    o, S = _chunked_scan(_hgrn2_chunk, S0.astype(f32), (q, logf, k, v), B_CHUNK)
    o = o * lax.rsqrt(jnp.mean(o * o, axis=-1, keepdims=True) + RMS_EPS) * norm_g
    y = o.reshape(Bn, T, D_B) * jax.nn.silu(gb.astype(f32))
    return y.astype(qb.dtype), S

def _retention_chunk(S, q, k, v, log_gamma):
    L = q.shape[1]
    idx = jnp.arange(L, dtype=jnp.float32)
    rel = idx[:, None] - idx[None, :]
    mask = (rel >= 0)[None]
    D = jnp.where(mask, jnp.exp(jnp.where(mask, rel[None], 0.0) * log_gamma[:, None, None]), 0.0)
    scores = jnp.einsum('bthk,bshk->bhts', q, k) * D[None]
    q_dec = jnp.exp((idx + 1.0)[:, None] * log_gamma[None])
    k_dec = jnp.exp((L - 1.0 - idx)[:, None] * log_gamma[None])
    o = jnp.einsum('bhts,bshv->bthv', scores, v) + jnp.einsum('bthk,bhkv->bthv', q * q_dec[None, :, :, None], S)
    S_new = jnp.exp(L * log_gamma)[None, :, None, None] * S + jnp.einsum('bshk,bshv->bhkv', k * k_dec[None, :, :, None], v)
    return S_new, o

def _retention_mixer(qc, kc, vc, gc, pos, S0):
    f32 = jnp.float32
    Bn, T, _ = qc.shape
    shp = (Bn, T, C_HEADS, C_DK)
    q = _rotary(qc.astype(f32).reshape(shp), pos)
    k = _rotary(kc.astype(f32).reshape(shp), pos) * (C_DK ** -0.5)
    v = vc.astype(f32).reshape(Bn, T, C_HEADS, C_DV)
    log_gamma = jnp.log1p(-jnp.exp2(-5.0 - jnp.arange(C_HEADS, dtype=f32)))
    step = functools.partial(_retention_chunk, log_gamma=log_gamma)
    o, S = _chunked_scan(step, S0.astype(f32), (q, k, v), C_CHUNK)
    mu = o.mean(-1, keepdims=True)
    var = jnp.square(o - mu).mean(-1, keepdims=True)
    o = (o - mu) * lax.rsqrt(var + GN_EPS)
    y = o.reshape(Bn, T, D_C) * jax.nn.silu(gc.astype(f32))
    return y.astype(qc.dtype), S

def _moe(x, router_w, router_b, wg, wu, wd):
    Bn, T, D = x.shape
    xt = x.reshape(Bn * T, D)
    logits = (xt @ router_w + router_b).astype(jnp.float32)
    probs = jax.nn.softmax(logits, axis=-1)
    pg = probs.reshape(-1, N_GROUPS, EXP_PER_GROUP)
    group_score = lax.top_k(pg, TOP_K)[0].sum(-1)
    g_sel = jnp.argmax(group_score, axis=-1)
    in_group = jnp.take_along_axis(pg, g_sel[:, None, None], axis=1)[:, 0]
    vals, idx = lax.top_k(in_group, TOP_K)
    gates = vals / vals.sum(-1, keepdims=True)
    expert_idx = g_sel[:, None] * EXP_PER_GROUP + idx
    combine = jnp.sum(jax.nn.one_hot(expert_idx, N_EXPERTS, dtype=jnp.float32) * gates[..., None], axis=1)
    h = jax.nn.silu(jnp.einsum('nd,edf->nef', xt, wg)) * jnp.einsum('nd,edf->nef', xt, wu)
    y = jnp.einsum('nef,efd->nd', h * combine[:, :, None].astype(h.dtype), wd)
    return y.reshape(Bn, T, D).astype(x.dtype)

def _trunk(x, pos, h0s, conv0s, sb0s, sc0s, params):
    (w_in, conv_w, conv_b, w_rgate, b_rgate, w_igate, b_igate, rglru_lambda,
     hgrn_lb_logits, hgrn_norm_g, w_out, ln1_g, ln1_b, router_w, router_b,
     exp_w_gate, exp_w_up, exp_w_down, ln2_g, ln2_b) = params
    s = jax.nn.softmax(hgrn_lb_logits.astype(jnp.float32), axis=0)
    lbs = jnp.cumsum(s, axis=0) - s[0]
    pts = _split_points()
    hs, convs, sbs, scs = [], [], [], []
    for l in range(DEPTH):
        proj = jnp.einsum('btd,de->bte', x, w_in[l])
        xa, ga, qb, fb, vb, gb, qc, kc, vc, gc = jnp.split(proj, pts, axis=-1)
        ya, h_new, conv_new = _rglru_mixer(xa, ga, conv0s[l], h0s[l], conv_w[l], conv_b[l],
                                           w_rgate[l], b_rgate[l], w_igate[l], b_igate[l], rglru_lambda[l])
        yb, sb_new = _hgrn2_mixer(qb, fb, vb, gb, sb0s[l], lbs[l], hgrn_norm_g[l])
        yc, sc_new = _retention_mixer(qc, kc, vc, gc, pos, sc0s[l])
        y_mix = jnp.einsum('bte,ed->btd', jnp.concatenate([ya, yb, yc], axis=-1), w_out[l])
        x = _layernorm(ALPHA * x + y_mix, ln1_g[l], ln1_b[l])
        x = _layernorm(ALPHA * x + _moe(x, router_w, router_b, exp_w_gate[l], exp_w_up[l], exp_w_down[l]),
                       ln2_g[l], ln2_b[l])
        hs.append(h_new)
        convs.append(conv_new)
        sbs.append(sb_new)
        scs.append(sc_new)
    return x, jnp.stack(hs), jnp.stack(convs), jnp.stack(sbs), jnp.stack(scs)

def setup_inputs(seed: int = 0) -> dict:
    key = jax.random.key(seed)
    ks = jax.random.split(key, 32)
    nrm = jax.random.normal
    f32 = jnp.float32
    u = jax.random.uniform(ks[13], (DEPTH, D_A), f32, 0.9, 0.999)
    a = u ** (1.0 / RGLRU_C)
    return {
        "x_prompt": nrm(ks[0], (BATCH, SEQ, D_MODEL), f32),
        "x_sample": nrm(ks[1], (DEC_BATCH, DEC_SEQ, D_MODEL), f32),
        "state_rglru_h": 0.5 * nrm(ks[2], (DEPTH, DEC_BATCH, D_A), f32),
        "state_conv": nrm(ks[3], (DEPTH, DEC_BATCH, CONV_W - 1, D_A), f32),
        "state_hgrn": 0.5 * nrm(ks[4], (DEPTH, DEC_BATCH, B_HEADS, B_DK, B_DV), f32),
        "state_ret": nrm(ks[5], (DEPTH, DEC_BATCH, C_HEADS, C_DK, C_DV), f32),
        "w_in": nrm(ks[6], (DEPTH, D_MODEL, D_IN), f32) * D_MODEL ** -0.5,
        "conv_w": nrm(ks[7], (DEPTH, CONV_W, D_A), f32) * CONV_W ** -0.5,
        "conv_b": 0.01 * nrm(ks[8], (DEPTH, D_A), f32),
        "w_rgate": nrm(ks[9], (DEPTH, A_BLOCKS, A_BLK, A_BLK), f32) * A_BLK ** -0.5,
        "b_rgate": 0.01 * nrm(ks[10], (DEPTH, A_BLOCKS, A_BLK), f32),
        "w_igate": nrm(ks[11], (DEPTH, A_BLOCKS, A_BLK, A_BLK), f32) * A_BLK ** -0.5,
        "b_igate": 0.01 * nrm(ks[12], (DEPTH, A_BLOCKS, A_BLK), f32),
        "rglru_lambda": jnp.log(a) - jnp.log1p(-a),
        "hgrn_lb_logits": 0.5 * nrm(ks[14], (DEPTH, D_B), f32),
        "hgrn_norm_g": 1.0 + 0.01 * nrm(ks[15], (DEPTH, B_DV), f32),
        "w_out": nrm(ks[16], (DEPTH, D_MIX, D_MODEL), f32) * (D_MIX ** -0.5 * BETA),
        "ln1_g": 1.0 + 0.01 * nrm(ks[17], (DEPTH, D_MODEL), f32),
        "ln1_b": 0.01 * nrm(ks[18], (DEPTH, D_MODEL), f32),
        "router_w": nrm(ks[19], (D_MODEL, N_EXPERTS), f32) * D_MODEL ** -0.5,
        "router_b": 0.01 * nrm(ks[20], (N_EXPERTS,), f32),
        "exp_w_gate": nrm(ks[21], (DEPTH, N_EXPERTS, D_MODEL, D_EXPERT), f32) * D_MODEL ** -0.5,
        "exp_w_up": nrm(ks[22], (DEPTH, N_EXPERTS, D_MODEL, D_EXPERT), f32) * D_MODEL ** -0.5,
        "exp_w_down": nrm(ks[23], (DEPTH, N_EXPERTS, D_EXPERT, D_MODEL), f32) * (D_EXPERT ** -0.5 * BETA),
        "ln2_g": 1.0 + 0.01 * nrm(ks[24], (DEPTH, D_MODEL), f32),
        "ln2_b": 0.01 * nrm(ks[25], (DEPTH, D_MODEL), f32),
    }

def reference(x_prompt, x_sample, state_rglru_h, state_conv, state_hgrn, state_ret,
              w_in, conv_w, conv_b, w_rgate, b_rgate, w_igate, b_igate, rglru_lambda,
              hgrn_lb_logits, hgrn_norm_g, w_out, ln1_g, ln1_b, router_w, router_b,
              exp_w_gate, exp_w_up, exp_w_down, ln2_g, ln2_b):
    params = (w_in, conv_w, conv_b, w_rgate, b_rgate, w_igate, b_igate, rglru_lambda,
              hgrn_lb_logits, hgrn_norm_g, w_out, ln1_g, ln1_b, router_w, router_b,
              exp_w_gate, exp_w_up, exp_w_down, ln2_g, ln2_b)
    f32 = jnp.float32
    Bp, Tp = x_prompt.shape[0], x_prompt.shape[1]
    z_h = jnp.zeros((DEPTH, Bp, D_A), f32)
    z_conv = jnp.zeros((DEPTH, Bp, CONV_W - 1, D_A), x_prompt.dtype)
    z_hgrn = jnp.zeros((DEPTH, Bp, B_HEADS, B_DK, B_DV), f32)
    z_ret = jnp.zeros((DEPTH, Bp, C_HEADS, C_DK, C_DV), f32)
    pos_p = jnp.arange(Tp, dtype=jnp.int32)
    pos_s = PAST_LEN + jnp.arange(x_sample.shape[1], dtype=jnp.int32)
    y_prompt, h_p, conv_p, hg_p, rt_p = _trunk(x_prompt, pos_p, z_h, z_conv, z_hgrn, z_ret, params)
    y_sample, h_s, conv_s, hg_s, rt_s = _trunk(x_sample, pos_s, state_rglru_h, state_conv,
                                               state_hgrn, state_ret, params)
    return (y_prompt, y_sample, h_p, h_s, conv_p, conv_s, hg_p, hg_s, rt_p, rt_s)


_drawn_inputs = setup_inputs


def setup_inputs(seed=0):
    import zlib

    import numpy as np

    out = dict(_drawn_inputs(seed))
    spreads = {}
    factors = {'b_rgate': 26.601, 'b_igate': 28.436, 'hgrn_norm_g': 8.0, 'ln2_g': 3.17, 'ln2_b': 3.248}
    for name, (base, spread) in spreads.items():
        noise = np.random.default_rng([zlib.crc32(name.encode()), seed]).standard_normal(out[name].shape)
        drawn = base * np.exp(spread * noise) if base else spread * noise
        out[name] = __import__('jax').numpy.asarray(drawn.astype(out[name].dtype))
    for name, factor in factors.items():
        out[name] = (out[name] * factor).astype(out[name].dtype)
    return out
```

```python
import numpy as np
import concourse.bass as bass
from concourse import mybir
from contextlib import ExitStack

D_MODEL, SEQ, DEPTH, DEC_BATCH, PAST_LEN = 1024, 512, 2, 8, 4096
P = 128
TOK = SEQ + DEC_BATCH
TILES = SEQ // P + 1
KC = D_MODEL // P
HALF = TOK // 2
D_A = D_B = 256
D_C = 512
CONV_W = 4
RGLRU_C = 8.0
DK_B, CHUNK_B = 64, 64
CHUNKS_B = SEQ // CHUNK_B
LEVELS = [32, 16, 8, 4, 2, 1]
C_HEADS, DK_C = 4, 128
N_EXPERTS, D_EXPERT = 16, 512
PAIRS = N_EXPERTS // 2
SLOTS = 128
PASSES = -(-TOK // SLOTS)
LN_EPS, RMS_EPS, GN_EPS, F_TINY = 1e-5, 1e-6, 1e-6, 1e-30
ALPHA = (2 * DEPTH) ** 0.25
COLS = dict(xa=0, ga=256, qb=512, fb=768, vb=1024, gb=1280, qc=1536, kc=2048, vc=2560, gc=3072)
F_SPLIT = 2.0 ** -60

UNIT = 1024
RAW_SLOTS, SPLIT_SLOTS = 6, 4
IN_PARTS = ["xa", "ga", "fb", "qb", "vb", "gb",
            "kc0", "qc0", "vc0", "gc0", "kc1", "qc1", "vc1", "gc1"]
MIX_UNITS = 2 * len(IN_PARTS) + 8
EXPERT_UNITS = 12
PAIR_UNITS = 2 * EXPERT_UNITS
PASS_UNITS = PAIRS * PAIR_UNITS
QUAD_TURNS = 30
PAIR_BANK_USES = [5, 5, 2, 2, 3, 3, 3, 4]

ORDER = (("gu", 0), ("gu", 1), ("d", 0), ("d", 1))
GATE_DONE, DOWN_FROM = [4, 12], [16, 20]

TABLE_COLS = [("ident", P), ("cos", TOK), ("sin", TOK), ("reset", SEQ), ("dret", C_HEADS * P),
              ("qdec", C_HEADS * P), ("kdec", C_HEADS), ("mean128", P), ("mean64", P), ("blockdiag", P),
              ("before", P), ("slot", P), ("key4", 4), ("key16", 16), ("seqdelta", DEC_BATCH)]
TABLE_AT, _n = {}, 0
for _name, _w in TABLE_COLS:
    TABLE_AT[_name] = (_n, _w)
    _n += _w
TABLE_W = _n


def shape_tables():
    f = np.float32
    t = {}
    i = np.arange(P)
    t["ident"] = np.eye(P)
    half = DK_C // 2
    inv = f(10000.0) ** (-np.arange(half, dtype=f) / f(half))
    pos = np.concatenate([np.arange(SEQ), np.full(DEC_BATCH, PAST_LEN)]).astype(f)
    ang = inv[:, None] * pos[None]
    t["cos"] = np.concatenate([np.cos(ang), np.cos(ang)])
    t["sin"] = np.concatenate([-np.sin(ang), np.sin(ang)])
    t["reset"] = np.broadcast_to((np.arange(SEQ) % CHUNK_B != 0), (P, SEQ))
    lg = np.log1p(-np.exp2(-5.0 - np.arange(C_HEADS, dtype=f))).astype(f)
    rel = (i[None, :] - i[:, None]).astype(f)
    scale = f(DK_C ** -0.5)
    t["dret"] = np.concatenate([np.where(rel >= 0, np.exp(np.where(rel >= 0, rel, 0) * g), 0) * scale for g in lg], 1)
    t["qdec"] = np.concatenate([np.broadcast_to(np.exp((i + 1).astype(f) * g), (P, P)) for g in lg], 1)
    t["kdec"] = np.stack([np.exp((P - 1.0 - i).astype(f) * g) * scale for g in lg], 1)
    t["mean128"] = np.full((P, P), 1 / 128)
    t["mean64"] = (i[:, None] // 64 == i[None] // 64) / 64
    t["blockdiag"] = (i[:, None] // 64 == i[None] // 64)
    t["before"] = (i[:, None] < i[None])
    t["slot"] = np.broadcast_to(i, (P, P))
    t["key4"] = np.broadcast_to(4 - np.arange(4), (P, 4))
    t["key16"] = np.broadcast_to(16 - np.arange(16), (P, 16))
    t["seqdelta"] = np.pad(np.eye(DEC_BATCH), ((0, P - DEC_BATCH), (0, 0)))
    levels = np.stack([(i[:, None] // (2 * m) == i[None] // (2 * m)) & (i[:, None] // m % 2 == 0) & (i[None] // m % 2 == 1)
                       for m in LEVELS], 1)
    layer_flag = np.broadcast_to((np.arange(DEPTH) > 0).astype(f)[:, None, None], (DEPTH, P, 1))
    return (np.concatenate([np.asarray(t[n], f) for n, _ in TABLE_COLS], 1),
            levels.astype(f).reshape(P, -1), np.ascontiguousarray(layer_flag))


GAMMA = [float(np.exp(np.log1p(-np.exp2(np.float32(-5.0 - h))))) for h in range(C_HEADS)]
GAMMA_CHUNK = [float(np.exp(np.float32(P) * np.log1p(-np.exp2(np.float32(-5.0 - h))))) for h in range(C_HEADS)]


def rows_of(t):
    return P if t < TILES - 1 else DEC_BATCH


def build_program(nc, A, O):
    f32, f32r, bf16, i32 = mybir.dt.float32, mybir.dt.float32r, mybir.dt.bfloat16, mybir.dt.int32
    u8 = mybir.dt.uint8
    ALU, ACT, AX = mybir.AluOpType, mybir.ActivationFunctionType, mybir.AxisListType
    (o_yp, o_ys, o_hp, o_hs, o_cp, o_cs, o_gp, o_gs, o_rp, o_rs) = O
    ctx = ExitStack()
    with ctx:
        def sb(name, shape, dt=f32):
            return ctx.enter_context(nc.sbuf_tensor(name, shape, dt))

        def sem(name):
            return ctx.enter_context(nc.semaphore(name))

        x = sb("x", [P, TILES, D_MODEL])
        raw = sb("raw", [P, RAW_SLOTS, UNIT])
        ws = sb("ws", [P, SPLIT_SLOTS, 2, UNIT], f32r)
        tab = sb("tab", [P, TABLE_W])
        lev = sb("lev", [P, len(LEVELS) * P], u8)
        before_bf = sb("before_bf", [P, P], bf16)
        ones_bf = sb("ones_bf", [P, P], bf16)
        ident_bf = sb("ident_bf", [P, P], bf16)
        eps = sb("eps", [P, 3])
        convw = sb("convw", [P, 2, CONV_W])
        convb = sb("convb", [P, 2])
        gbias = sb("gbias", [P, 2, 2])
        gw = sb("gw", [P, 2, 2, P])
        lam = sb("lam", [P, 2])
        c8 = sb("c8", [P, 2])
        lamt = sb("lamt", [P, 3, 2])
        lbl = sb("lbl", [P, DEPTH, 2])
        lbt = sb("lbt", [P, 5, 2])
        flag = sb("flag", [P, 1])
        lb = sb("lb", [P, 2])
        oml = sb("oml", [P, 2])
        ng = sb("ng", [P, 1])
        h0 = sb("h0", [P, 2, DEC_BATCH])
        rw = sb("rw", [P, KC, N_EXPERTS])
        rb = sb("rb", [N_EXPERTS, 1])
        stats = sb("stats", [P, TILES, 12])
        mv = sb("mv", [P, TILES, 2])
        lnrs = sb("lnrs", [P, TILES, 2])
        outst = sb("outst", [P, 2, 20])
        csst = sb("csst", [P, 2, 3, DEC_BATCH])
        lg = sb("lg", [P, TILES, N_EXPERTS])
        rt = sb("rt", [P, 6, TILES, N_EXPERTS])
        rg = sb("rg", [P, 8, TILES, 4])
        posm = sb("posm", [P, TILES, N_EXPERTS])
        comb = sb("comb", [P, TILES, N_EXPERTS])
        mask_bf = sb("mask_bf", [P, TILES, N_EXPERTS], bf16)
        cnt = sb("cnt", [P, 8])
        cnt_i = sb("cnt_i", [P, DEPTH], i32)
        passes_f = sb("passes_f", [P, 1])
        passes_i = sb("passes_i", [P, DEPTH + 1], i32)
        pg = sb("pg", [P, TILES, 2])
        pc = sb("pc", [P, 2, TILES, 2])
        cb3 = sb("cb3", [P, TILES, 2, 3], bf16)
        gsl = sb("gsl", [P, 2])
        bl = sb("bl", [P, 2, CHUNKS_B])

        def table(name, rows=P):
            a, w = TABLE_AT[name]
            return tab[0:rows, a:a + w]
        ident = table("ident")

        mixer = ExitStack()
        xsT = mixer.enter_context(nc.sbuf_tensor("xsT", [P, 2, KC, TOK], f32r))
        Z = mixer.enter_context(nc.sbuf_tensor("mixer", [P, 15216], f32))
        y32 = mixer.enter_context(nc.sbuf_tensor("y32", [P, KC, TOK], f32))
        mixer.close()
        xsM = sb("xsM", [P, 2, TILES, D_MODEL], f32r)
        XeT = sb("XeT", [P, 2, KC, 2 * SLOTS], f32r)
        Pm = sb("Pm", [P, TILES, 2, SLOTS], f32r)
        PT = sb("PT", [SLOTS, 2, TOK], f32r)
        ye = sb("ye", [SLOTS, 2, 2, D_MODEL], f32r)
        hT = sb("hT", [P, 2, 4, SLOTS], f32r)
        Pbf = sb("Pbf", [P, TILES, 2, SLOTS], bf16)
        act_g = sb("act_g", [SLOTS, D_EXPERT])
        act_h = sb("act_h", [SLOTS, D_EXPERT])
        lngb2 = sb("lngb2", [P, 2, D_MODEL])
        x1T = Z[:, 4000:4000 + KC * TOK].rearrange("p (k t) -> p k t", k=KC)
        lgT = Z[0:N_EXPERTS, 8160:8160 + TOK]
        lngb1 = Z[:, 8680:8680 + 2 * D_MODEL].rearrange("p (n d) -> p n d", n=2)
        ysT = xsT

        def z(off, *dims):
            n = int(np.prod(dims))
            v = Z[:, off:off + n]
            if len(dims) == 1:
                return v
            names = "abcde"[:len(dims)]
            kw = {c: d for c, d in zip(names[1:], dims[1:])}
            return v.rearrange(f"p ({' '.join(names)}) -> p {' '.join(names)}", **kw)
        b_f, b_k, b_q = z(0, 2, TOK), z(1040, 2, TOK), z(2080, 2, TOK)
        b_v, b_g = z(3120, TILES, D_B), z(4400, 2, TOK)
        W0 = 5440
        b_t1, b_t2, b_b = z(W0, 2, TOK), z(W0 + 1040, 2, TOK), z(W0 + 2080, 2, TOK)
        b_acc = z(W0 + 3120, 2, 4, 2, P)
        b_S = z(W0 + 5168, CHUNKS_B + 1, 2, P)
        b_Vx = Z[0:DEC_BATCH, W0 + 5168:W0 + 5168 + 2048].rearrange("p (h n v) -> p h n v", h=4, n=DEC_BATCH)
        b_kT = z(W0 + 7472, 4, D_B)
        b_S0 = z(W0 + 8496, 2, DEC_BATCH, DK_B)
        a_x = z(W0, 2, SEQ + 3)
        a_xs = z(W0 + 1032, 2, CONV_W, DEC_BATCH)
        a_u, a_r, a_i = z(W0 + 1096, 2, TOK), z(W0 + 2136, 2, TOK), z(W0 + 3176, 2, TOK)
        a_a, a_t, a_g = z(W0 + 4216, 2, TOK), z(W0 + 5256, 2, TOK), z(W0 + 6296, 2, TOK)
        c_k, c_q, c_t1, c_sw = z(0, 2, TOK), z(1040, 2, TOK), z(2080, 2, TOK), z(3120, 2, TOK)
        c_v, c_g = z(4160, TILES, 256), z(5440, 2, TOK)
        c_sc, c_qd, c_kT = z(6480, 4, 2, P), z(7504, 2, 4, P), z(8528, 4, 2, P)
        c_S = z(9552, 5, 2, P)
        c_S0 = z(10832, 2, DEC_BATCH, P)
        c_Vx = Z[0:DEC_BATCH, 12880:12880 + 2048].rearrange("p (h n v) -> p h n v", h=2, n=DEC_BATCH)
        ksT = Z[0:DEC_BATCH, 14960:15216]
        outst_t = Z[0:20, W0 + 7472:W0 + 7472 + D_A]

        ps = ctx.enter_context(nc.psum_tensor("ps", [P, 8, 512], f32))

        SEMS = """waits_apart x_loaded tables_loaded tables_ready params_loaded gw_zero params_ready small_in small_exp prob_exp lg_shifted last_counts x_tile_ready
          passes_known w_high w_split w_used
          xT_ps xT_high xT_low
          xa_sb u_ready gates_ps r_gate i_gate tanh_a ratio_ready sqrt_a h_ready ga_ready states_ps states_sb states_t
          f_sig k_sig q_silu v_b g_b k_ready clamped log_ab b_ready arg_ready e_ready qk_ready lev_ps lev_done
          eb_ready p_ready tr_ps kT_sb ks_sb vx_ready kv_ps s_new ds_ps s_ready o_ps o_sb sq_sb ms_ps ms_sqrt y_b y_a
          hg_out hg_in
          rot_swapped rot_sin rot_k rot_q v_c g_c sc_ps sc_ready qd_ready ctr_ps ckT_sb cks_sb cvx_ready ckv_ps cs_new
          cds_ps cs_ready co_ps co_sb cmean_ps cd_ready csq_sb cvar_ps cvar_sqrt y_c cs_out cs_in
          y_high y_low mix_done mv_ready std_ready lnrs_ready ln_scaled ln_loaded ln1_done x1T_ps x1T_sb lgT_ps lgT_sb
          lg_ps mask_ready pos_ps posm_ready routed xm_high xm_low x_scaled
          p_built cb_ready p_bf pt_ps pt_sb gs_ps gs_sb gath_ps gath_high gath_low silu_done h_done ht_ps ht_high ht_low
          ye_high ye_low scat_ps scat_done ln2_scaled out_done""".split()
        s = {}
        for n in SEMS:
            s[n] = sem(n)
        raw_loaded = [sem(f"raw_loaded{i}") for i in range(RAW_SLOTS)]
        quad_free = [sem(f"quad_free{i}") for i in range(2)]
        bank_free = [sem(f"bank_free{i}") for i in range(8)]

        w_in_v = A["w_in"].rearrange("l (k p) c -> l p k c", p=P)
        w_out_v = A["w_out"].rearrange("l (k p) c -> l p k c", p=P)
        wg_v = A["exp_w_gate"].rearrange("l e (k p) f -> l e p k f", p=P)
        wu_v = A["exp_w_up"].rearrange("l e (k p) f -> l e p k f", p=P)
        wd_v = A["exp_w_down"].rearrange("l e (k p) d -> l e p k d", p=P)

        def wait_apart(engine, semaphore, count):
            engine.wait_ge(semaphore, count)
            engine.sem_inc(s["waits_apart"], 1)

        def part_col(name):
            return COLS[name.rstrip("01")] + (256 if name.endswith("1") else 0)

        block = ctx.enter_context(nc.Block())

        @block.sync
        def _(sp):
            def load(u, k, src, shape4=True):
                slot = k % RAW_SLOTS
                sp.wait_ge(s["w_split"], u + k + 1)
                dst = raw[:, slot, :].rearrange("p (k c) -> p k c", k=src.shape[1])
                sp.dma_start(dst, src).then_inc(raw_loaded[slot], 16)

            with sp.Fori(0, DEPTH) as l:
                sp.wait_ge(s["passes_known"], l + 1)
                before = sp.value_load(passes_i[0:1, bass.ds(l, 1)], min_val=0, max_val=DEPTH * PASSES)
                base = sp.snap(l * MIX_UNITS + before * PASS_UNITS)
                k = 0
                for part in IN_PARTS:
                    c = part_col(part)
                    for half in range(2):
                        load(base, k, w_in_v[l, :, 4 * half:4 * half + 4, c:c + 256])
                        k += 1
                for c in range(4):
                    for half in range(2):
                        load(base, k, w_out_v[l, :, 4 * half:4 * half + 4, c * 256:c * 256 + 256])
                        k += 1

                def experts(done):
                    with sp.Fori(0, PAIRS) as g:
                        first = sp.snap(base + MIX_UNITS + done * PASS_UNITS + g * PAIR_UNITS)
                        j = 0
                        for kind, e in ORDER:
                            ex = g * 2 + e
                            if kind == "gu":
                                for v in (wg_v, wu_v):
                                    for q in range(4):
                                        load(first, j, v[l, ex, :, 2 * q:2 * q + 2, :])
                                        j += 1
                            else:
                                for half in range(2):
                                    for q in range(2):
                                        load(first, j, wd_v[l, ex, :, 2 * q:2 * q + 2, half * 512:half * 512 + 512])
                                        j += 1
                experts(0)
                wait_apart(sp, s["routed"], l + 1)
                most = sp.value_load(cnt_i[0:1, bass.ds(l, 1)], min_val=0, max_val=TOK)
                with sp.Fori(1, PASSES) as r:
                    with sp.If(most > r * SLOTS):
                        experts(r)

        @block.gpsimd
        def _(pool):
            def high(u, uses, k):
                slot, dst = k % RAW_SLOTS, k % SPLIT_SLOTS
                pool.wait_ge(raw_loaded[slot], (uses + k // RAW_SLOTS + 1) * 16)
                wait_apart(pool, s["w_used"], u + k + 1)
                nc.gpsimd.tensor_scalar(ws[:, dst, 0, :], raw[:, slot, :], 1.0, 0.0, ALU.mult, ALU.add).then_inc(s["w_high"], 1)

            nc.gpsimd.memset(gw[:], 0.0).then_inc(s["gw_zero"], 1)
            with pool.Fori(0, DEPTH) as l:
                pool.wait_ge(s["passes_known"], l + 1)
                before = pool.value_load(passes_i[0:1, bass.ds(l, 1)], min_val=0, max_val=DEPTH * PASSES)
                base = pool.snap(l * MIX_UNITS + before * PASS_UNITS)
                uses = pool.snap(l * (MIX_UNITS // RAW_SLOTS) + before * (PASS_UNITS // RAW_SLOTS))
                rot = 0
                for k in range(MIX_UNITS):
                    high(base, uses, k)
                    if k % 2 == 1 and k // 2 >= 1 and k // 2 - 1 < len(IN_PARTS) and IN_PARTS[k // 2 - 1][:2] in ("kc", "qc"):
                        pool.wait_ge(s["rot_swapped"], l * 4 + rot + 1)
                        sinb = table("sin").unsqueeze(1).to_broadcast([P, 2, TOK])
                        nc.gpsimd.tensor_tensor(c_sw, c_sw, sinb, ALU.mult).then_inc(s["rot_sin"], 1)
                        rot += 1
                pool.wait_ge(s["routed"], l + 1)
                most = pool.value_load(cnt_i[0:1, bass.ds(l, 1)], min_val=0, max_val=TOK)
                with pool.Fori(0, PASSES) as r:
                    with pool.If(most > r * SLOTS):
                        with pool.Fori(0, PAIRS) as g:
                            n = pool.snap((before + r) * PAIRS + g)
                            first = pool.snap(base + MIX_UNITS + r * PASS_UNITS + g * PAIR_UNITS)
                            wait_apart(pool, s["p_built"], n + 1)
                            for rows, t0, t1 in ((P, 0, 4), (DEC_BATCH, 4, 5)):
                                op = nc.gpsimd.tensor_scalar(Pbf[0:rows, t0:t1].rearrange("p t e c -> p (t e c)"),
                                                             Pm[0:rows, t0:t1].rearrange("p t e c -> p (t e c)").bitcast(f32),
                                                             1.0, 0.0, ALU.mult, ALU.add)
                            op.then_inc(s["p_bf"], 1)
                            done = pool.snap(uses + MIX_UNITS // RAW_SLOTS + (r * PAIRS + g) * (PAIR_UNITS // RAW_SLOTS))
                            for k in range(PAIR_UNITS):
                                high(first, done, k)

        SPLIT3 = ((0, 0), (0, 1), (1, 0))

        @block.tensor
        def _(pe):
            pe.wait_ge(s["tables_ready"], 1)
            with pe.Fori(0, DEPTH) as l:
                pe.wait_ge(s["passes_known"], l + 1)
                before = pe.value_load(passes_i[0:1, bass.ds(l, 1)], min_val=0, max_val=DEPTH * PASSES)
                base = pe.snap(l * MIX_UNITS + before * PASS_UNITS)
                turns = [0]
                unit = [0]

                def turn(apart=False):
                    q = turns[0] % 2
                    pe.wait_ge(quad_free[q], l * QUAD_TURNS + turns[0] // 2 + 1)
                    if apart:
                        pe.sem_inc(s["waits_apart"], 1)
                    turns[0] += 1
                    return 4 * q

                for t in range(TILES):
                    r = rows_of(t)
                    b = turn()
                    wait_apart(pe, s["x_tile_ready"], l * TILES + t + 1)
                    for k in range(KC):
                        op = nc.tensor.transpose(ps[:, b + k // 4, (k % 4) * P:(k % 4) * P + r],
                                                 x[0:r, t, k * P:(k + 1) * P], ident[0:r, 0:r])
                    op.then_inc(s["xT_ps"], 1)

                def project(token_major):
                    b = turn()
                    for half in range(2):
                        k0 = unit[0]
                        pe.wait_ge(s["w_split"], base + k0 + 1 + RAW_SLOTS)
                        w = ws[:, k0 % SPLIT_SLOTS].rearrange("p a (k c) -> p a k c", k=4)
                        if not token_major:
                            for c in range(2):
                                for th in range(2):
                                    for k in range(4):
                                        for n, (a, bb) in enumerate(SPLIT3):
                                            op = nc.tensor.matmul(ps[:, b + 2 * c + th, 0:HALF], w[:, a, k, c * P:(c + 1) * P],
                                                                  xsT[:, bb, 4 * half + k, th * HALF:(th + 1) * HALF],
                                                                  start=half + k + n == 0, stop=half == 1 and k == 3 and n == 2)
                        else:
                            for t in range(TILES):
                                r = rows_of(t)
                                for k in range(4):
                                    for n, (a, bb) in enumerate(SPLIT3):
                                        op = nc.tensor.matmul(ps[0:r, b + t % 4, 256 * (t // 4):256 * (t // 4) + 256],
                                                              xsT[:, bb, 4 * half + k, t * P:t * P + r], w[:, a, k, :],
                                                              start=half + k + n == 0 and t < 4,
                                                              stop=half == 1 and k == 3 and n == 2, skip_group_check=True)
                        op.then_inc(s["w_used"], 1)
                        unit[0] += 1

                pe.wait_ge(s["xT_low"], (l + 1) * TILES)
                for part in ("xa", "ga", "fb", "qb"):
                    project(False)

                pe.wait_ge(s["u_ready"], l + 1)
                for gate in range(2):
                    b = turn()
                    if gate == 0:
                        pe.wait_ge(s["params_ready"], l + 1)
                    for c in range(2):
                        for th in range(2):
                            op = nc.tensor.matmul(ps[:, b + 2 * c + th, 0:HALF], gw[:, gate, c, :],
                                                  a_u[:, c, th * HALF:(th + 1) * HALF], start=True, stop=True)
                    op.then_inc(s["gates_ps"], 1)
                project(True)
                project(False)
                b = turn()
                pe.wait_ge(s["states_sb"], l + 1)
                for c in range(2):
                    op = nc.tensor.transpose(ps[0:20, b, c * P:(c + 1) * P], outst[:, c, :], ident)
                op.then_inc(s["states_ps"], 1)

                for n in range(len(LEVELS) + 1):
                    b = turn()
                    if n == 0:
                        pe.wait_ge(s["k_ready"], l + 1)
                        pe.wait_ge(s["q_silu"], l + 1)
                    else:
                        pe.wait_ge(s["qk_ready"], l * len(LEVELS) + n)
                    for t in range(4):
                        for h in range(4):
                            pr, c, sl = slice(64 * (h % 2), 64 * (h % 2) + 64), h // 2, slice(t * P, (t + 1) * P)
                            kk, qq = (b_k, b_q) if n == 0 else (b_t2, b_t2)
                            at = (t % 2) * 256 + c * P
                            op = nc.tensor.matmul(ps[:, b + 2 * (h % 2) + t // 2, at:at + P], kk[pr, c, sl], qq[pr, c, sl],
                                                  start=True, stop=True, skip_group_check=True)
                    op.then_inc(s["lev_ps"], 1)
                b = turn()
                pe.wait_ge(s["p_ready"], l + 1)
                for t in range(4):
                    for c in range(2):
                        nc.tensor.transpose(ps[:, b + t // 2, (t % 2) * 256 + c * P:(t % 2) * 256 + (c + 1) * P],
                                            b_k[:, c, t * P:(t + 1) * P], ident)
                for c in range(2):
                    op = nc.tensor.transpose(ps[0:DEC_BATCH, b + 2, c * P:(c + 1) * P], b_k[:, c, SEQ:TOK], ident)
                op.then_inc(s["tr_ps"], 1)
                b = turn()
                pe.wait_ge(s["ks_sb"], l + 1)
                pe.wait_ge(s["vx_ready"], l + 1)
                for h in range(4):
                    op = nc.tensor.matmul(ps[64 * (h % 2):64 * (h % 2) + 64, b + h // 2, :], ksT[:, h * 64:(h + 1) * 64],
                                          b_Vx[:, h].rearrange("p n v -> p (n v)"), start=True, stop=True,
                                          skip_group_check=True)
                op.then_inc(s["kv_ps"], 1)
                b = turn()
                pe.wait_ge(s["kT_sb"], l + 1)
                for ch in range(CHUNKS_B):
                    pr = slice(64 * (ch % 2), 64 * (ch % 2) + 64)
                    for c in range(2):
                        at = (ch // 2 % 2) * 256 + c * P
                        op = nc.tensor.matmul(ps[:, b + 2 * (ch % 2) + ch // 4, at:at + P],
                                              b_kT[pr, ch // 2, c * P:(c + 1) * P], b_v[pr, ch // 2, c * P:(c + 1) * P],
                                              start=True, stop=True, skip_group_check=True)
                op.then_inc(s["ds_ps"], 1)
                b = turn()
                pe.wait_ge(s["lev_done"], (l + 1) * (len(LEVELS) + 1))
                pe.wait_ge(s["s_ready"], l + 1)
                pe.wait_ge(s["s_new"], l + 1)
                for c in range(2):
                    for t in range(4):
                        for hh in range(2):
                            h = 2 * c + hh
                            nc.tensor.matmul(ps[64 * hh:64 * hh + 64, b + c, t * P:(t + 1) * P],
                                             b_v[:, t, h * 64:(h + 1) * 64], b_acc[:, hh, t, c, :],
                                             start=t == 0, stop=False, skip_group_check=True)
                        for ch in (2 * t, 2 * t + 1):
                            nc.tensor.matmul(ps[:, b + c, ch * 64:(ch + 1) * 64], b_S[:, ch, c, :],
                                             b_q[:, c, ch * 64:(ch + 1) * 64], start=False, stop=True, skip_group_check=True)
                for h in range(4):
                    pr, c = slice(64 * (h % 2), 64 * (h % 2) + 64), h // 2
                    for n in range(DEC_BATCH):
                        op = nc.tensor.matmul(ps[pr, b + 2, c * DEC_BATCH + n:c * DEC_BATCH + n + 1], b_S0[pr, c, n, :],
                                              b_q[pr, c, SEQ + n:SEQ + n + 1], start=True, stop=True, skip_group_check=True)
                op.then_inc(s["o_ps"], 1)
                b = turn()
                pe.wait_ge(s["sq_sb"], l + 1)
                for c in range(2):
                    for th in range(2):
                        op = nc.tensor.matmul(ps[:, b + 2 * c + th, 0:HALF], table("mean64"),
                                              b_t2[:, c, th * HALF:(th + 1) * HALF], start=True, stop=True)
                op.then_inc(s["ms_ps"], 1)

                for j in range(2):
                    n2 = l * 2 + j + 1
                    for part in ("kc", "qc", "vc", "gc"):
                        project(part == "vc")
                    b = turn()
                    pe.wait_ge(s["rot_k"], n2)
                    pe.wait_ge(s["rot_q"], n2)
                    for t in range(4):
                        for h in range(2):
                            op = nc.tensor.matmul(ps[:, b + t // 2, (t % 2) * 256 + h * P:(t % 2) * 256 + (h + 1) * P],
                                                  c_k[:, h, t * P:(t + 1) * P], c_q[:, h, t * P:(t + 1) * P],
                                                  start=True, stop=True, skip_group_check=True)
                    op.then_inc(s["sc_ps"], 1)
                    b = turn()
                    for t in range(4):
                        for h in range(2):
                            nc.tensor.transpose(ps[:, b + t // 2, (t % 2) * 256 + h * P:(t % 2) * 256 + (h + 1) * P],
                                                c_k[:, h, t * P:(t + 1) * P], ident)
                    for h in range(2):
                        op = nc.tensor.transpose(ps[0:DEC_BATCH, b + 2, h * P:(h + 1) * P], c_k[:, h, SEQ:TOK], ident)
                    op.then_inc(s["ctr_ps"], 1)
                    b = turn()
                    pe.wait_ge(s["cks_sb"], n2)
                    pe.wait_ge(s["cvx_ready"], n2)
                    for h in range(2):
                        for nh in range(2):
                            op = nc.tensor.matmul(ps[:, b + 2 * h + nh, :], ksT[:, h * P:(h + 1) * P],
                                                  c_Vx[:, h, 4 * nh:4 * nh + 4, :].rearrange("p n v -> p (n v)"),
                                                  start=True, stop=True)
                    op.then_inc(s["ckv_ps"], 1)
                    b = turn()
                    pe.wait_ge(s["ckT_sb"], n2)
                    pe.wait_ge(s["v_c"], n2)
                    for t in range(4):
                        for h in range(2):
                            op = nc.tensor.matmul(ps[:, b + t // 2, (t % 2) * 256 + h * P:(t % 2) * 256 + (h + 1) * P],
                                                  c_kT[:, t, h, :], c_v[:, t, h * P:(h + 1) * P],
                                                  start=True, stop=True, skip_group_check=True)
                    op.then_inc(s["cds_ps"], 1)
                    b = turn()
                    pe.wait_ge(s["sc_ready"], n2)
                    pe.wait_ge(s["qd_ready"], n2)
                    pe.wait_ge(s["cs_ready"], n2)
                    pe.wait_ge(s["cs_new"], n2)
                    for h in range(2):
                        for t in range(4):
                            nc.tensor.matmul(ps[:, b + h, t * P:(t + 1) * P], c_v[:, t, h * P:(h + 1) * P], c_sc[:, t, h, :],
                                             start=t == 0, stop=t == 0, skip_group_check=True)
                            if t:
                                nc.tensor.matmul(ps[:, b + h, t * P:(t + 1) * P], c_S[:, t, h, :], c_qd[:, h, t, :],
                                                 start=False, stop=True, skip_group_check=True)
                    for h in range(2):
                        for n in range(DEC_BATCH):
                            op = nc.tensor.matmul(ps[:, b + 2, h * DEC_BATCH + n:h * DEC_BATCH + n + 1], c_S0[:, h, n, :],
                                                  c_q[:, h, SEQ + n:SEQ + n + 1], start=True, stop=True, skip_group_check=True)
                    op.then_inc(s["co_ps"], 1)
                    for what, ready in (("cmean_ps", "co_sb"), ("cvar_ps", "csq_sb")):
                        b = turn()
                        pe.wait_ge(s[ready], n2)
                        src = c_t1 if what == "cmean_ps" else c_sw
                        for h in range(2):
                            for th in range(2):
                                op = nc.tensor.matmul(ps[:, b + 2 * h + th, 0:HALF], table("mean128"),
                                                      src[:, h, th * HALF:(th + 1) * HALF], start=True, stop=True)
                        op.then_inc(s[what], 1)

                pe.wait_ge(s["y_low"], l + 1)
                for cc in range(4):
                    b = turn()
                    for half in range(2):
                        k0 = unit[0]
                        pe.wait_ge(s["w_split"], base + k0 + 1 + RAW_SLOTS)
                        w = ws[:, k0 % SPLIT_SLOTS].rearrange("p a (k c) -> p a k c", k=4)
                        for t in range(TILES):
                            r = rows_of(t)
                            for k in range(4):
                                for n, (a, bb) in enumerate(SPLIT3):
                                    op = nc.tensor.matmul(ps[0:r, b + t % 4, 256 * (t // 4):256 * (t // 4) + 256],
                                                          ysT[:, bb, 4 * half + k, t * P:t * P + r], w[:, a, k, :],
                                                          start=half + k + n == 0 and t < 4,
                                                          stop=half == 1 and k == 3 and n == 2, skip_group_check=True)
                        op.then_inc(s["w_used"], 1)
                        unit[0] += 1

                for t in range(TILES):
                    r = rows_of(t)
                    pe.wait_ge(s["ln1_done"], l * TILES + t + 1)
                    b = turn(apart=True)
                    for k in range(KC):
                        op = nc.tensor.transpose(ps[:, b + k // 4, (k % 4) * P:(k % 4) * P + r],
                                                 x[0:r, t, k * P:(k + 1) * P], ident[0:r, 0:r])
                    op.then_inc(s["x1T_ps"], 1)
                b = turn()
                pe.wait_ge(s["x1T_sb"], (l + 1) * TILES)
                for th in range(2):
                    for k in range(KC):
                        op = nc.tensor.matmul(ps[0:N_EXPERTS, b + th, 0:HALF], rw[:, k, :], x1T[:, k, th * HALF:(th + 1) * HALF],
                                              start=k == 0, stop=k == KC - 1)
                op.then_inc(s["lgT_ps"], 1)
                pe.wait_ge(s["lgT_sb"], l + 1)
                b = turn(apart=True)
                for t in range(TILES):
                    r = rows_of(t)
                    op = nc.tensor.transpose(ps[0:r, b, t * N_EXPERTS:(t + 1) * N_EXPERTS], lgT[:, t * P:t * P + r],
                                             ident[0:N_EXPERTS, 0:N_EXPERTS])
                op.then_inc(s["lg_ps"], 1)
                b = turn()
                pe.wait_ge(s["mask_ready"], l + 1)
                for t in range(TILES + 1):
                    r = rows_of(t) if t < TILES else P
                    for tt in range(min(t, TILES - 1) + 1):
                        rr = rows_of(tt)
                        lhsT = before_bf if tt == t else ones_bf
                        op = nc.tensor.matmul(ps[0:r, b, t * N_EXPERTS:(t + 1) * N_EXPERTS], lhsT[0:rr, 0:r],
                                              mask_bf[0:rr, tt, :], start=tt == 0, stop=tt == min(t, TILES - 1),
                                              skip_group_check=True)
                op.then_inc(s["pos_ps"], 1)
                assert turns[0] == 2 * QUAD_TURNS, turns
                assert unit[0] == MIX_UNITS

                pe.wait_ge(s["routed"], l + 1)
                for q in range(2):
                    pe.wait_ge(quad_free[q], (l + 1) * QUAD_TURNS + 1)
                pe.wait_ge(s["xm_low"], (l + 1) * TILES)
                most = pe.value_load(cnt_i[0:1, bass.ds(l, 1)], min_val=0, max_val=TOK)
                with pe.Fori(0, PASSES) as rnd:
                    with pe.If(most > rnd * SLOTS):
                        with pe.Fori(0, PAIRS) as g:
                            n = pe.snap((before + rnd) * PAIRS + g)
                            first = pe.snap(base + MIX_UNITS + rnd * PASS_UNITS + g * PAIR_UNITS + RAW_SLOTS)
                            used = [0] * 8
                            j = [0]

                            def bank(i):
                                pe.wait_ge(bank_free[i], n * PAIR_BANK_USES[i] + used[i] + 1)
                                used[i] += 1
                                return i

                            pe.wait_ge(s["p_bf"], n + 1)
                            for e in range(2):
                                b = bank(4 + e)
                                pbt = ps[:, b, :].bitcast(bf16)
                                for t in range(TILES):
                                    r = rows_of(t)
                                    op = nc.tensor.transpose(pbt[:, t * P:t * P + r], Pbf[0:r, t, e, :], ident_bf[0:r, 0:r])
                                op.then_inc(s["pt_ps"], 1)
                            pe.wait_ge(s["cb_ready"], n + 1)
                            b = bank(6)
                            for e in range(2):
                                for t in range(TILES):
                                    r = rows_of(t)
                                    op = nc.tensor.matmul(ps[:, b, 4 * e:4 * e + 3], Pbf[0:r, t, e, :], cb3[0:r, t, e, :],
                                                          start=t == 0, stop=t == TILES - 1, skip_group_check=True)
                            op.then_inc(s["gs_ps"], 1)
                            for k in range(KC):
                                if k % 2 == 0:
                                    b = bank(k // 2)
                                for t in range(TILES):
                                    r = rows_of(t)
                                    for a in range(2):
                                        op = nc.tensor.matmul(ps[:, b, (k % 2) * 256:(k % 2) * 256 + 256],
                                                              xsM[0:r, a, t, k * P:(k + 1) * P],
                                                              Pm[0:r, t].rearrange("p e c -> p (e c)"),
                                                              start=t + a == 0, stop=t == TILES - 1 and a == 1,
                                                              skip_group_check=True)
                                if k % 2 == 1:
                                    op.then_inc(s["gath_ps"], 1)

                            def gate_up(e):
                                for m in range(2):
                                    b = bank(2 * (e % 2) + m)
                                    if e == 0 and m == 0:
                                        pe.wait_ge(s["gath_low"], (n + 1) * (KC // 2))
                                    for q in range(4):
                                        k0 = j[0]
                                        pe.wait_ge(s["w_split"], first + k0 + 1)
                                        w = ws[:, k0 % SPLIT_SLOTS].rearrange("p a (k c) -> p a k c", k=2)
                                        for kk in range(2):
                                            for i3, (a, bb) in enumerate(SPLIT3):
                                                op = nc.tensor.matmul(ps[:, b, :], XeT[:, bb, 2 * q + kk, e * SLOTS:(e + 1) * SLOTS],
                                                                      w[:, a, kk, :], start=q + kk + i3 == 0,
                                                                      stop=q == 3 and kk == 1 and i3 == 2)
                                        op.then_inc(s["w_used"], 1)
                                        j[0] += 1

                            def turn_h(e):
                                b = bank(4)
                                pe.wait_ge(s["h_done"], n * 2 + e + 1)
                                for q in range(4):
                                    op = nc.tensor.transpose(ps[:, b, q * P:(q + 1) * P], act_h[:, q * P:(q + 1) * P], ident)
                                op.then_inc(s["ht_ps"], 1)

                            def down(e):
                                for half in range(2):
                                    b = bank(5 + half)
                                    for q in range(2):
                                        k0 = j[0]
                                        pe.wait_ge(s["w_split"], first + k0 + 1)
                                        if half + q == 0:
                                            pe.wait_ge(s["ht_low"], n * 2 + e + 1)
                                        w = ws[:, k0 % SPLIT_SLOTS].rearrange("p a (k c) -> p a k c", k=2)
                                        for kk in range(2):
                                            for i3, (a, bb) in enumerate(SPLIT3):
                                                op = nc.tensor.matmul(ps[:, b, :], hT[:, bb, 2 * q + kk, :], w[:, a, kk, :],
                                                                      start=q + kk + i3 == 0, stop=q == 1 and kk == 1 and i3 == 2)
                                        op.then_inc(s["w_used"], 1)
                                        j[0] += 1

                            def scatter():
                                pe.wait_ge(s["pt_sb"], (n + 1) * 2)
                                pe.wait_ge(s["ye_low"], (n + 1) * 4)
                                for i in range(2 * TILES):
                                    t, half = i // 2, i % 2
                                    r = rows_of(t)
                                    b = bank((7, 0, 1)[i % 3])
                                    for e2 in range(2):
                                        for a in range(2):
                                            op = nc.tensor.matmul(ps[0:r, b, :], PT[:, e2, t * P:t * P + r],
                                                                  ye[:, e2, a, half * 512:half * 512 + 512],
                                                                  start=e2 + a == 0, stop=e2 == 1 and a == 1)
                                    op.then_inc(s["scat_ps"], 1)

                            gate_up(0)
                            gate_up(1)
                            turn_h(0)
                            down(0)
                            turn_h(1)
                            down(1)
                            scatter()
                            assert used == PAIR_BANK_USES, used
                            assert j[0] == PAIR_UNITS

        @block.scalar
        def _(act):
            def quad(q):
                return ps[:, 4 * q:4 * q + 4, 0:HALF]
            act.dma_start(tab[:], A["tables"]).then_inc(s["tables_loaded"], 16)
            act.dma_start(Z[:, 0:len(LEVELS) * P], A["levels"]).then_inc(s["tables_loaded"], 16)
            act.dma_start(rw[:], A["router_w"].rearrange("(k p) e -> p k e", p=P)).then_inc(s["tables_loaded"], 16)
            act.dma_start(rb[:], A["router_b"].rearrange("(e o) -> e o", o=1)).then_inc(s["tables_loaded"], 16)
            for t in range(4):
                act.dma_start(x[:, t, :], A["x_prompt"][0, t * P:(t + 1) * P, :]).then_inc(s["x_loaded"], 16)
            act.dma_start(x[0:DEC_BATCH, 4, :], A["x_sample"].rearrange("b o d -> (b o) d")).then_inc(s["x_loaded"], 16)
            act.wait_ge(s["gw_zero"], 1)
            act.wait_ge(s["tables_ready"], 1)
            with act.Fori(0, DEPTH) as l:
                turns = [0]

                def turn():
                    turns[0] += 1
                    return 4 * ((turns[0] - 1) % 2)
                act.wait_ge(s["passes_known"], l + 1)
                before = act.value_load(passes_i[0:1, bass.ds(l, 1)], min_val=0, max_val=DEPTH * PASSES)
                base = act.snap(l * MIX_UNITS + before * PASS_UNITS)
                act.wait_ge(s["x_tile_ready"], (l + 1) * TILES)
                for c in range(2):
                    cs = slice(c * P, (c + 1) * P)
                    act.dma_start(convw[:, c, :], A["conv_w"][l, :, cs].rearrange("j p -> p j"),
                                  allow_slow_non_contiguous=True).then_inc(s["params_loaded"], 16)
                    act.dma_start(convb[:, c:c + 1], A["conv_b"][l, cs].rearrange("(p o) -> p o", o=1)).then_inc(s["params_loaded"], 16)
                    act.dma_start(lam[:, c:c + 1], A["rglru_lambda"][l, cs].rearrange("(p o) -> p o", o=1)).then_inc(s["params_loaded"], 16)
                    for d in range(DEPTH):
                        act.dma_start(lbl[:, d, c:c + 1], A["hgrn_lb_logits"][d, cs].rearrange("(p o) -> p o", o=1)).then_inc(s["params_loaded"], 16)
                    act.dma_start(h0[:, c, :], A["state_rglru_h"][l, :, cs].rearrange("n p -> p n"),
                                  allow_slow_non_contiguous=True).then_inc(s["params_loaded"], 16)
                    for jj in range(CONV_W - 1):
                        act.dma_start(csst[:, c, jj, :], A["state_conv"][l, :, jj, cs].rearrange("n p -> p n"),
                                      allow_slow_non_contiguous=True).then_inc(s["params_loaded"], 16)
                for gate, (w, bb) in enumerate((("w_rgate", "b_rgate"), ("w_igate", "b_igate"))):
                    for g4 in range(4):
                        pr, c = slice(64 * (g4 % 2), 64 * (g4 % 2) + 64), g4 // 2
                        act.dma_start(gw[pr, gate, c, pr], A[w][l, g4, :, :]).then_inc(s["params_loaded"], 16)
                        act.dma_start(gbias[pr, gate, c:c + 1], A[bb][l, g4, :].rearrange("(p o) -> p o", o=1)).then_inc(s["params_loaded"], 16)
                for hh in range(2):
                    act.dma_start(ng[64 * hh:64 * hh + 64, :], A["hgrn_norm_g"][l, :].rearrange("(p o) -> p o", o=1)).then_inc(s["params_loaded"], 16)
                act.dma_start(flag[:], A["layer_flag"][l]).then_inc(s["params_loaded"], 16)
                act.dma_start(o_cs[l, :, 0:2, :], A["state_conv"][l, :, 1:3, :]).then_inc(s["out_done"], 16)

                for t in range(TILES):
                    r = rows_of(t)
                    b = turn()
                    act.wait_ge(s["xT_ps"], l * TILES + t + 1)
                    src = ps[:, b:b + 2, :].rearrange("p b (k c) -> p (b k) c", c=P)[:, :, 0:r]
                    nc.scalar.activation(xsT[:, 0, :, t * P:t * P + r], src, ACT.Copy).then_inc(s["xT_high"], 1)
                act.wait_ge(s["small_in"], l + 1)
                nc.scalar.activation(lamt[:, 0, :], lamt[:, 0, :], ACT.Exp)
                nc.scalar.activation(lbt[:, 1:3, :], lbt[:, 1:3, :], ACT.Exp)
                act.drain()
                act.sem_inc(s["small_exp"], 1)
                parts = [0]

                def part():
                    b = turn()
                    parts[0] += 1
                    act.wait_ge(s["w_used"], base + 2 * parts[0] + SPLIT_SLOTS)
                    return b, ps[:, b:b + 4, 0:HALF]

                def quad4(v):
                    return v.rearrange("p c (h t) -> p (c h) t", h=2)
                b, q4 = part()
                pv = ps[:, b:b + 4, 0:HALF].rearrange("p (c h) t -> p c h t", c=2)
                act.wait_ge(s["params_ready"], l + 1)
                nc.scalar.activation(a_x[:, :, 3:3 + HALF], pv[:, :, 0, :], ACT.Copy)
                nc.scalar.activation(a_x[:, :, 3 + HALF:3 + SEQ], pv[:, :, 1, 0:SEQ - HALF], ACT.Copy)
                nc.scalar.activation(a_xs[:, :, 3, :], pv[:, :, 1, SEQ - HALF:HALF], ACT.Copy)
                act.drain()
                act.sem_inc(quad_free[b // 4], 1)
                act.sem_inc(s["xa_sb"], 1)
                b, q4 = part()
                nc.scalar.activation(quad4(a_g), q4, ACT.Gelu_apprx_tanh).then_inc(quad_free[b // 4], 1)
                b, q4 = part()
                nc.scalar.activation(quad4(b_f), q4, ACT.Sigmoid).then_inc(s["f_sig"], 1)
                nc.scalar.activation(quad4(b_k), q4, ACT.Sigmoid, scale=-1.0)
                act.drain()
                act.sem_inc(s["k_sig"], 1)
                act.sem_inc(quad_free[b // 4], 1)
                b, q4 = part()
                nc.scalar.activation(quad4(b_q), q4, ACT.Silu)
                act.drain()
                act.sem_inc(s["q_silu"], 1)
                act.sem_inc(quad_free[b // 4], 1)
                for gate, (dst, name) in enumerate(((a_r, "r_gate"), (a_i, "i_gate"))):
                    b = turn()
                    act.wait_ge(s["gates_ps"], 2 * l + gate + 1)
                    for c in range(2):
                        nc.scalar.activation(dst[:, c, :].rearrange("p (h t) -> p h t", h=2), ps[:, b + 2 * c:b + 2 * c + 2, 0:HALF],
                                             ACT.Sigmoid, bias=gbias[:, gate, c:c + 1])
                    act.drain()
                    act.sem_inc(s[name], 1)
                    act.sem_inc(quad_free[b // 4], 1)
                for c in range(2):
                    nc.scalar.activation(a_t[:, c, :], a_r[:, c, :], ACT.Tanh, scale=c8[:, c:c + 1])
                for c in range(2):
                    nc.scalar.activation(a_a[:, c, :], a_r[:, c, :], ACT.Exp, scale=c8[:, c:c + 1])
                act.drain()
                act.sem_inc(s["tanh_a"], 1)
                b, q4 = part()
                nc.scalar.activation(b_v[:, 0:4, :], ps[:, b:b + 4, 0:256], ACT.Copy)
                nc.scalar.activation(b_v[0:DEC_BATCH, 4, :], ps[0:DEC_BATCH, b, 256:512], ACT.Copy)
                act.drain()
                act.sem_inc(s["v_b"], 1)
                act.sem_inc(quad_free[b // 4], 1)
                b, q4 = part()
                nc.scalar.activation(quad4(b_g), q4, ACT.Silu)
                act.drain()
                act.sem_inc(s["g_b"], 1)
                act.sem_inc(quad_free[b // 4], 1)
                act.wait_ge(s["ratio_ready"], l + 1)
                nc.scalar.activation(a_t[:], a_t[:], ACT.Sqrt).then_inc(s["sqrt_a"], 1)
                b = turn()
                act.wait_ge(s["states_ps"], l + 1)
                nc.scalar.activation(outst_t[:], ps[0:20, b, 0:D_A], ACT.Copy)
                act.drain()
                act.sem_inc(quad_free[b // 4], 1)
                act.dma_start(o_hp[l], outst_t[0:1, :]).then_inc(s["states_t"], 16)
                act.dma_start(o_cp[l, 0], outst_t[1:4, :]).then_inc(s["states_t"], 16)
                act.dma_start(o_hs[l], outst_t[4:12, :]).then_inc(s["states_t"], 16)
                act.dma_start(o_cs[l, :, 2, :], outst_t[12:20, :]).then_inc(s["states_t"], 16)
                act.wait_ge(s["y_a"], l + 1)
                for h in range(4):
                    act.dma_start(b_S0[64 * (h % 2):64 * (h % 2) + 64, h // 2], A["state_hgrn"][l, :, h].rearrange("n k v -> k n v"))\
                       .then_inc(s["hg_in"], 16)
                act.wait_ge(s["clamped"], l + 1)
                nc.scalar.activation(b_t1[:], b_t1[:], ACT.Ln)
                nc.scalar.activation(b_t2[:], b_t2[:], ACT.Ln)
                act.drain()
                act.sem_inc(s["log_ab"], 1)
                for n in range(len(LEVELS)):
                    act.wait_ge(s["arg_ready"], l * len(LEVELS) + n + 1)
                    nc.scalar.activation(b_t1[:, :, 0:SEQ], b_t1[:, :, 0:SEQ], ACT.Exp).then_inc(s["e_ready"], 1)
                act.wait_ge(s["eb_ready"], 2 * l + 1)
                nc.scalar.activation(b_t1[:, :, 0:SEQ], b_b[:, :, 0:SEQ], ACT.Exp)
                nc.scalar.activation(bl[:], b_b[:, :, CHUNK_B - 1:SEQ:CHUNK_B], ACT.Exp)
                nc.scalar.activation(b_t2[:, :, 0:SEQ], b_t2[:, :, 0:SEQ], ACT.Exp)
                act.drain()
                act.sem_inc(s["eb_ready"], 1)
                turns[0] += len(LEVELS) + 1
                b = turn()
                act.wait_ge(s["tr_ps"], l + 1)
                nc.scalar.activation(ksT[:], ps[0:DEC_BATCH, b + 2, 0:256], ACT.Copy)
                act.wait_ge(s["states_t"], (l + 1) * 64)
                nc.scalar.activation(b_kT, ps[:, b:b + 2, :].rearrange("p b (t c) -> p (b t) c", t=2), ACT.Copy)
                act.drain()
                act.sem_inc(s["ks_sb"], 1)
                act.sem_inc(s["kT_sb"], 1)
                act.sem_inc(quad_free[b // 4], 1)
                turn()
                turn()
                b = turn()
                act.wait_ge(s["o_ps"], l + 1)
                nc.scalar.activation(b_t1[:, :, 0:SEQ], ps[:, b:b + 2, :], ACT.Copy)
                nc.scalar.activation(b_t1[:, :, SEQ:TOK], ps[:, b + 2, 0:16].rearrange("p (c n) -> p c n", c=2), ACT.Copy)
                nc.scalar.activation(b_t2[:, :, 0:SEQ], ps[:, b:b + 2, :], ACT.Square)
                nc.scalar.activation(b_t2[:, :, SEQ:TOK], ps[:, b + 2, 0:16].rearrange("p (c n) -> p c n", c=2), ACT.Square)
                act.drain()
                act.sem_inc(s["sq_sb"], 1)
                act.sem_inc(quad_free[b // 4], 1)
                for hh in range(2):
                    pr = slice(64 * hh, 64 * hh + 64)
                    act.dma_start(o_gp[l, 0].rearrange("(c hh) k v -> hh k c v", hh=2)[hh], b_S[pr, CHUNKS_B, :, 64 * hh:64 * hh + 64])\
                       .then_inc(s["hg_out"], 16)
                for h in range(4):
                    act.dma_start(o_gs[l, :, h].rearrange("n k v -> k n v"), b_S0[64 * (h % 2):64 * (h % 2) + 64, h // 2])\
                       .then_inc(s["hg_out"], 16)
                b = turn()
                act.wait_ge(s["ms_ps"], l + 1)
                nc.scalar.activation(quad4(b_b), ps[:, b:b + 4, 0:HALF], ACT.Sqrt, bias=eps[:, 1:2])
                act.drain()
                act.sem_inc(s["ms_sqrt"], 1)
                act.sem_inc(quad_free[b // 4], 1)

                for j in range(2):
                    n2 = l * 2 + j + 1
                    if j == 0:
                        act.wait_ge(s["y_b"], l + 1)
                        act.wait_ge(s["hg_out"], (l + 1) * 96)
                    else:
                        act.wait_ge(s["y_c"], l * 2 + 1)
                        act.wait_ge(s["cs_out"], (l * 2 + 1) * 64)
                    for h in range(2):
                        act.dma_start(c_S0[:, h], A["state_ret"][l, :, 2 * j + h].rearrange("n k v -> k n v")).then_inc(s["cs_in"], 16)
                    for i, name in enumerate(("kc", "qc")):
                        b, q4 = part()
                        if i == 1:
                            act.wait_ge(s["rot_k"], n2)
                        for lo in (0, 64):
                            nc.scalar.activation(quad4(c_sw)[64 - lo:128 - lo], ps[lo:lo + 64, b:b + 4, 0:HALF], ACT.Copy)
                        act.drain()
                        act.sem_inc(s["rot_swapped"], 1)
                    b, q4 = part()
                    nc.scalar.activation(c_v[:, 0:4, :], ps[:, b:b + 4, 0:256], ACT.Copy)
                    nc.scalar.activation(c_v[0:DEC_BATCH, 4, :], ps[0:DEC_BATCH, b, 256:512], ACT.Copy)
                    act.drain()
                    act.sem_inc(s["v_c"], 1)
                    act.sem_inc(quad_free[b // 4], 1)
                    b, q4 = part()
                    nc.scalar.activation(quad4(c_g), q4, ACT.Silu)
                    act.drain()
                    act.sem_inc(s["g_c"], 1)
                    act.sem_inc(quad_free[b // 4], 1)
                    turn()
                    b = turn()
                    act.wait_ge(s["ctr_ps"], n2)
                    nc.scalar.activation(ksT[:], ps[0:DEC_BATCH, b + 2, 0:256], ACT.Copy, scale=float(DK_C ** -0.5))
                    act.drain()
                    act.sem_inc(s["cks_sb"], 1)
                    for h in range(2):
                        nc.scalar.activation(c_kT[:, :, h, :], ps[:, b:b + 2, :].rearrange("p b (t h c) -> p (b t) h c", t=2, h=2)[:, :, h, :],
                                             ACT.Copy, scale=table("kdec")[:, 2 * j + h:2 * j + h + 1])
                    act.drain()
                    act.sem_inc(s["ckT_sb"], 1)
                    act.sem_inc(quad_free[b // 4], 1)
                    turn()
                    turn()
                    b = turn()
                    act.wait_ge(s["co_ps"], n2)
                    nc.scalar.activation(c_t1[:, :, 0:SEQ], ps[:, b:b + 2, :], ACT.Copy)
                    nc.scalar.activation(c_t1[:, :, SEQ:TOK], ps[:, b + 2, 0:16].rearrange("p (c n) -> p c n", c=2), ACT.Copy)
                    act.drain()
                    act.sem_inc(s["co_sb"], 1)
                    act.sem_inc(quad_free[b // 4], 1)
                    for h in range(2):
                        act.dma_start(o_rp[l, 0, 2 * j + h], c_S[:, 4, h, :]).then_inc(s["cs_out"], 16)
                        act.dma_start(o_rs[l, :, 2 * j + h].rearrange("n k v -> k n v"), c_S0[:, h]).then_inc(s["cs_out"], 16)
                    turn()
                    act.wait_ge(s["cd_ready"], n2)
                    nc.scalar.activation(c_sw[:], c_t1[:], ACT.Square).then_inc(s["csq_sb"], 1)
                    b = turn()
                    act.wait_ge(s["cvar_ps"], n2)
                    nc.scalar.activation(quad4(c_sw), ps[:, b:b + 4, 0:HALF], ACT.Sqrt, bias=eps[:, 2:3])
                    act.drain()
                    act.sem_inc(s["cvar_sqrt"], 1)
                    act.sem_inc(quad_free[b // 4], 1)

                act.wait_ge(s["y_c"], 2 * l + 2)
                for k in range(0, KC, 2):
                    nc.scalar.activation(ysT[:, 0, k:k + 2, :], y32[:, k:k + 2, :], ACT.Copy).then_inc(s["y_high"], 1)
                turns[0] += 4
                act.wait_ge(s["y_low"], l + 1)
                act.wait_ge(s["cs_out"], (l + 1) * 128)
                for n, nm in enumerate(("ln1_g", "ln1_b")):
                    act.dma_start(lngb1[:, n, :], A[nm][bass.ds(l, 1), :].to_broadcast([P, D_MODEL])).then_inc(s["ln_loaded"], 16)
                act.wait_ge(s["mv_ready"], 2 * l + 1)
                nc.scalar.activation(lnrs[:, :, 0], mv[:, :, 1], ACT.Sqrt, bias=eps[:, 0:1]).then_inc(s["std_ready"], 1)
                act.wait_ge(s["lnrs_ready"], 2 * l + 1)
                for t in range(TILES):
                    r = rows_of(t)
                    nc.scalar.activation(x[0:r, t, :], x[0:r, t, :], ACT.Identity, bias=lnrs[0:r, t, 1:2],
                                         scale=lnrs[0:r, t, 0:1]).then_inc(s["ln_scaled"], 1)
                for t in range(TILES):
                    r = rows_of(t)
                    b = turn()
                    act.wait_ge(s["ln1_done"], l * TILES + t + 1)
                    nc.scalar.activation(xsM[0:r, 0, t, :], x[0:r, t, :], ACT.Copy).then_inc(s["xm_high"], 1)
                    act.wait_ge(s["x1T_ps"], l * TILES + t + 1)
                    src = ps[:, b:b + 2, :].rearrange("p b (k c) -> p (b k) c", c=P)[:, :, 0:r]
                    nc.scalar.activation(x1T[:, :, t * P:t * P + r], src, ACT.Copy)
                    act.drain()
                    act.sem_inc(s["x1T_sb"], 1)
                    act.sem_inc(quad_free[b // 4], 1)
                for n, nm in enumerate(("ln2_g", "ln2_b")):
                    act.dma_start(lngb2[:, n, :], A[nm][bass.ds(l, 1), :].to_broadcast([P, D_MODEL])).then_inc(s["ln_loaded"], 16)
                b = turn()
                act.wait_ge(s["lgT_ps"], l + 1)
                nc.scalar.activation(lgT.rearrange("p (h t) -> p h t", h=2), ps[0:N_EXPERTS, b:b + 2, 0:HALF], ACT.Identity, bias=rb[:, 0:1])
                act.drain()
                act.sem_inc(s["lgT_sb"], 1)
                act.sem_inc(quad_free[b // 4], 1)
                act.wait_ge(s["lg_shifted"], l + 1)
                nc.scalar.activation(rt[:, 0], rt[:, 0], ACT.Exp).then_inc(s["prob_exp"], 1)

                act.wait_ge(s["routed"], l + 1)
                act.wait_ge(s["xm_low"], (l + 1) * TILES)
                for t in range(TILES):
                    r = rows_of(t)
                    nc.scalar.activation(x[0:r, t, :], x[0:r, t, :], ACT.Copy, scale=float(ALPHA)).then_inc(s["x_scaled"], 1)
                most = act.value_load(cnt_i[0:1, bass.ds(l, 1)], min_val=0, max_val=TOK)
                with act.Fori(0, PASSES) as rnd:
                    with act.If(most > rnd * SLOTS):
                        with act.Fori(0, PAIRS) as g:
                            n = act.snap((before + rnd) * PAIRS + g)
                            first = act.snap(base + MIX_UNITS + rnd * PASS_UNITS + g * PAIR_UNITS + SPLIT_SLOTS)
                            for k in range(KC // 2):
                                act.wait_ge(s["gath_ps"], n * (KC // 2) + k + 1)
                                nc.scalar.activation(XeT[:, 0, 2 * k:2 * k + 2, :].rearrange("p k c -> p (k c)"), ps[:, k, :], ACT.Copy)\
                                    .then_inc(s["gath_high"], 1)
                            for e in range(2):
                                act.wait_ge(s["pt_ps"], n * 2 + e + 1)
                                nc.scalar.activation(PT[:, e, :], ps[:, 4 + e, :].bitcast(bf16)[:, 0:TOK], ACT.Copy)
                                act.drain()
                                act.sem_inc(s["pt_sb"], 1)
                                act.sem_inc(bank_free[4 + e], 1)

                            def silu(e):
                                act.wait_ge(s["w_used"], first + GATE_DONE[e])
                                act.wait_ge(s["h_done"], n * 2 + e + 1)
                                nc.scalar.activation(act_g[:], ps[:, 2 * (e % 2), :], ACT.Silu)
                                act.drain()
                                act.sem_inc(s["silu_done"], 1)
                                act.sem_inc(bank_free[2 * (e % 2)], 1)

                            def ht(e):
                                act.wait_ge(s["ht_ps"], n * 2 + e + 1)
                                nc.scalar.activation(hT[:, 0].rearrange("p q c -> p (q c)"), ps[:, 4, :], ACT.Copy).then_inc(s["ht_high"], 1)

                            def out(e):
                                for half in range(2):
                                    act.wait_ge(s["w_used"], first + DOWN_FROM[e] + 2 * half + 2)
                                    nc.scalar.activation(ye[:, e % 2, 0, half * 512:half * 512 + 512], ps[:, 5 + half, :], ACT.Copy)\
                                        .then_inc(s["ye_high"], 1)
                            silu(0)
                            silu(1)
                            ht(0)
                            out(0)
                            ht(1)
                            out(1)
                act.wait_ge(s["mv_ready"], 2 * l + 2)
                nc.scalar.activation(lnrs[:, :, 0], mv[:, :, 1], ACT.Sqrt, bias=eps[:, 0:1]).then_inc(s["std_ready"], 1)
                act.wait_ge(s["lnrs_ready"], 2 * l + 2)
                for t in range(TILES):
                    r = rows_of(t)
                    nc.scalar.activation(x[0:r, t, :], x[0:r, t, :], ACT.Identity, bias=lnrs[0:r, t, 1:2],
                                         scale=lnrs[0:r, t, 0:1]).then_inc(s["ln2_scaled"], 1)
            for t in range(4):
                act.wait_ge(s["x_tile_ready"], DEPTH * TILES + t + 1)
                act.dma_start(o_yp[0, t * P:(t + 1) * P, :], x[:, t, :]).then_inc(s["out_done"], 16)
            act.wait_ge(s["x_tile_ready"], (DEPTH + 1) * TILES)
            act.dma_start(o_ys.rearrange("b o d -> (b o) d"), x[0:DEC_BATCH, 4, :]).then_inc(s["out_done"], 16)
            act.wait_ge(s["out_done"], (DEPTH + TILES) * 16)
            act.wait_ge(s["states_t"], DEPTH * 64)
            act.wait_ge(s["hg_out"], DEPTH * 96)
            act.wait_ge(s["cs_out"], DEPTH * 2 * 64)

        @block.vector
        def _(dve):
            V = nc.vector
            TT, TS, STT = V.tensor_tensor, V.tensor_scalar, V.scalar_tensor_tensor
            dve.sem_inc(s["w_split"], RAW_SLOTS)
            dve.sem_inc(s["w_used"], SPLIT_SLOTS)
            dve.sem_inc(s["h_done"], 1)
            for q in quad_free + bank_free:
                dve.sem_inc(q, 1)
            V.memset(passes_i[:], 0)
            V.memset(passes_f[:], 0.0)
            V.memset(eps[:, 0:1], LN_EPS)
            V.memset(eps[:, 1:2], RMS_EPS)
            V.memset(eps[:, 2:3], GN_EPS)
            V.memset(ones_bf[:], 1.0)
            V.memset(lg[:], 0.0)
            V.memset(mv[:], 1.0)
            V.memset(posm[:], 0.0)
            dve.drain()
            dve.sem_inc(s["passes_known"], 1)
            dve.wait_ge(s["tables_loaded"], 64)
            nc.vector.tensor_copy(lev[:], Z[:, 0:len(LEVELS) * P])
            V.tensor_copy(before_bf[:], table("before"))
            V.tensor_copy(ident_bf[:], ident)
            dve.drain()
            dve.sem_inc(s["tables_ready"], 1)
            dve.wait_ge(s["x_loaded"], TILES * 16)
            dve.sem_inc(s["x_tile_ready"], TILES)

            with dve.Fori(0, DEPTH) as l:
                dve.wait_ge(s["passes_known"], l + 1)
                before = dve.value_load(passes_i[0:1, bass.ds(l, 1)], min_val=0, max_val=DEPTH * PASSES)
                base = dve.snap(l * MIX_UNITS + before * PASS_UNITS)
                turns = [0]
                lows = [0]
                parts = [0]

                def turn():
                    turns[0] += 1
                    return 4 * ((turns[0] - 1) % 2)

                def low(first, k):
                    dve.wait_ge(s["w_high"], first + k + 1)
                    TT(ws[:, k % SPLIT_SLOTS, 1, :], raw[:, k % RAW_SLOTS, :], ws[:, k % SPLIT_SLOTS, 0, :].bitcast(f32),
                       ALU.subtract).then_inc(s["w_split"], 1)

                def next_part(n=1):
                    for _ in range(2 * n):
                        low(base, lows[0])
                        lows[0] += 1

                next_part(2)
                for t in range(TILES):
                    r = rows_of(t)
                    b = turn()
                    dve.wait_ge(s["xT_high"], l * TILES + t + 1)
                    src = ps[:, b:b + 2, :].rearrange("p b (k c) -> p (b k) c", c=P)[:, :, 0:r]
                    TT(xsT[:, 1, :, t * P:t * P + r], src, xsT[:, 0, :, t * P:t * P + r].bitcast(f32), ALU.subtract)
                    dve.drain()
                    dve.sem_inc(s["xT_low"], 1)
                    dve.sem_inc(quad_free[b // 4], 1)

                dve.wait_ge(s["params_loaded"], (l + 1) * (2 * 9 + 16 + 3) * 16 - 0)
                STT(lamt[:, 0, :], lam[:], -1.0, lam[:], ALU.mult, ALU.min)
                V.tensor_tensor(lbt[:, 0, :], lbl[:, 0, :], lbl[:, 1, :], ALU.max)
                dve.drain()
                TT(lbt[:, 1, :], lbl[:, 0, :], lbt[:, 0, :], ALU.subtract)
                TT(lbt[:, 2, :], lbl[:, 1, :], lbt[:, 0, :], ALU.subtract)
                dve.drain()
                dve.sem_inc(s["small_in"], 1)
                dve.wait_ge(s["small_exp"], l + 1)
                TS(lamt[:, 1, :], lamt[:, 0, :], 2.0, None, ALU.add)
                TT(lbt[:, 3, :], lbt[:, 1, :], lbt[:, 2, :], ALU.add)
                dve.drain()
                V.reciprocal(lamt[:, 2, :], lamt[:, 1, :])
                V.reciprocal(lbt[:, 4, :], lbt[:, 3, :])
                dve.drain()
                TT(lamt[:, 0, :], lamt[:, 0, :], lamt[:, 2, :], ALU.mult)
                STT(lb[:], lbt[:, 2, :], flag[:, 0:1], lbt[:, 4, :], ALU.mult, ALU.mult)
                dve.drain()
                TT(lamt[:, 1, :], lamt[:, 0, :], lamt[:, 0, :], ALU.mult)
                TS(oml[:], lb[:], -1.0, 1.0, ALU.mult, ALU.add)
                V.memset(lamt[:, 2, :], 1.0 / 17)
                dve.drain()
                for odd in (15, 13, 11, 9, 7, 5, 3, 1):
                    TT(lamt[:, 2, :], lamt[:, 2, :], lamt[:, 1, :], ALU.mult)
                    dve.drain()
                    TS(lamt[:, 2, :], lamt[:, 2, :], 1.0 / odd, None, ALU.add)
                    dve.drain()
                TT(lamt[:, 2, :], lamt[:, 2, :], lamt[:, 0, :], ALU.mult)
                TS(lamt[:, 1, :], lam[:], 0.0, RGLRU_C, ALU.min, ALU.mult)
                dve.drain()
                STT(c8[:], lamt[:, 2, :], -2.0 * RGLRU_C, lamt[:, 1, :], ALU.mult, ALU.add)
                V.memset(a_x[:, :, 0:3], 0.0)
                for c in range(2):
                    V.tensor_copy(a_xs[:, c, 0:3, :], csst[:, c])
                dve.drain()
                dve.sem_inc(s["params_ready"], 1)

                next_part()
                dve.wait_ge(s["xa_sb"], l + 1)
                for j in range(CONV_W):
                    for c in range(2):
                        taps = ((a_u[:, c, 0:SEQ], a_x[:, c, j:j + SEQ]), (a_u[:, c, SEQ:TOK], a_xs[:, c, j, :]))
                        for dst, src in taps:
                            if j == 0:
                                TS(dst, src, convw[:, c, 0:1], convb[:, c:c + 1], ALU.mult, ALU.add)
                            else:
                                STT(dst, src, convw[:, c, j:j + 1], dst, ALU.mult, ALU.add)
                    dve.drain()
                dve.sem_inc(s["u_ready"], 1)
                next_part()
                turns[0] += 4
                turns[0] += 2
                next_part()
                dve.wait_ge(s["tanh_a"], l + 1)
                TS(a_r[:], a_t[:], -1.0, 1.0, ALU.mult, ALU.add)
                TT(a_i[:], a_i[:], a_u[:], ALU.mult)
                dve.drain()
                V.reciprocal(a_r[:], a_r[:])
                dve.drain()
                TT(a_t[:], a_t[:], a_r[:], ALU.mult)
                dve.drain()
                TS(a_t[:], a_t[:], -2.0, 0.0, ALU.mult, ALU.max)
                dve.drain()
                dve.sem_inc(s["ratio_ready"], 1)
                next_part()
                dve.wait_ge(s["k_sig"], l + 1)
                for c in range(2):
                    TS(b_f[:, c, :], b_f[:, c, :], oml[:, c:c + 1], lb[:, c:c + 1], ALU.mult, ALU.add)
                    TS(b_k[:, c, :], b_k[:, c, :], oml[:, c:c + 1], None, ALU.mult)
                dve.drain()
                TS(b_f[:], b_f[:], F_TINY, None, ALU.max).then_inc(s["k_ready"], 1)
                dve.wait_ge(s["sqrt_a"], l + 1)
                TT(a_t[:], a_t[:], a_i[:], ALU.mult)
                dve.drain()
                for c in range(2):
                    V.tensor_tensor_scan(a_i[:, c, 0:SEQ], a_a[:, c, 0:SEQ], a_t[:, c, 0:SEQ], 0.0, ALU.mult, ALU.add)
                TT(a_i[:, :, SEQ:TOK], a_a[:, :, SEQ:TOK], h0[:], ALU.mult)
                dve.drain()
                TT(a_i[:, :, SEQ:TOK], a_i[:, :, SEQ:TOK], a_t[:, :, SEQ:TOK], ALU.add)
                dve.drain()
                V.tensor_copy(outst[:, :, 0:1], a_i[:, :, SEQ - 1:SEQ])
                V.tensor_copy(outst[:, :, 1:4], a_x[:, :, SEQ:SEQ + 3])
                V.tensor_copy(outst[:, :, 4:12], a_i[:, :, SEQ:TOK])
                V.tensor_copy(outst[:, :, 12:20], a_xs[:, :, 3, :])
                TT(y32[:, 0:2, :], a_i[:], a_g[:], ALU.mult)
                dve.drain()
                dve.sem_inc(s["states_sb"], 1)
                dve.sem_inc(s["y_a"], 1)
                turns[0] += 3

                TS(b_t1[:], b_f[:], F_SPLIT, None, ALU.max)
                TS(b_t2[:], b_f[:], 1.0 / F_SPLIT, 1.0, ALU.mult, ALU.min)
                dve.drain()
                dve.sem_inc(s["clamped"], 1)
                next_part(2)
                dve.wait_ge(s["v_b"], l + 1)
                for h in range(4):
                    TT(b_Vx[:, h], b_v[0:DEC_BATCH, 4, h * 64:(h + 1) * 64].unsqueeze(1).to_broadcast([DEC_BATCH, DEC_BATCH, 64]),
                       table("seqdelta", DEC_BATCH).unsqueeze(2).to_broadcast([DEC_BATCH, DEC_BATCH, 64]), ALU.mult)
                dve.drain()
                dve.sem_inc(s["vx_ready"], 1)
                b = turn()
                dve.wait_ge(s["lev_ps"], l * (len(LEVELS) + 1) + 1)
                acc16 = b_acc.rearrange("p h t c s -> p (h t c) s")
                TT(acc16, ps[:, b:b + 4, :].rearrange("p b (n s) -> p (b n) s", s=P), ident.unsqueeze(1).to_broadcast([P, 16, P]), ALU.mult)
                dve.drain()
                dve.sem_inc(s["lev_done"], 1)
                dve.sem_inc(quad_free[b // 4], 1)
                dve.wait_ge(s["log_ab"], l + 1)
                TT(b_t1[:], b_t1[:], b_t2[:], ALU.add)
                dve.drain()
                for c in range(2):
                    V.tensor_tensor_scan(b_b[:, c, 0:SEQ], table("reset"), b_t1[:, c, 0:SEQ], 0.0, ALU.mult, ALU.add)
                dve.drain()

                def level_done(n):
                    b = turn()
                    wait_apart(dve, s["lev_ps"], l * (len(LEVELS) + 1) + n + 2)
                    mask = lev[:, n * P:(n + 1) * P].unsqueeze(1).to_broadcast([P, 16, P])
                    V.copy_predicated(acc16, mask, ps[:, b:b + 4, :].rearrange("p b (n s) -> p (b n) s", s=P))
                    dve.drain()
                    dve.sem_inc(s["lev_done"], 1)
                    dve.sem_inc(quad_free[b // 4], 1)
                for n, m in enumerate(LEVELS):
                    for c in range(2):
                        bb = b_b[:, c, 0:SEQ].rearrange("p (n m) -> p n m", m=2 * m)
                        ee = b_t1[:, c, 0:SEQ].rearrange("p (n m) -> p n m", m=2 * m)
                        mid = bb[:, :, m - 1:m].to_broadcast([P, SEQ // (2 * m), m])
                        TT(ee[:, :, m:2 * m], bb[:, :, m:2 * m], mid, ALU.subtract)
                        TT(ee[:, :, 0:m], mid, bb[:, :, 0:m], ALU.subtract)
                    dve.drain()
                    dve.sem_inc(s["arg_ready"], 1)
                    if n > 0:
                        level_done(n - 1)
                    dve.wait_ge(s["e_ready"], l * len(LEVELS) + n + 1)
                    for c in range(2):
                        ee = b_t1[:, c, 0:SEQ].rearrange("p (n m) -> p n m", m=2 * m)
                        oo = b_t2[:, c, 0:SEQ].rearrange("p (n m) -> p n m", m=2 * m)
                        qq = b_q[:, c, 0:SEQ].rearrange("p (n m) -> p n m", m=2 * m)
                        kk = b_k[:, c, 0:SEQ].rearrange("p (n m) -> p n m", m=2 * m)
                        TT(oo[:, :, m:2 * m], qq[:, :, m:2 * m], ee[:, :, m:2 * m], ALU.mult)
                        TT(oo[:, :, 0:m], kk[:, :, 0:m], ee[:, :, 0:m], ALU.mult)
                    dve.drain()
                    dve.sem_inc(s["qk_ready"], 1)
                level_done(len(LEVELS) - 1)
                last = b_b[:, :, CHUNK_B - 1:SEQ:CHUNK_B].unsqueeze(3).to_broadcast([P, 2, CHUNKS_B, CHUNK_B])
                TT(b_t2[:, :, 0:SEQ].rearrange("p c (n m) -> p c n m", m=CHUNK_B), last,
                   b_b[:, :, 0:SEQ].rearrange("p c (n m) -> p c n m", m=CHUNK_B), ALU.subtract)
                dve.drain()
                dve.sem_inc(s["eb_ready"], 1)
                dve.wait_ge(s["eb_ready"], 2 * l + 2)
                TT(b_q[:, :, 0:SEQ], b_q[:, :, 0:SEQ], b_t1[:, :, 0:SEQ], ALU.mult)
                TT(b_k[:, :, 0:SEQ], b_k[:, :, 0:SEQ], b_t2[:, :, 0:SEQ], ALU.mult)
                dve.drain()
                dve.sem_inc(s["p_ready"], 1)
                turn()
                b = turn()
                dve.wait_ge(s["hg_in"], (l + 1) * 64)
                TT(b_S0, b_S0, b_f[:, :, SEQ:TOK].unsqueeze(3).to_broadcast([P, 2, DEC_BATCH, DK_B]), ALU.mult)
                dve.drain()
                dve.wait_ge(s["kv_ps"], l + 1)
                TT(b_S0.rearrange("p c n v -> p c (n v)"), ps[:, b:b + 2, :], b_S0.rearrange("p c n v -> p c (n v)"), ALU.add)
                dve.drain()
                dve.sem_inc(s["s_new"], 1)
                dve.sem_inc(quad_free[b // 4], 1)
                b = turn()
                dve.wait_ge(s["ds_ps"], l + 1)
                V.memset(b_S[:, 0], 0.0)
                for odd in range(2):
                    TT(b_S[:, 1 + odd::2], ps[:, b + 2 * odd:b + 2 * odd + 2, :].rearrange("p b (n c k) -> p (b n) c k", c=2, k=P),
                       table("blockdiag").unsqueeze(1).unsqueeze(1).to_broadcast([P, 4, 2, P]), ALU.mult)
                dve.drain()
                dve.sem_inc(quad_free[b // 4], 1)
                for ch in range(1, CHUNKS_B):
                    for c in range(2):
                        STT(b_S[:, ch + 1, c, :], b_S[:, ch, c, :], bl[:, c, ch:ch + 1], b_S[:, ch + 1, c, :], ALU.mult, ALU.add)
                    dve.drain()
                dve.sem_inc(s["s_ready"], 1)
                turn()
                turn()
                dve.wait_ge(s["ms_sqrt"], l + 1)
                V.reciprocal(b_b[:], b_b[:])
                dve.drain()
                STT(b_t1[:], b_t1[:], ng[:, 0:1], b_b[:], ALU.mult, ALU.mult)
                dve.drain()
                dve.wait_ge(s["g_b"], l + 1)
                TT(y32[:, 2:4, :], b_t1[:], b_g[:], ALU.mult)
                dve.drain()
                dve.sem_inc(s["y_b"], 1)

                cosb = table("cos").rearrange("p (h t) -> p h t", h=2)
                for j in range(2):
                    n2 = l * 2 + j + 1
                    for i, (dst, name) in enumerate(((c_k, "rot_k"), (c_q, "rot_q"))):
                        b = turn()
                        dve.wait_ge(s["rot_swapped"], l * 4 + 2 * j + i + 1)
                        pv = ps[:, b:b + 4, 0:HALF].rearrange("p (c h) t -> p c h t", c=2)
                        for c in range(2):
                            TT(dst[:, c, :].rearrange("p (h t) -> p h t", h=2), pv[:, c], cosb, ALU.mult)
                        dve.drain()
                        dve.sem_inc(quad_free[b // 4], 1)
                        next_part()
                        dve.wait_ge(s["rot_sin"], l * 4 + 2 * j + i + 1)
                        TT(dst[:], dst[:], c_sw[:], ALU.add)
                        dve.drain()
                        dve.sem_inc(s[name], 1)
                    turn()
                    turn()
                    next_part(2)
                    dve.wait_ge(s["v_c"], n2)
                    for h in range(2):
                        TT(c_Vx[:, h], c_v[0:DEC_BATCH, 4, h * P:(h + 1) * P].unsqueeze(1).to_broadcast([DEC_BATCH, DEC_BATCH, P]),
                           table("seqdelta", DEC_BATCH).unsqueeze(2).to_broadcast([DEC_BATCH, DEC_BATCH, P]), ALU.mult)
                    dve.drain()
                    dve.sem_inc(s["cvx_ready"], 1)
                    b = turn()
                    dve.wait_ge(s["sc_ps"], n2)
                    dm = table("dret").rearrange("p (h c) -> p h c", h=4)[:, 2 * j:2 * j + 2].unsqueeze(1).to_broadcast([P, 4, 2, P])
                    TT(c_sc, ps[:, b:b + 2, :].rearrange("p b (t h c) -> p (b t) h c", t=2, h=2), dm, ALU.mult)
                    qdt = table("qdec").rearrange("p (h c) -> p h c", h=4)[:, 2 * j:2 * j + 2].unsqueeze(2).to_broadcast([P, 2, 4, P])
                    TT(c_qd, c_q[:, :, 0:SEQ].rearrange("p h (t c) -> p h t c", t=4), qdt, ALU.mult)
                    dve.drain()
                    dve.sem_inc(s["sc_ready"], 1)
                    dve.sem_inc(s["qd_ready"], 1)
                    dve.sem_inc(quad_free[b // 4], 1)
                    turn()
                    b = turn()
                    dve.wait_ge(s["cs_in"], n2 * 32)
                    dve.wait_ge(s["ckv_ps"], n2)
                    for h in range(2):
                        v0 = c_S0[:, h].rearrange("p n v -> p (n v)").rearrange("p (b c) -> p b c", b=2)
                        STT(v0, v0, GAMMA[2 * j + h], ps[:, b + 2 * h:b + 2 * h + 2, :], ALU.mult, ALU.add)
                    dve.drain()
                    dve.sem_inc(s["cs_new"], 1)
                    dve.sem_inc(quad_free[b // 4], 1)
                    b = turn()
                    dve.wait_ge(s["cds_ps"], n2)
                    V.tensor_copy(c_S[:, 1:].rearrange("p t h c -> p (t h c)"), ps[:, b:b + 2, :].rearrange("p b c -> p (b c)"))
                    dve.drain()
                    dve.sem_inc(quad_free[b // 4], 1)
                    for t in range(1, 4):
                        for h in range(2):
                            STT(c_S[:, t + 1, h, :], c_S[:, t, h, :], GAMMA_CHUNK[2 * j + h], c_S[:, t + 1, h, :], ALU.mult, ALU.add)
                        dve.drain()
                    dve.sem_inc(s["cs_ready"], 1)
                    turn()
                    b = turn()
                    dve.wait_ge(s["cmean_ps"], n2)
                    o4 = c_t1.rearrange("p c (h t) -> p (c h) t", h=2)
                    TT(o4, o4, ps[:, b:b + 4, 0:HALF], ALU.subtract)
                    dve.drain()
                    dve.sem_inc(s["cd_ready"], 1)
                    dve.sem_inc(quad_free[b // 4], 1)
                    turn()
                    dve.wait_ge(s["g_c"], n2)
                    dve.wait_ge(s["csq_sb"], n2)
                    TT(c_t1[:], c_t1[:], c_g[:], ALU.mult)
                    dve.wait_ge(s["cvar_sqrt"], n2)
                    V.reciprocal(c_sw[:], c_sw[:])
                    dve.drain()
                    TT(y32[:, 4 + 2 * j:6 + 2 * j, :], c_t1[:], c_sw[:], ALU.mult)
                    dve.drain()
                    dve.sem_inc(s["y_c"], 1)

                for k in range(0, KC, 2):
                    dve.wait_ge(s["y_high"], l * 4 + k // 2 + 1)
                    TT(ysT[:, 1, k:k + 2, :], y32[:, k:k + 2, :], ysT[:, 0, k:k + 2, :].bitcast(f32), ALU.subtract)
                dve.drain()
                dve.sem_inc(s["y_low"], 1)
                for cc in range(4):
                    b = turn()
                    if cc < 2:
                        next_part()
                    cols = slice(cc * 256, cc * 256 + 256)
                    dve.wait_ge(s["w_used"], base + 2 * len(IN_PARTS) + 2 * cc + 2 + SPLIT_SLOTS)
                    STT(x[:, 0:4, cols], x[:, 0:4, cols], float(ALPHA), ps[:, b:b + 4, 0:256], ALU.mult, ALU.add)
                    STT(x[0:DEC_BATCH, 4, cols], x[0:DEC_BATCH, 4, cols], float(ALPHA), ps[0:DEC_BATCH, b, 256:512], ALU.mult, ALU.add)
                    dve.drain()
                    dve.sem_inc(quad_free[b // 4], 1)
                assert lows[0] == MIX_UNITS, lows

                def norm_stats(which):
                    for t in range(TILES):
                        r = rows_of(t)
                        for hf in range(2):
                            V.bn_stats(stats[0:r, t, 6 * hf:6 * hf + 6], x[0:r, t, hf * 512:hf * 512 + 512])
                    dve.drain()
                    for t in range(TILES):
                        r = rows_of(t)
                        V.bn_aggr(mv[0:r, t, :], stats[0:r, t, :])
                    dve.drain()
                    dve.sem_inc(s["mv_ready"], 1)
                    dve.wait_ge(s["std_ready"], 2 * l + which)
                    V.reciprocal(lnrs[:, :, 0], lnrs[:, :, 0])
                    dve.drain()
                    STT(lnrs[:, :, 1], mv[:, :, 0], -1.0, lnrs[:, :, 0], ALU.mult, ALU.mult)
                    dve.drain()
                    dve.sem_inc(s["lnrs_ready"], 1)

                def gain(t, gb):
                    r = rows_of(t)
                    TT(x[0:r, t, :], x[0:r, t, :], gb[0:r, 0, :], ALU.mult)
                    dve.drain()
                    TT(x[0:r, t, :], x[0:r, t, :], gb[0:r, 1, :], ALU.add)
                    dve.drain()

                norm_stats(1)
                dve.wait_ge(s["ln_loaded"], l * 64 + 32)
                for t in range(TILES):
                    dve.wait_ge(s["ln_scaled"], l * TILES + t + 1)
                    gain(t, lngb1)
                    dve.sem_inc(s["ln1_done"], 1)
                for t in range(TILES):
                    r = rows_of(t)
                    dve.wait_ge(s["xm_high"], l * TILES + t + 1)
                    TT(xsM[0:r, 1, t, :], x[0:r, t, :], xsM[0:r, 0, t, :].bitcast(f32), ALU.subtract).then_inc(s["xm_low"], 1)
                turns[0] += TILES + 1

                b = turn()
                dve.wait_ge(s["lg_ps"], l + 1)
                V.tensor_copy(lg[:, 0:4, :], ps[:, b, 0:64].rearrange("p (t e) -> p t e", t=4))
                V.tensor_copy(lg[0:DEC_BATCH, 4, :], ps[0:DEC_BATCH, b, 64:80])
                dve.drain()
                dve.sem_inc(quad_free[b // 4], 1)

                def top(out, src):
                    V.tensor_reduce(out, src, AX.X, ALU.max)
                    dve.drain()

                def wide(v):
                    return v.to_broadcast([P, TILES, N_EXPERTS])
                mx, sm = rg[:, 0, :, 0:1], rg[:, 0, :, 1:2]
                v1, v2, k1 = rg[:, 0, :, 2:3], rg[:, 0, :, 3:4], rg[:, 7, :, 0:1]
                top(mx, lg[:])
                TT(rt[:, 0], lg[:], wide(mx), ALU.subtract)
                dve.drain()
                dve.sem_inc(s["lg_shifted"], 1)
                dve.wait_ge(s["prob_exp"], l + 1)
                V.tensor_reduce(sm, rt[:, 0], AX.X, ALU.add)
                dve.drain()
                V.reciprocal(sm, sm)
                dve.drain()
                pr = rt[:, 0]
                TT(pr, pr, wide(sm), ALU.mult)
                dve.drain()
                p4 = pr.rearrange("p t (g e) -> p t g e", g=4)
                TT(rg[:, 1], p4[:, :, :, 0], p4[:, :, :, 1], ALU.max)
                TT(rg[:, 2], p4[:, :, :, 0], p4[:, :, :, 1], ALU.min)
                TT(rg[:, 3], p4[:, :, :, 2], p4[:, :, :, 3], ALU.max)
                TT(rg[:, 4], p4[:, :, :, 2], p4[:, :, :, 3], ALU.min)
                dve.drain()
                TT(rg[:, 5], rg[:, 1], rg[:, 3], ALU.max)
                TT(rg[:, 6], rg[:, 1], rg[:, 3], ALU.min)
                TT(rg[:, 2], rg[:, 2], rg[:, 4], ALU.max)
                dve.drain()
                TT(rg[:, 6], rg[:, 6], rg[:, 2], ALU.max)
                dve.drain()
                TT(rg[:, 5], rg[:, 5], rg[:, 6], ALU.add)
                dve.drain()

                def first_of(dst, src, best, key, scratch, n):
                    top(best, src)
                    TT(dst, src, best.to_broadcast([P, TILES, n]), ALU.is_equal)
                    dve.drain()
                    TT(dst, dst, key.unsqueeze(1).to_broadcast([P, TILES, n]), ALU.mult)
                    dve.drain()
                    top(scratch, dst)
                    TT(dst, dst, scratch.to_broadcast([P, TILES, n]), ALU.is_equal)
                    dve.drain()
                first_of(rg[:, 1], rg[:, 5], mx, table("key4"), k1, 4)
                selb = rg[:, 1].unsqueeze(3).to_broadcast([P, TILES, 4, 4])
                pm = rt[:, 1]
                pm4 = pm.rearrange("p t (g e) -> p t g e", g=4)
                TS(rg[:, 2], rg[:, 1], 1.0, None, ALU.subtract)
                for t in range(TILES):
                    TT(pm4[:, t], p4[:, t], selb[:, t], ALU.mult)
                dve.drain()
                for t in range(TILES):
                    TT(pm4[:, t], pm4[:, t], rg[:, 2].unsqueeze(3).to_broadcast([P, TILES, 4, 4])[:, t], ALU.add)
                dve.drain()
                first_of(rt[:, 2], pm, v1, table("key16"), k1, N_EXPERTS)
                STT(rt[:, 3], rt[:, 2], -4.0, pm, ALU.mult, ALU.add)
                dve.drain()
                first_of(rt[:, 4], rt[:, 3], v2, table("key16"), k1, N_EXPERTS)
                TT(rt[:, 5], rt[:, 2], rt[:, 4], ALU.add)
                TT(sm, v1, v2, ALU.add)
                dve.drain()
                V.tensor_copy(mask_bf[:], rt[:, 5])
                V.reciprocal(sm, sm)
                dve.drain()
                dve.sem_inc(s["mask_ready"], 1)
                TT(v1, v1, sm, ALU.mult)
                TT(v2, v2, sm, ALU.mult)
                dve.drain()
                TT(rt[:, 2], rt[:, 2], wide(v1), ALU.mult)
                TT(rt[:, 4], rt[:, 4], wide(v2), ALU.mult)
                dve.drain()
                TT(comb[:], rt[:, 2], rt[:, 4], ALU.add)
                b = turn()
                dve.wait_ge(s["pos_ps"], l + 1)
                TS(posm[:, 0:4, :], ps[:, b, 0:64].rearrange("p (t e) -> p t e", t=4), 1.0, None, ALU.add)
                TS(posm[0:DEC_BATCH, 4, :], ps[0:DEC_BATCH, b, 64:80], 1.0, None, ALU.add)
                V.tensor_reduce(cnt[:, 0:1], ps[:, b, 80:96], AX.X, ALU.max)
                dve.drain()
                dve.sem_inc(quad_free[b // 4], 1)
                TT(posm[:], posm[:], rt[:, 5], ALU.mult)
                V.tensor_copy(cnt_i[:, bass.ds(l, 1)], cnt[:, 0:1])
                for r in range(PASSES):
                    TS(cnt[:, 1 + r:2 + r], cnt[:, 0:1], float(r * SLOTS), None, ALU.is_gt)
                dve.drain()
                TS(posm[:], posm[:], -1.0, None, ALU.add)
                V.tensor_reduce(cnt[:, 6:7], cnt[:, 1:6], AX.X, ALU.add)
                dve.drain()
                TT(passes_f[:], passes_f[:], cnt[:, 6:7], ALU.add)
                dve.drain()
                V.tensor_copy(passes_i[:, bass.ds(l + 1, 1)], passes_f[:])
                dve.drain()
                dve.sem_inc(s["routed"], 1)
                dve.sem_inc(s["passes_known"], 1)

                most = dve.value_load(cnt_i[0:1, bass.ds(l, 1)], min_val=0, max_val=TOK)
                wait_apart(dve, s["x_scaled"], (l + 1) * TILES)
                with dve.Fori(0, PASSES) as rnd:
                    with dve.If(most > rnd * SLOTS):
                        with dve.Fori(0, PAIRS) as g:
                            n = dve.snap((before + rnd) * PAIRS + g)
                            first = dve.snap(base + MIX_UNITS + rnd * PASS_UNITS + g * PAIR_UNITS)
                            cols = bass.ds(g * 2, 2)
                            V.tensor_copy(pg[:], posm[:, :, cols])
                            V.tensor_copy(pc[:, 0], comb[:, :, cols])
                            dve.drain()
                            iota = table("slot").unsqueeze(1).to_broadcast([P, 2, SLOTS])
                            for t in range(TILES):
                                r = rows_of(t)
                                TT(Pm[0:r, t], iota[0:r], pg[0:r, t].unsqueeze(2).to_broadcast([r, 2, SLOTS]), ALU.is_equal)
                            dve.drain()
                            dve.sem_inc(s["p_built"], 1)
                            for i in range(3):
                                V.tensor_copy(cb3[:, :, :, i], pc[:, i % 2])
                                dve.drain()
                                if i < 2:
                                    TT(pc[:, (i + 1) % 2], pc[:, i % 2], cb3[:, :, :, i], ALU.subtract)
                                    dve.drain()
                            dve.sem_inc(s["cb_ready"], 1)
                            for k in range(4):
                                low(first, k)
                            dve.wait_ge(s["gs_ps"], n + 1)
                            V.tensor_reduce(gsl[:], ps[:, 6, 0:8].rearrange("p (e i) -> p e i", i=4)[:, :, 0:3], AX.X, ALU.add)
                            dve.drain()
                            dve.sem_inc(bank_free[6], 1)
                            for k in range(KC // 2):
                                dve.wait_ge(s["gath_high"], n * (KC // 2) + k + 1)
                                TT(XeT[:, 1, 2 * k:2 * k + 2, :].rearrange("p k c -> p (k c)"), ps[:, k, :],
                                   XeT[:, 0, 2 * k:2 * k + 2, :].rearrange("p k c -> p (k c)").bitcast(f32), ALU.subtract)
                                dve.drain()
                                dve.sem_inc(s["gath_low"], 1)
                                dve.sem_inc(bank_free[k], 1)

                            def gated(e):
                                dve.wait_ge(s["silu_done"], n * 2 + e + 1)
                                if e > 0:
                                    dve.wait_ge(s["ht_ps"], n * 2 + e)
                                STT(act_h[:], act_g[:], gsl[:, e:e + 1], ps[:, 2 * (e % 2) + 1, :], ALU.mult, ALU.mult)
                                dve.drain()
                                dve.sem_inc(s["h_done"], 1)
                                dve.sem_inc(bank_free[2 * (e % 2) + 1], 1)

                            def ht(e):
                                dve.wait_ge(s["ht_high"], n * 2 + e + 1)
                                TT(hT[:, 1].rearrange("p q c -> p (q c)"), ps[:, 4, :], hT[:, 0].rearrange("p q c -> p (q c)").bitcast(f32),
                                   ALU.subtract)
                                dve.drain()
                                dve.sem_inc(s["ht_low"], 1)
                                dve.sem_inc(bank_free[4], 1)

                            def out(e, half):
                                dve.wait_ge(s["ye_high"], n * 4 + 2 * e + half + 1)
                                hs = slice(half * 512, half * 512 + 512)
                                TT(ye[:, e % 2, 1, hs], ps[:, 5 + half, :], ye[:, e % 2, 0, hs].bitcast(f32), ALU.subtract)
                                dve.drain()
                                dve.sem_inc(s["ye_low"], 1)
                                dve.sem_inc(bank_free[5 + half], 1)

                            def gather_back():
                                for i in range(2 * TILES):
                                    t, hs = i // 2, slice((i % 2) * 512, (i % 2) * 512 + 512)
                                    r = rows_of(t)
                                    b = (7, 0, 1)[i % 3]
                                    dve.wait_ge(s["scat_ps"], n * 2 * TILES + i + 1)
                                    TT(x[0:r, t, hs], ps[0:r, b, :], x[0:r, t, hs], ALU.add)
                                    dve.drain()
                                    dve.sem_inc(bank_free[b], 1)
                            k = 4

                            def after(units):
                                nonlocal k
                                for _ in range(units):
                                    if k < PAIR_UNITS:
                                        low(first, k)
                                        k += 1
                            after(8)
                            gated(0)
                            after(8)
                            gated(1)
                            ht(0)
                            after(2)
                            out(0, 0)
                            after(2)
                            out(0, 1)
                            ht(1)
                            out(1, 0)
                            out(1, 1)
                            gather_back()
                        TS(posm[:], posm[:], -float(SLOTS), None, ALU.add)
                        dve.drain()
                norm_stats(2)
                dve.wait_ge(s["ln_loaded"], l * 64 + 64)
                for t in range(TILES):
                    dve.wait_ge(s["ln2_scaled"], l * TILES + t + 1)
                    gain(t, lngb2)
                    dve.sem_inc(s["x_tile_ready"], 1)


_IN = ["x_prompt", "x_sample", "state_rglru_h", "state_conv", "state_hgrn", "state_ret", "w_in", "conv_w", "conv_b",
       "w_rgate", "b_rgate", "w_igate", "b_igate", "rglru_lambda", "hgrn_lb_logits", "hgrn_norm_g", "w_out", "ln1_g",
       "ln1_b", "router_w", "router_b", "exp_w_gate", "exp_w_up", "exp_w_down", "ln2_g", "ln2_b"]
_OUT = [("y_prompt", (1, SEQ, D_MODEL)), ("y_sample", (DEC_BATCH, 1, D_MODEL)),
        ("h_prompt", (DEPTH, 1, D_A)), ("h_sample", (DEPTH, DEC_BATCH, D_A)),
        ("conv_prompt", (DEPTH, 1, CONV_W - 1, D_A)), ("conv_sample", (DEPTH, DEC_BATCH, CONV_W - 1, D_A)),
        ("hgrn_prompt", (DEPTH, 1, 4, DK_B, DK_B)), ("hgrn_sample", (DEPTH, DEC_BATCH, 4, DK_B, DK_B)),
        ("ret_prompt", (DEPTH, 1, C_HEADS, DK_C, DK_C)), ("ret_sample", (DEPTH, DEC_BATCH, C_HEADS, DK_C, DK_C))]


def kernel(**inputs):
    import concourse.bacc as bacc
    from concourse.bass_utils import run_bass_kernel_spmd
    nc = bacc.Bacc("TRN2", target_bir_lowering=False, num_devices=1)
    tables, levels, layer_flag = shape_tables()
    arrays = {n: np.ascontiguousarray(inputs[n]) for n in _IN}
    arrays.update(tables=tables, levels=levels, layer_flag=layer_flag)
    aps = {n: nc.dram_tensor(f"in_{n}", a.shape, mybir.dt.from_np(a.dtype), kind="ExternalInput").ap() for n, a in arrays.items()}
    outs = [nc.dram_tensor(f"out_{n}", shape, mybir.dt.float32, kind="ExternalOutput").ap() for n, shape in _OUT]
    build_program(nc, aps, outs)
    r = run_bass_kernel_spmd(nc, [{f"in_{n}": a for n, a in arrays.items()}], core_ids=[0])
    return tuple(r.results[0][f"out_{n}"] for n, _ in _OUT)
```

```python
import numpy as np
import concourse.bass as bass
from concourse import mybir
from contextlib import ExitStack

D_MODEL, SEQ, DEPTH, DEC_BATCH, PAST_LEN = 1024, 512, 2, 8, 4096
P = 128
TOK = SEQ + DEC_BATCH
TILES = SEQ // P + 1
KC = D_MODEL // P
HALF = TOK // 2
D_A = D_B = 256
D_C = 512
CONV_W = 4
RGLRU_C = 8.0
DK_B, CHUNK_B = 64, 64
CHUNKS_B = SEQ // CHUNK_B
LEVELS = [32, 16, 8, 4, 2, 1]
C_HEADS, DK_C = 4, 128
N_EXPERTS, D_EXPERT = 16, 512
PAIRS = N_EXPERTS // 2
SLOTS = 128
PASSES = -(-TOK // SLOTS)
LN_EPS, RMS_EPS, GN_EPS, F_TINY = 1e-5, 1e-6, 1e-6, 1e-30
ALPHA = (2 * DEPTH) ** 0.25
COLS = dict(xa=0, ga=256, qb=512, fb=768, vb=1024, gb=1280, qc=1536, kc=2048, vc=2560, gc=3072)
F_SPLIT = 2.0 ** -60

UNIT = 1024
RAW_SLOTS, SPLIT_SLOTS = 6, 4
EXPERT_SPLIT_SLOTS = 6
IN_PARTS = ["xa", "ga", "fb", "qb", "vb", "gb",
            "kc0", "qc0", "vc0", "gc0", "kc1", "qc1", "vc1", "gc1"]
SINE_AFTER = [2 * IN_PARTS.index(n) + 1 for n in ("vc0", "vc0", "qc1", "vc1")]
MIX_UNITS = 2 * len(IN_PARTS) + 8
EXPERT_UNITS = 12
PAIR_UNITS = 2 * EXPERT_UNITS
PASS_UNITS = PAIRS * PAIR_UNITS
QUAD_TURNS = 30
PAIR_BANK_USES = [2, 2, 2, 2, 5, 6, 5, 3]

SCATTER_BANKS = (7, 5, 6, 4)

PAIR_LOWS = "VVVVVG" * 4
MIX_LOWS = "G" * 30 + PAIR_LOWS[-RAW_SLOTS:]
LOW_CREDITS = {who: PAIR_LOWS[-RAW_SLOTS:].count(who) for who in "VG"}

ORDER = (("gu", 0), ("gu", 1), ("d", 0), ("d", 1))
GATE_DONE, UP_DONE, DOWN_FROM = [4, 12], [8, 16], [16, 20]

TABLE_COLS = [("ident", P), ("cos", TOK), ("sin", TOK), ("reset", SEQ), ("dret", C_HEADS * P),
              ("qdec", C_HEADS * P), ("kdec", C_HEADS), ("mean128", P), ("mean64", P), ("blockdiag", P),
              ("before", P), ("slot", P), ("key4", 4), ("key16", 16), ("seqdelta", DEC_BATCH)]
TABLE_AT, _n = {}, 0
for _name, _w in TABLE_COLS:
    TABLE_AT[_name] = (_n, _w)
    _n += _w
TABLE_W = _n


def shape_tables():
    f = np.float32
    t = {}
    i = np.arange(P)
    t["ident"] = np.eye(P)
    half = DK_C // 2
    inv = f(10000.0) ** (-np.arange(half, dtype=f) / f(half))
    pos = np.concatenate([np.arange(SEQ), np.full(DEC_BATCH, PAST_LEN)]).astype(f)
    ang = inv[:, None] * pos[None]
    t["cos"] = np.concatenate([np.cos(ang), np.cos(ang)])
    t["sin"] = np.concatenate([-np.sin(ang), np.sin(ang)])
    t["reset"] = np.broadcast_to((np.arange(SEQ) % CHUNK_B != 0), (P, SEQ))
    lg = np.log1p(-np.exp2(-5.0 - np.arange(C_HEADS, dtype=f))).astype(f)
    rel = (i[None, :] - i[:, None]).astype(f)
    scale = f(DK_C ** -0.5)
    t["dret"] = np.concatenate([np.where(rel >= 0, np.exp(np.where(rel >= 0, rel, 0) * g), 0) * scale for g in lg], 1)
    t["qdec"] = np.concatenate([np.broadcast_to(np.exp((i + 1).astype(f) * g), (P, P)) for g in lg], 1)
    t["kdec"] = np.stack([np.exp((P - 1.0 - i).astype(f) * g) * scale for g in lg], 1)
    t["mean128"] = np.full((P, P), 1 / 128)
    t["mean64"] = (i[:, None] // 64 == i[None] // 64) / 64
    t["blockdiag"] = (i[:, None] // 64 == i[None] // 64)
    t["before"] = (i[:, None] < i[None])
    t["slot"] = np.broadcast_to(i, (P, P))
    t["key4"] = np.broadcast_to(4 - np.arange(4), (P, 4))
    t["key16"] = np.broadcast_to(16 - np.arange(16), (P, 16))
    t["seqdelta"] = np.pad(np.eye(DEC_BATCH), ((0, P - DEC_BATCH), (0, 0)))
    levels = np.stack([(i[:, None] // (2 * m) == i[None] // (2 * m)) & (i[:, None] // m % 2 == 0) & (i[None] // m % 2 == 1)
                       for m in LEVELS], 1)
    layer_flag = np.broadcast_to((np.arange(DEPTH) > 0).astype(f)[:, None, None], (DEPTH, P, 1))
    return (np.concatenate([np.asarray(t[n], f) for n, _ in TABLE_COLS], 1),
            levels.astype(f).reshape(P, -1), np.ascontiguousarray(layer_flag))


GAMMA = [float(np.exp(np.log1p(-np.exp2(np.float32(-5.0 - h))))) for h in range(C_HEADS)]
GAMMA_CHUNK = [float(np.exp(np.float32(P) * np.log1p(-np.exp2(np.float32(-5.0 - h))))) for h in range(C_HEADS)]


def lows_count(lows, who, k):
    return lows[:k + 1].count(who) if k >= 0 else -PAIR_LOWS[len(PAIR_LOWS) + k + 1:].count(who)


def lows_base(who, layers, pairs):
    return layers * MIX_LOWS.count(who) + pairs * PAIR_LOWS.count(who) + LOW_CREDITS[who]


def rows_of(t):
    return P if t < TILES - 1 else DEC_BATCH


def build_program(nc, A, O):
    f32, f32r, bf16, i32 = mybir.dt.float32, mybir.dt.float32r, mybir.dt.bfloat16, mybir.dt.int32
    u8 = mybir.dt.uint8
    ALU, ACT, AX = mybir.AluOpType, mybir.ActivationFunctionType, mybir.AxisListType
    (o_yp, o_ys, o_hp, o_hs, o_cp, o_cs, o_gp, o_gs, o_rp, o_rs) = O
    ctx = ExitStack()
    with ctx:
        def sb(name, shape, dt=f32):
            return ctx.enter_context(nc.sbuf_tensor(name, shape, dt))

        def sem(name):
            return ctx.enter_context(nc.semaphore(name))

        x = sb("x", [P, TILES, D_MODEL])
        raw = sb("raw", [P, RAW_SLOTS, UNIT])
        ws = sb("ws", [P, SPLIT_SLOTS, 2, UNIT], f32r)
        tab = sb("tab", [P, TABLE_W])
        lev = sb("lev", [P, len(LEVELS) * P], u8)
        before_bf = sb("before_bf", [P, P], bf16)
        ones_bf = sb("ones_bf", [P, P], bf16)
        ident_bf = sb("ident_bf", [P, P], bf16)
        eps = sb("eps", [P, 3])
        convw = sb("convw", [P, 2, CONV_W])
        convb = sb("convb", [P, 2])
        gbias = sb("gbias", [P, 2, 2])
        gw = sb("gw", [P, 2, 2, P])
        lam = sb("lam", [P, 2])
        c8 = sb("c8", [P, 2])
        lamt = sb("lamt", [P, 3, 2])
        lbl = sb("lbl", [P, DEPTH, 2])
        lbt = sb("lbt", [P, 5, 2])
        flag = sb("flag", [P, 1])
        lb = sb("lb", [P, 2])
        oml = sb("oml", [P, 2])
        ng = sb("ng", [P, 1])
        h0 = sb("h0", [P, 2, DEC_BATCH])
        rw = sb("rw", [P, KC, N_EXPERTS])
        rb = sb("rb", [N_EXPERTS, 1])
        stats = sb("stats", [P, TILES, 24])
        mv = sb("mv", [P, TILES, 2])
        lnrs = sb("lnrs", [P, TILES, 2])
        outst = sb("outst", [P, 2, 20])
        csst = sb("csst", [P, 2, 3, DEC_BATCH])
        lg = sb("lg", [P, TILES, N_EXPERTS])
        rt = sb("rt", [P, 6, TILES, N_EXPERTS])
        rg = sb("rg", [P, 8, TILES, 4])
        posm = sb("posm", [P, TILES, N_EXPERTS])
        comb = sb("comb", [P, TILES, N_EXPERTS])
        mask_bf = sb("mask_bf", [P, TILES, N_EXPERTS], bf16)
        cnt = sb("cnt", [P, 8])
        cnt_i = sb("cnt_i", [P, DEPTH], i32)
        passes_f = sb("passes_f", [P, 1])
        passes_i = sb("passes_i", [P, DEPTH + 1], i32)
        pg = sb("pg", [P, TILES, 2])
        pc = sb("pc", [P, 2, TILES, 2])
        cb3 = sb("cb3", [P, TILES, 2, 3], bf16)
        gsl = sb("gsl", [P, 2])
        bl = sb("bl", [P, 2, CHUNKS_B])

        def table(name, rows=P):
            a, w = TABLE_AT[name]
            return tab[0:rows, a:a + w]
        ident = table("ident")

        mixer = ExitStack()
        xsT = mixer.enter_context(nc.sbuf_tensor("xsT", [P, 2, KC, TOK], f32r))
        Z = mixer.enter_context(nc.sbuf_tensor("mixer", [P, 15216], f32))
        y32 = mixer.enter_context(nc.sbuf_tensor("y32", [P, KC, TOK], f32))
        mixer.close()
        xsM = sb("xsM", [P, 2, TILES, D_MODEL], f32r)
        with nc.sbuf_tensor("lngb2", [P, 2, D_MODEL], f32) as lngb2:
            pass
        XeT = sb("XeT", [P, 2, KC, 2 * SLOTS], f32r)
        Pm = sb("Pm", [P, TILES, 2, SLOTS], f32r)
        PT = sb("PT", [SLOTS, 2, TOK], f32r)
        ye = sb("ye", [SLOTS, 2, 2, D_MODEL], f32r)
        hT = sb("hT", [P, 2, 4, SLOTS], f32r)
        Pbf = sb("Pbf", [P, TILES, 2, SLOTS], bf16)
        act_g = sb("act_g", [SLOTS, D_EXPERT])
        act_h = sb("act_h", [SLOTS, D_EXPERT])
        ws_more = sb("ws_more", [P, EXPERT_SPLIT_SLOTS - SPLIT_SLOTS, 2, UNIT], f32r)

        def split_slot(k, part, experts):
            if not experts:
                return ws[:, k % SPLIT_SLOTS, part]
            k = k % EXPERT_SPLIT_SLOTS
            return ws[:, k, part] if k < SPLIT_SLOTS else ws_more[:, k - SPLIT_SLOTS, part]
        x1T = Z[:, 4000:4000 + KC * TOK].rearrange("p (k t) -> p k t", k=KC)
        lgT = Z[0:N_EXPERTS, 8160:8160 + TOK]
        lngb1 = Z[:, 8680:8680 + 2 * D_MODEL].rearrange("p (n d) -> p n d", n=2)
        ysT = xsT

        def z(off, *dims):
            n = int(np.prod(dims))
            v = Z[:, off:off + n]
            if len(dims) == 1:
                return v
            names = "abcde"[:len(dims)]
            kw = {c: d for c, d in zip(names[1:], dims[1:])}
            return v.rearrange(f"p ({' '.join(names)}) -> p {' '.join(names)}", **kw)
        b_f, b_k, b_q = z(0, 2, TOK), z(1040, 2, TOK), z(2080, 2, TOK)
        b_v, b_g = z(3120, TILES, D_B), z(4400, 2, TOK)
        W0 = 5440
        b_t1, b_t2, b_b = z(W0, 2, TOK), z(W0 + 1040, 2, TOK), z(W0 + 2080, 2, TOK)
        lev_e = [b_t1, y32[:, 4:6, :]]
        lev_qk = [b_t2, y32[:, 6:8, :]]
        kept = [y32[:, 4:6, :], y32[:, 6:8, :]]
        b_acc = z(W0 + 3120, 2, 4, 2, P)
        b_S = z(W0 + 5168, CHUNKS_B + 1, 2, P)
        b_Vx = Z[0:DEC_BATCH, W0 + 5168:W0 + 5168 + 2048].rearrange("p (h n v) -> p h n v", h=4, n=DEC_BATCH)
        b_kT = z(W0 + 7472, 4, D_B)
        b_S0 = z(W0 + 8496, 2, DEC_BATCH, DK_B)
        a_x = z(W0, 2, SEQ + 3)
        a_xs = z(W0 + 1032, 2, CONV_W, DEC_BATCH)
        a_u, a_r, a_i = z(W0 + 1096, 2, TOK), z(W0 + 2136, 2, TOK), z(W0 + 3176, 2, TOK)
        a_a, a_t, a_g = z(W0 + 4216, 2, TOK), z(W0 + 5256, 2, TOK), z(W0 + 6296, 2, TOK)
        c_k, c_q, c_t1, c_sw = z(0, 2, TOK), z(1040, 2, TOK), z(2080, 2, TOK), z(3120, 2, TOK)
        c_swapped = [c_sw, c_t1]
        c_v, c_g = z(4160, TILES, 256), z(5440, 2, TOK)
        c_sc, c_qd, c_kT = z(6480, 4, 2, P), z(7504, 2, 4, P), z(8528, 4, 2, P)
        c_S = z(9552, 5, 2, P)
        c_S0 = z(10832, 2, DEC_BATCH, P)
        c_Vx = Z[0:DEC_BATCH, 12880:12880 + 2048].rearrange("p (h n v) -> p h n v", h=2, n=DEC_BATCH)
        ksT = Z[0:DEC_BATCH, 14960:15216]
        outst_t = Z[0:20, W0 + 7472:W0 + 7472 + D_A]

        ps = ctx.enter_context(nc.psum_tensor("ps", [P, 8, 512], f32))

        SEMS = """waits_apart ident_loaded kept_sb x_loaded tables_loaded tables_ready params_loaded gw_zero params_ready small_in small_exp prob_exp lg_shifted last_counts x_tile_ready
          passes_known w_high v_split g_split w_used
          xT_ps xT_high xT_low
          xa_sb u_ready gates_ps r_gate i_gate tanh_a ratio_ready sqrt_a h_ready ga_ready states_ps states_sb states_t
          f_sig k_sig q_silu v_b g_b k_ready clamped log_ab b_ready arg_ready e_ready qk_ready lev_ps lev_done
          eb_ready p_ready tr_ps kT_sb ks_sb vx_ready kv_ps s_new ds_ps s_ready o_ps o_sb sq_sb ms_ps ms_sqrt y_b y_a
          hg_out hg_in
          rot_swapped rot_sin rot_k rot_q v_c g_c sc_ps sc_ready qd_ready ctr_ps ckT_sb cks_sb cvx_ready ckv_ps cs_new
          cds_ps cs_ready co_ps co_sb cmean_ps cd_ready csq_sb cvar_ps cvar_sqrt y_c cs_out cs_in
          y_high y_low mix_done mv_ready std_ready lnrs_ready ln_scaled ln_loaded ln1_done x1T_ps x1T_sb lgT_ps lgT_sb
          lg_ps mask_ready pos_ps posm_ready routed xm_high xm_low x_scaled
          p_built cb_ready p_bf pt_ps pt_sb gs_ps gs_sb gath_ps gath_high gath_low silu_done h_done ht_ps ht_high ht_low
          ye_high ye_low scat_ps scat_done ln2_scaled out_done""".split()
        s = {}
        for n in SEMS:
            s[n] = sem(n)
        raw_loaded = [sem(f"raw_loaded{i}") for i in range(RAW_SLOTS)]
        quad_free = [sem(f"quad_free{i}") for i in range(2)]
        bank_free = [sem(f"bank_free{i}") for i in range(8)]

        w_in_v = A["w_in"].rearrange("l (k p) c -> l p k c", p=P)
        w_out_v = A["w_out"].rearrange("l (k p) c -> l p k c", p=P)
        wg_v = A["exp_w_gate"].rearrange("l e (k p) f -> l e p k f", p=P)
        wu_v = A["exp_w_up"].rearrange("l e (k p) f -> l e p k f", p=P)
        wd_v = A["exp_w_down"].rearrange("l e (k p) d -> l e p k d", p=P)

        def wait_apart(engine, semaphore, count):
            engine.wait_ge(semaphore, count)
            engine.sem_inc(s["waits_apart"], 1)

        split = {"V": s["v_split"], "G": s["g_split"]}

        def wait_split(engine, layers, pairs, lows, k):
            who = lows[k]
            engine.wait_ge(split[who], lows_base(who, layers, pairs) + lows_count(lows, who, k))

        def part_col(name):
            return COLS[name.rstrip("01")] + (256 if name.endswith("1") else 0)

        block = ctx.enter_context(nc.Block())

        @block.sync
        def _(sp):
            def load(layers, pairs, lows, k, src):
                slot = k % RAW_SLOTS
                wait_split(sp, layers, pairs, lows, k - RAW_SLOTS)
                dst = raw[:, slot, :].rearrange("p (k c) -> p k c", k=src.shape[1])
                sp.dma_start(dst, src).then_inc(raw_loaded[slot], 16)

            sp.wait_ge(s["gw_zero"], 1)

            def parameters(l):
                for c in range(2):
                    cs = slice(c * P, (c + 1) * P)
                    sp.dma_start(convw[:, c, :], A["conv_w"][l, :, cs].rearrange("j p -> p j"),
                                  allow_slow_non_contiguous=True).then_inc(s["params_loaded"], 16)
                    sp.dma_start(convb[:, c:c + 1], A["conv_b"][l, cs].rearrange("(p o) -> p o", o=1)).then_inc(s["params_loaded"], 16)
                    sp.dma_start(lam[:, c:c + 1], A["rglru_lambda"][l, cs].rearrange("(p o) -> p o", o=1)).then_inc(s["params_loaded"], 16)
                    for d in range(DEPTH):
                        sp.dma_start(lbl[:, d, c:c + 1], A["hgrn_lb_logits"][d, cs].rearrange("(p o) -> p o", o=1)).then_inc(s["params_loaded"], 16)
                    sp.dma_start(h0[:, c, :], A["state_rglru_h"][l, :, cs].rearrange("n p -> p n"),
                                  allow_slow_non_contiguous=True).then_inc(s["params_loaded"], 16)
                    for jj in range(CONV_W - 1):
                        sp.dma_start(csst[:, c, jj, :], A["state_conv"][l, :, jj, cs].rearrange("n p -> p n"),
                                      allow_slow_non_contiguous=True).then_inc(s["params_loaded"], 16)
                for gate, (w, bb) in enumerate((("w_rgate", "b_rgate"), ("w_igate", "b_igate"))):
                    for g4 in range(4):
                        pr, c = slice(64 * (g4 % 2), 64 * (g4 % 2) + 64), g4 // 2
                        sp.dma_start(gw[pr, gate, c, pr], A[w][l, g4, :, :]).then_inc(s["params_loaded"], 16)
                        sp.dma_start(gbias[pr, gate, c:c + 1], A[bb][l, g4, :].rearrange("(p o) -> p o", o=1)).then_inc(s["params_loaded"], 16)
                for hh in range(2):
                    sp.dma_start(ng[64 * hh:64 * hh + 64, :], A["hgrn_norm_g"][l, :].rearrange("(p o) -> p o", o=1)).then_inc(s["params_loaded"], 16)
                sp.dma_start(flag[:], A["layer_flag"][l]).then_inc(s["params_loaded"], 16)

            with sp.Fori(0, DEPTH) as l:
                sp.wait_ge(s["passes_known"], l + 1)
                before = sp.value_load(passes_i[0:1, bass.ds(l, 1)], min_val=0, max_val=DEPTH * PASSES)
                pairs = sp.snap(before * PAIRS)
                k = 0
                for part in IN_PARTS:
                    c = part_col(part)
                    if k == RAW_SLOTS:
                        parameters(l)
                    for half in range(2):
                        load(l, pairs, MIX_LOWS, k, w_in_v[l, :, 4 * half:4 * half + 4, c:c + 256])
                        k += 1
                for c in range(4):
                    for half in range(2):
                        load(l, pairs, MIX_LOWS, k, w_out_v[l, :, 4 * half:4 * half + 4, c * 256:c * 256 + 256])
                        k += 1

                def experts(done):
                    with sp.Fori(0, PAIRS) as g:
                        n = sp.snap((before + done) * PAIRS + g)
                        j = 0
                        for kind, e in ORDER:
                            ex = g * 2 + e
                            if kind == "gu":
                                for v in (wg_v, wu_v):
                                    for q in range(4):
                                        load(l + 1, n, PAIR_LOWS, j, v[l, ex, :, 2 * q:2 * q + 2, :])
                                        j += 1
                            else:
                                for half in range(2):
                                    for q in range(2):
                                        load(l + 1, n, PAIR_LOWS, j, wd_v[l, ex, :, 2 * q:2 * q + 2, half * 512:half * 512 + 512])
                                        j += 1
                experts(0)
                wait_apart(sp, s["routed"], l + 1)
                most = sp.value_load(cnt_i[0:1, bass.ds(l, 1)], min_val=0, max_val=TOK)
                with sp.Fori(1, PASSES) as r:
                    with sp.If(most > r * SLOTS):
                        experts(r)

        @block.gpsimd
        def _(pool):
            def parts(u, uses, lows, k):
                slot, experts = k % RAW_SLOTS, lows is PAIR_LOWS
                dst = [split_slot(k, part, experts) for part in range(2)]
                pool.wait_ge(raw_loaded[slot], (uses + k // RAW_SLOTS + 1) * 16)
                wait_apart(pool, s["w_used"], u + k + 1 - (EXPERT_SPLIT_SLOTS - SPLIT_SLOTS if experts else 0))
                nc.gpsimd.tensor_scalar(dst[0], raw[:, slot, :], 1.0, 0.0, ALU.mult, ALU.add).then_inc(s["w_high"], 1)
                if lows[k] == "G":
                    pool.drain()
                    nc.gpsimd.tensor_tensor(dst[1], raw[:, slot, :], dst[0].bitcast(f32),
                                            ALU.subtract).then_inc(s["g_split"], 1)

            nc.gpsimd.memset(gw[:], 0.0).then_inc(s["gw_zero"], 1)
            with pool.Fori(0, DEPTH) as l:
                pool.wait_ge(s["passes_known"], l + 1)
                before = pool.value_load(passes_i[0:1, bass.ds(l, 1)], min_val=0, max_val=DEPTH * PASSES)
                base = pool.snap(l * MIX_UNITS + before * PASS_UNITS)
                uses = pool.snap(l * (MIX_UNITS // RAW_SLOTS) + before * (PASS_UNITS // RAW_SLOTS))
                rot = 0
                for k in range(MIX_UNITS):
                    parts(base, uses, MIX_LOWS, k)
                    for _ in range(SINE_AFTER.count(k)):
                        pool.wait_ge(s["rot_swapped"], l * 4 + rot + 1)
                        sinb = table("sin").unsqueeze(1).to_broadcast([P, 2, TOK])
                        nc.gpsimd.tensor_tensor(c_swapped[rot % 2], c_swapped[rot % 2], sinb, ALU.mult).then_inc(s["rot_sin"], 1)
                        rot += 1
                pool.wait_ge(s["routed"], l + 1)
                most = pool.value_load(cnt_i[0:1, bass.ds(l, 1)], min_val=0, max_val=TOK)
                with pool.Fori(0, PASSES) as r:
                    with pool.If(most > r * SLOTS):
                        def to_bf16(n):
                            wait_apart(pool, s["p_built"], n + 1)
                            for rows, t0, t1 in ((P, 0, 4), (DEC_BATCH, 4, 5)):
                                op = nc.gpsimd.tensor_scalar(Pbf[0:rows, t0:t1].rearrange("p t e c -> p (t e c)"),
                                                             Pm[0:rows, t0:t1].rearrange("p t e c -> p (t e c)").bitcast(f32),
                                                             1.0, 0.0, ALU.mult, ALU.add)
                            op.then_inc(s["p_bf"], 1)

                        def experts(g, last):
                            n = pool.snap((before + r) * PAIRS + g)
                            first = pool.snap(base + MIX_UNITS + r * PASS_UNITS + g * PAIR_UNITS)
                            done = pool.snap(uses + MIX_UNITS // RAW_SLOTS + (r * PAIRS + g) * (PAIR_UNITS // RAW_SLOTS))
                            for k in range(PAIR_UNITS):
                                parts(first, done, PAIR_LOWS, k)
                                if k == UP_DONE[1] + 1 and not last:
                                    pool.wait_ge(s["gs_ps"], n + 1)
                                    to_bf16(n + 1)
                        to_bf16(pool.snap((before + r) * PAIRS))
                        wait_apart(pool, s["w_used"], base + MIX_UNITS + r * PASS_UNITS + SPLIT_SLOTS)
                        with pool.Fori(0, PAIRS - 1) as g:
                            experts(g, False)
                        experts(PAIRS - 1, True)

        SPLIT3 = ((0, 0), (0, 1), (1, 0))

        @block.tensor
        def _(pe):
            pe.wait_ge(s["ident_loaded"], 16)
            with pe.Fori(0, DEPTH) as l:
                pe.wait_ge(s["passes_known"], l + 1)
                before = pe.value_load(passes_i[0:1, bass.ds(l, 1)], min_val=0, max_val=DEPTH * PASSES)
                pairs = pe.snap(before * PAIRS)
                turns = [0]
                unit = [0]

                def turn(apart=False):
                    q = turns[0] % 2
                    pe.wait_ge(quad_free[q], l * QUAD_TURNS + turns[0] // 2 + 1)
                    if apart:
                        pe.sem_inc(s["waits_apart"], 1)
                    turns[0] += 1
                    return 4 * q

                for t in range(TILES):
                    r = rows_of(t)
                    b = turn()
                    wait_apart(pe, s["x_tile_ready"], l * TILES + t + 1)
                    for k in range(KC):
                        op = nc.tensor.transpose(ps[:, b + k // 4, (k % 4) * P:(k % 4) * P + r],
                                                 x[0:r, t, k * P:(k + 1) * P], ident[0:r, 0:r])
                    op.then_inc(s["xT_ps"], 1)

                def project(token_major):
                    b = turn()
                    for half in range(2):
                        k0 = unit[0]
                        wait_split(pe, l, pairs, MIX_LOWS, k0)
                        w = [split_slot(k0, part, False).rearrange("p (k c) -> p k c", k=4) for part in range(2)]
                        if not token_major:
                            for c in range(2):
                                for th in range(2):
                                    for k in range(4):
                                        for n, (a, bb) in enumerate(SPLIT3):
                                            op = nc.tensor.matmul(ps[:, b + 2 * c + th, 0:HALF], w[a][:, k, c * P:(c + 1) * P],
                                                                  xsT[:, bb, 4 * half + k, th * HALF:(th + 1) * HALF],
                                                                  start=half + k + n == 0, stop=half == 1 and k == 3 and n == 2)
                        else:
                            for t in range(TILES):
                                r = rows_of(t)
                                for k in range(4):
                                    for n, (a, bb) in enumerate(SPLIT3):
                                        op = nc.tensor.matmul(ps[0:r, b + t % 4, 256 * (t // 4):256 * (t // 4) + 256],
                                                              xsT[:, bb, 4 * half + k, t * P:t * P + r], w[a][:, k, :],
                                                              start=half + k + n == 0 and t < 4,
                                                              stop=half == 1 and k == 3 and n == 2, skip_group_check=True)
                        op.then_inc(s["w_used"], 1)
                        unit[0] += 1

                pe.wait_ge(s["tables_ready"], 1)
                pe.wait_ge(s["xT_low"], (l + 1) * TILES)
                for part in ("xa", "ga", "fb", "qb"):
                    project(False)

                pe.wait_ge(s["u_ready"], l + 1)
                for gate in range(2):
                    b = turn()
                    if gate == 0:
                        pe.wait_ge(s["params_ready"], l + 1)
                    for c in range(2):
                        for th in range(2):
                            op = nc.tensor.matmul(ps[:, b + 2 * c + th, 0:HALF], gw[:, gate, c, :],
                                                  a_u[:, c, th * HALF:(th + 1) * HALF], start=True, stop=True)
                    op.then_inc(s["gates_ps"], 1)
                project(True)
                project(False)
                b = turn()
                pe.wait_ge(s["states_sb"], l + 1)
                for c in range(2):
                    op = nc.tensor.transpose(ps[0:20, b, c * P:(c + 1) * P], outst[:, c, :], ident)
                op.then_inc(s["states_ps"], 1)

                for n in range(len(LEVELS) + 1):
                    b = turn()
                    if n == 0:
                        pe.wait_ge(s["k_ready"], l + 1)
                        pe.wait_ge(s["q_silu"], l + 1)
                    else:
                        pe.wait_ge(s["qk_ready"], l * len(LEVELS) + n)
                    for t in range(4):
                        for h in range(4):
                            pr, c, sl = slice(64 * (h % 2), 64 * (h % 2) + 64), h // 2, slice(t * P, (t + 1) * P)
                            kk, qq = (b_k, b_q) if n == 0 else (lev_qk[(n - 1) % 2],) * 2
                            at = (t % 2) * 256 + c * P
                            op = nc.tensor.matmul(ps[:, b + 2 * (h % 2) + t // 2, at:at + P], kk[pr, c, sl], qq[pr, c, sl],
                                                  start=True, stop=True, skip_group_check=True)
                    op.then_inc(s["lev_ps"], 1)
                project(False)
                b = turn()
                pe.wait_ge(s["p_ready"], l + 1)
                for t in range(4):
                    for c in range(2):
                        nc.tensor.transpose(ps[:, b + t // 2, (t % 2) * 256 + c * P:(t % 2) * 256 + (c + 1) * P],
                                            b_k[:, c, t * P:(t + 1) * P], ident)
                for c in range(2):
                    op = nc.tensor.transpose(ps[0:DEC_BATCH, b + 2, c * P:(c + 1) * P], b_k[:, c, SEQ:TOK], ident)
                op.then_inc(s["tr_ps"], 1)
                b = turn()
                pe.wait_ge(s["ks_sb"], l + 1)
                pe.wait_ge(s["vx_ready"], l + 1)
                for h in range(4):
                    op = nc.tensor.matmul(ps[64 * (h % 2):64 * (h % 2) + 64, b + h // 2, :], ksT[:, h * 64:(h + 1) * 64],
                                          b_Vx[:, h].rearrange("p n v -> p (n v)"), start=True, stop=True,
                                          skip_group_check=True)
                op.then_inc(s["kv_ps"], 1)
                b = turn()
                pe.wait_ge(s["kT_sb"], l + 1)
                for ch in range(CHUNKS_B):
                    pr = slice(64 * (ch % 2), 64 * (ch % 2) + 64)
                    for c in range(2):
                        at = (ch // 2 % 2) * 256 + c * P
                        op = nc.tensor.matmul(ps[:, b + 2 * (ch % 2) + ch // 4, at:at + P],
                                              b_kT[pr, ch // 2, c * P:(c + 1) * P], b_v[pr, ch // 2, c * P:(c + 1) * P],
                                              start=True, stop=True, skip_group_check=True)
                op.then_inc(s["ds_ps"], 1)
                project(False)
                b = turn()
                pe.wait_ge(s["lev_done"], (l + 1) * (len(LEVELS) + 1))
                pe.wait_ge(s["s_ready"], l + 1)
                pe.wait_ge(s["s_new"], l + 1)
                for c in range(2):
                    for t in range(4):
                        for hh in range(2):
                            h = 2 * c + hh
                            nc.tensor.matmul(ps[64 * hh:64 * hh + 64, b + c, t * P:(t + 1) * P],
                                             b_v[:, t, h * 64:(h + 1) * 64], b_acc[:, hh, t, c, :],
                                             start=t == 0, stop=False, skip_group_check=True)
                        for ch in (2 * t, 2 * t + 1):
                            nc.tensor.matmul(ps[:, b + c, ch * 64:(ch + 1) * 64], b_S[:, ch, c, :],
                                             b_q[:, c, ch * 64:(ch + 1) * 64], start=False, stop=True, skip_group_check=True)
                for h in range(4):
                    pr, c = slice(64 * (h % 2), 64 * (h % 2) + 64), h // 2
                    for n in range(DEC_BATCH):
                        op = nc.tensor.matmul(ps[pr, b + 2, c * DEC_BATCH + n:c * DEC_BATCH + n + 1], b_S0[pr, c, n, :],
                                              b_q[pr, c, SEQ + n:SEQ + n + 1], start=True, stop=True, skip_group_check=True)
                op.then_inc(s["o_ps"], 1)
                b = turn()
                pe.wait_ge(s["sq_sb"], l + 1)
                for c in range(2):
                    for th in range(2):
                        op = nc.tensor.matmul(ps[:, b + 2 * c + th, 0:HALF], table("mean64"),
                                              b_t2[:, c, th * HALF:(th + 1) * HALF], start=True, stop=True)
                op.then_inc(s["ms_ps"], 1)

                for j in range(2):
                    n2 = l * 2 + j + 1
                    for part in ("kc", "qc", "vc", "gc") if j else ("vc", "gc"):
                        project(part == "vc")
                    b = turn()
                    pe.wait_ge(s["rot_k"], n2)
                    pe.wait_ge(s["rot_q"], n2)
                    for t in range(4):
                        for h in range(2):
                            op = nc.tensor.matmul(ps[:, b + t // 2, (t % 2) * 256 + h * P:(t % 2) * 256 + (h + 1) * P],
                                                  c_k[:, h, t * P:(t + 1) * P], c_q[:, h, t * P:(t + 1) * P],
                                                  start=True, stop=True, skip_group_check=True)
                    op.then_inc(s["sc_ps"], 1)
                    b = turn()
                    for t in range(4):
                        for h in range(2):
                            nc.tensor.transpose(ps[:, b + t // 2, (t % 2) * 256 + h * P:(t % 2) * 256 + (h + 1) * P],
                                                c_k[:, h, t * P:(t + 1) * P], ident)
                    for h in range(2):
                        op = nc.tensor.transpose(ps[0:DEC_BATCH, b + 2, h * P:(h + 1) * P], c_k[:, h, SEQ:TOK], ident)
                    op.then_inc(s["ctr_ps"], 1)
                    b = turn()
                    pe.wait_ge(s["cks_sb"], n2)
                    pe.wait_ge(s["cvx_ready"], n2)
                    for h in range(2):
                        for nh in range(2):
                            op = nc.tensor.matmul(ps[:, b + 2 * h + nh, :], ksT[:, h * P:(h + 1) * P],
                                                  c_Vx[:, h, 4 * nh:4 * nh + 4, :].rearrange("p n v -> p (n v)"),
                                                  start=True, stop=True)
                    op.then_inc(s["ckv_ps"], 1)
                    b = turn()
                    pe.wait_ge(s["ckT_sb"], n2)
                    pe.wait_ge(s["v_c"], n2)
                    for t in range(4):
                        for h in range(2):
                            op = nc.tensor.matmul(ps[:, b + t // 2, (t % 2) * 256 + h * P:(t % 2) * 256 + (h + 1) * P],
                                                  c_kT[:, t, h, :], c_v[:, t, h * P:(h + 1) * P],
                                                  start=True, stop=True, skip_group_check=True)
                    op.then_inc(s["cds_ps"], 1)
                    b = turn()
                    pe.wait_ge(s["sc_ready"], n2)
                    pe.wait_ge(s["qd_ready"], n2)
                    pe.wait_ge(s["cs_ready"], n2)
                    pe.wait_ge(s["cs_new"], n2)
                    for h in range(2):
                        for t in range(4):
                            nc.tensor.matmul(ps[:, b + h, t * P:(t + 1) * P], c_v[:, t, h * P:(h + 1) * P], c_sc[:, t, h, :],
                                             start=t == 0, stop=t == 0, skip_group_check=True)
                            if t:
                                nc.tensor.matmul(ps[:, b + h, t * P:(t + 1) * P], c_S[:, t, h, :], c_qd[:, h, t, :],
                                                 start=False, stop=True, skip_group_check=True)
                    for h in range(2):
                        for n in range(DEC_BATCH):
                            op = nc.tensor.matmul(ps[:, b + 2, h * DEC_BATCH + n:h * DEC_BATCH + n + 1], c_S0[:, h, n, :],
                                                  c_q[:, h, SEQ + n:SEQ + n + 1], start=True, stop=True, skip_group_check=True)
                    op.then_inc(s["co_ps"], 1)
                    for what, ready in (("cmean_ps", "co_sb"), ("cvar_ps", "csq_sb")):
                        b = turn()
                        pe.wait_ge(s[ready], n2)
                        src = c_t1 if what == "cmean_ps" else c_sw
                        for h in range(2):
                            for th in range(2):
                                op = nc.tensor.matmul(ps[:, b + 2 * h + th, 0:HALF], table("mean128"),
                                                      src[:, h, th * HALF:(th + 1) * HALF], start=True, stop=True)
                        op.then_inc(s[what], 1)

                for cc in range(4):
                    b = turn()
                    for half in range(2):
                        k0 = unit[0]
                        wait_split(pe, l, pairs, MIX_LOWS, k0)
                        if cc == 0:
                            pe.wait_ge(s["y_low"], l * 5 + (2, 5)[half])
                        w = [split_slot(k0, part, False).rearrange("p (k c) -> p k c", k=4) for part in range(2)]
                        for t in range(TILES):
                            r = rows_of(t)
                            for k in range(4):
                                for n, (a, bb) in enumerate(SPLIT3):
                                    op = nc.tensor.matmul(ps[0:r, b + t % 4, 256 * (t // 4):256 * (t // 4) + 256],
                                                          ysT[:, bb, 4 * half + k, t * P:t * P + r], w[a][:, k, :],
                                                          start=half + k + n == 0 and t < 4,
                                                          stop=half == 1 and k == 3 and n == 2, skip_group_check=True)
                        op.then_inc(s["w_used"], 1)
                        unit[0] += 1

                def logits(bank, th):
                    for k in range(KC):
                        op = nc.tensor.matmul(ps[0:N_EXPERTS, bank, 0:HALF], rw[:, k, :], x1T[:, k, th * HALF:(th + 1) * HALF],
                                              start=k == 0, stop=k == KC - 1)
                    op.then_inc(s["lgT_ps"], 1)

                for t in range(TILES):
                    r = rows_of(t)
                    pe.wait_ge(s["ln1_done"], l * TILES + t + 1)
                    b = turn(apart=True)
                    for k in range(KC):
                        op = nc.tensor.transpose(ps[:, b + k // 4, (k % 4) * P:(k % 4) * P + r],
                                                 x[0:r, t, k * P:(k + 1) * P], ident[0:r, 0:r])
                    op.then_inc(s["x1T_ps"], 1)
                    if t == 3:
                        pe.wait_ge(s["x1T_sb"], l * TILES + 3)
                        logits(4 - b + 2, 0)
                b = turn()
                pe.wait_ge(s["x1T_sb"], (l + 1) * TILES)
                logits(b, 1)
                pe.wait_ge(s["lgT_sb"], l + 1)
                b = turn(apart=True)
                for t in range(TILES):
                    r = rows_of(t)
                    op = nc.tensor.transpose(ps[0:r, b, t * N_EXPERTS:(t + 1) * N_EXPERTS], lgT[:, t * P:t * P + r],
                                             ident[0:N_EXPERTS, 0:N_EXPERTS])
                op.then_inc(s["lg_ps"], 1)
                b = turn()
                pe.wait_ge(s["mask_ready"], l + 1)
                for t in range(TILES + 1):
                    r = rows_of(t) if t < TILES else P
                    for tt in range(min(t, TILES - 1) + 1):
                        rr = rows_of(tt)
                        lhsT = before_bf if tt == t else ones_bf
                        op = nc.tensor.matmul(ps[0:r, b, t * N_EXPERTS:(t + 1) * N_EXPERTS], lhsT[0:rr, 0:r],
                                              mask_bf[0:rr, tt, :], start=tt == 0, stop=tt == min(t, TILES - 1),
                                              skip_group_check=True)
                op.then_inc(s["pos_ps"], 1)
                assert turns[0] == 2 * QUAD_TURNS, turns
                assert unit[0] == MIX_UNITS

                pe.wait_ge(s["routed"], l + 1)
                for q in range(2):
                    pe.wait_ge(quad_free[q], (l + 1) * QUAD_TURNS + 1)
                pe.wait_ge(s["xm_low"], (l + 1) * TILES)
                most = pe.value_load(cnt_i[0:1, bass.ds(l, 1)], min_val=0, max_val=TOK)
                with pe.Fori(0, PASSES) as rnd:
                    with pe.If(most > rnd * SLOTS):
                        def gather(n, ks, used):
                            if ks[0] == 0:
                                pe.wait_ge(s["p_built"], n + 1)
                            for k in ks:
                                if k % 2 == 0:
                                    pe.wait_ge(bank_free[k // 2], used[k // 2])
                                for t in range(TILES):
                                    r = rows_of(t)
                                    for a in range(2):
                                        op = nc.tensor.matmul(ps[:, k // 2, (k % 2) * 256:(k % 2) * 256 + 256],
                                                              xsM[0:r, a, t, k * P:(k + 1) * P],
                                                              Pm[0:r, t].rearrange("p e c -> p (e c)"),
                                                              start=t + a == 0, stop=t == TILES - 1 and a == 1,
                                                              skip_group_check=True)
                                if k % 2 == 1:
                                    op.then_inc(s["gath_ps"], 1)

                        def experts(g, last):
                            n = pe.snap((before + rnd) * PAIRS + g)
                            used = [1, 1, 1, 1, 0, 0, 0, 0]
                            j = [0]

                            def bank(i):
                                pe.wait_ge(bank_free[i], n * PAIR_BANK_USES[i] + used[i] + 1)
                                used[i] += 1
                                return i

                            def gate_up(e, m):
                                b = bank(2 * e + m)
                                if e == 0 and m == 0:
                                    pe.wait_ge(s["gath_low"], (n + 1) * (KC // 2))
                                for q in range(4):
                                    k0 = j[0]
                                    wait_split(pe, l + 1, n, PAIR_LOWS, k0)
                                    w = [split_slot(k0, part, True).rearrange("p (k c) -> p k c", k=2) for part in range(2)]
                                    for kk in range(2):
                                        for i3, (a, bb) in enumerate(SPLIT3):
                                            op = nc.tensor.matmul(ps[:, b, :], XeT[:, bb, 2 * q + kk, e * SLOTS:(e + 1) * SLOTS],
                                                                  w[a][:, kk, :], start=q + kk + i3 == 0,
                                                                  stop=q == 3 and kk == 1 and i3 == 2)
                                    op.then_inc(s["w_used"], 1)
                                    j[0] += 1

                            def slots():
                                pe.wait_ge(s["p_bf"], n + 1)
                                for e in range(2):
                                    b = bank(4 + e)
                                    pbt = ps[:, b, :].bitcast(bf16)
                                    for t in range(TILES):
                                        r = rows_of(t)
                                        op = nc.tensor.transpose(pbt[:, t * P:t * P + r], Pbf[0:r, t, e, :], ident_bf[0:r, 0:r])
                                    op.then_inc(s["pt_ps"], 1)
                                pe.wait_ge(s["cb_ready"], n + 1)
                                b = bank(6)
                                for e in range(2):
                                    for t in range(TILES):
                                        r = rows_of(t)
                                        op = nc.tensor.matmul(ps[:, b, 4 * e:4 * e + 3], Pbf[0:r, t, e, :], cb3[0:r, t, e, :],
                                                              start=t == 0, stop=t == TILES - 1, skip_group_check=True)
                                op.then_inc(s["gs_ps"], 1)

                            def turn_h(e):
                                b = bank(4)
                                pe.wait_ge(s["h_done"], n * 2 + e + 2)
                                for q in range(4):
                                    op = nc.tensor.transpose(ps[:, b, q * P:(q + 1) * P], act_h[:, q * P:(q + 1) * P], ident)
                                op.then_inc(s["ht_ps"], 1)

                            def down(e):
                                for half in range(2):
                                    b = bank(5 + half)
                                    for q in range(2):
                                        k0 = j[0]
                                        wait_split(pe, l + 1, n, PAIR_LOWS, k0)
                                        if half + q == 0:
                                            pe.wait_ge(s["ht_low"], n * 2 + e + 1)
                                        w = [split_slot(k0, part, True).rearrange("p (k c) -> p k c", k=2) for part in range(2)]
                                        for kk in range(2):
                                            for i3, (a, bb) in enumerate(SPLIT3):
                                                op = nc.tensor.matmul(ps[:, b, :], hT[:, bb, 2 * q + kk, :], w[a][:, kk, :],
                                                                      start=q + kk + i3 == 0, stop=q == 1 and kk == 1 and i3 == 2)
                                        op.then_inc(s["w_used"], 1)
                                        j[0] += 1

                            def gather_next(ks):
                                if not last:
                                    gather(n + 1, ks, {k // 2: n * PAIR_BANK_USES[k // 2] + used[k // 2] + 1 for k in ks})
                                    for k in ks[::2]:
                                        used[k // 2] += 1

                            def scatter():
                                pe.wait_ge(s["pt_sb"], (n + 1) * 2)
                                pe.wait_ge(s["ye_low"], (n + 1) * 4)
                                for i in range(2 * TILES):
                                    t, half = i // 2, i % 2
                                    r = rows_of(t)
                                    b = bank(SCATTER_BANKS[i % 4])
                                    for e2 in range(2):
                                        for a in range(2):
                                            op = nc.tensor.matmul(ps[0:r, b, :], PT[:, e2, t * P:t * P + r],
                                                                  ye[:, e2, a, half * 512:half * 512 + 512],
                                                                  start=e2 + a == 0, stop=e2 == 1 and a == 1)
                                    op.then_inc(s["scat_ps"], 1)

                            gate_up(0, 0)
                            gate_up(0, 1)
                            slots()
                            gate_up(1, 0)
                            turn_h(0)
                            gate_up(1, 1)
                            down(0)
                            turn_h(1)
                            gather_next([0, 1, 2, 3])
                            down(1)
                            gather_next([4, 5, 6, 7])
                            scatter()
                            assert used == [u + (i < 4) * (not last) for i, u in enumerate(PAIR_BANK_USES)], used
                            assert j[0] == PAIR_UNITS
                        n0 = pe.snap((before + rnd) * PAIRS)
                        gather(n0, list(range(KC)), {b: n0 * PAIR_BANK_USES[b] + 1 for b in range(4)})
                        with pe.Fori(0, PAIRS - 1) as g:
                            experts(g, False)
                        experts(PAIRS - 1, True)

        @block.scalar
        def _(act):
            def quad(q):
                return ps[:, 4 * q:4 * q + 4, 0:HALF]
            act.dma_start(ident, A["tables"][:, 0:P]).then_inc(s["ident_loaded"], 16)
            for t in range(4):
                act.dma_start(x[:, t, :], A["x_prompt"][0, t * P:(t + 1) * P, :]).then_inc(s["x_loaded"], 16)
            act.dma_start(x[0:DEC_BATCH, 4, :], A["x_sample"].rearrange("b o d -> (b o) d")).then_inc(s["x_loaded"], 16)
            act.dma_start(tab[:, P:TABLE_W], A["tables"][:, P:TABLE_W]).then_inc(s["tables_loaded"], 16)
            act.dma_start(Z[:, 0:len(LEVELS) * P], A["levels"]).then_inc(s["tables_loaded"], 16)
            act.dma_start(rw[:], A["router_w"].rearrange("(k p) e -> p k e", p=P)).then_inc(s["tables_loaded"], 16)
            act.dma_start(rb[:], A["router_b"].rearrange("(e o) -> e o", o=1)).then_inc(s["tables_loaded"], 16)
            with act.Fori(0, DEPTH) as l:
                turns = [0]

                def turn():
                    turns[0] += 1
                    return 4 * ((turns[0] - 1) % 2)
                act.wait_ge(s["passes_known"], l + 1)
                before = act.value_load(passes_i[0:1, bass.ds(l, 1)], min_val=0, max_val=DEPTH * PASSES)
                base = act.snap(l * MIX_UNITS + before * PASS_UNITS)
                act.dma_start(o_cs[l, :, 0:2, :], A["state_conv"][l, :, 1:3, :]).then_inc(s["out_done"], 16)

                for t in range(TILES):
                    r = rows_of(t)
                    b = turn()
                    act.wait_ge(s["xT_ps"], l * TILES + t + 1)
                    src = ps[:, b:b + 2, :].rearrange("p b (k c) -> p (b k) c", c=P)[:, :, 0:r]
                    nc.scalar.activation(xsT[:, 0, :, t * P:t * P + r], src, ACT.Copy).then_inc(s["xT_high"], 1)
                act.wait_ge(s["tables_ready"], 1)
                act.wait_ge(s["small_in"], l + 1)
                nc.scalar.activation(lamt[:, 0, :], lamt[:, 0, :], ACT.Exp)
                nc.scalar.activation(lbt[:, 1:3, :], lbt[:, 1:3, :], ACT.Exp)
                act.drain()
                act.sem_inc(s["small_exp"], 1)
                parts = [0]

                def part():
                    b = turn()
                    parts[0] += 1
                    act.wait_ge(s["w_used"], base + 2 * parts[0] + SPLIT_SLOTS)
                    return b, ps[:, b:b + 4, 0:HALF]

                def quad4(v):
                    return v.rearrange("p c (h t) -> p (c h) t", h=2)
                b, q4 = part()
                pv = ps[:, b:b + 4, 0:HALF].rearrange("p (c h) t -> p c h t", c=2)
                act.wait_ge(s["params_ready"], l + 1)
                nc.scalar.activation(a_x[:, :, 3:3 + HALF], pv[:, :, 0, :], ACT.Copy)
                nc.scalar.activation(a_x[:, :, 3 + HALF:3 + SEQ], pv[:, :, 1, 0:SEQ - HALF], ACT.Copy)
                nc.scalar.activation(a_xs[:, :, 3, :], pv[:, :, 1, SEQ - HALF:HALF], ACT.Copy)
                act.drain()
                act.sem_inc(quad_free[b // 4], 1)
                act.sem_inc(s["xa_sb"], 1)
                b, q4 = part()
                nc.scalar.activation(quad4(a_g), q4, ACT.Gelu_apprx_tanh).then_inc(quad_free[b // 4], 1)
                b, q4 = part()
                nc.scalar.activation(quad4(b_f), q4, ACT.Sigmoid).then_inc(s["f_sig"], 1)
                nc.scalar.activation(quad4(b_k), q4, ACT.Sigmoid, scale=-1.0)
                act.drain()
                act.sem_inc(s["k_sig"], 1)
                act.sem_inc(quad_free[b // 4], 1)
                b, q4 = part()
                nc.scalar.activation(quad4(b_q), q4, ACT.Silu)
                act.drain()
                act.sem_inc(s["q_silu"], 1)
                act.sem_inc(quad_free[b // 4], 1)
                for gate, (dst, name) in enumerate(((a_r, "r_gate"), (a_i, "i_gate"))):
                    b = turn()
                    act.wait_ge(s["gates_ps"], 2 * l + gate + 1)
                    for c in range(2):
                        nc.scalar.activation(dst[:, c, :].rearrange("p (h t) -> p h t", h=2), ps[:, b + 2 * c:b + 2 * c + 2, 0:HALF],
                                             ACT.Sigmoid, bias=gbias[:, gate, c:c + 1])
                    act.drain()
                    act.sem_inc(s[name], 1)
                    act.sem_inc(quad_free[b // 4], 1)
                for c in range(2):
                    nc.scalar.activation(a_t[:, c, :], a_r[:, c, :], ACT.Tanh, scale=c8[:, c:c + 1])
                for c in range(2):
                    nc.scalar.activation(a_a[:, c, :], a_r[:, c, :], ACT.Exp, scale=c8[:, c:c + 1])
                act.drain()
                act.sem_inc(s["tanh_a"], 1)
                b, q4 = part()
                nc.scalar.activation(b_v[:, 0:4, :], ps[:, b:b + 4, 0:256], ACT.Copy)
                nc.scalar.activation(b_v[0:DEC_BATCH, 4, :], ps[0:DEC_BATCH, b, 256:512], ACT.Copy)
                act.drain()
                act.sem_inc(s["v_b"], 1)
                act.sem_inc(quad_free[b // 4], 1)
                act.wait_ge(s["ratio_ready"], l + 1)
                nc.scalar.activation(a_t[:], a_t[:], ACT.Sqrt).then_inc(s["sqrt_a"], 1)
                b, q4 = part()
                nc.scalar.activation(quad4(b_g), q4, ACT.Silu)
                act.drain()
                act.sem_inc(s["g_b"], 1)
                act.sem_inc(quad_free[b // 4], 1)
                b = turn()
                act.wait_ge(s["states_ps"], l + 1)
                nc.scalar.activation(outst_t[:], ps[0:20, b, 0:D_A], ACT.Copy)
                act.drain()
                act.sem_inc(quad_free[b // 4], 1)
                act.wait_ge(s["clamped"], l + 1)
                nc.scalar.activation(b_t1[:], b_t1[:], ACT.Ln)
                nc.scalar.activation(b_t2[:], b_t2[:], ACT.Ln)
                act.drain()
                act.sem_inc(s["log_ab"], 1)
                act.dma_start(o_hp[l], outst_t[0:1, :]).then_inc(s["states_t"], 16)
                act.dma_start(o_cp[l, 0], outst_t[1:4, :]).then_inc(s["states_t"], 16)
                act.dma_start(o_hs[l], outst_t[4:12, :]).then_inc(s["states_t"], 16)
                act.dma_start(o_cs[l, :, 2, :], outst_t[12:20, :]).then_inc(s["states_t"], 16)
                act.wait_ge(s["y_a"], l + 1)
                for h in range(4):
                    act.dma_start(b_S0[64 * (h % 2):64 * (h % 2) + 64, h // 2], A["state_hgrn"][l, :, h].rearrange("n k v -> k n v"))\
                       .then_inc(s["hg_in"], 16)
                for n in range(len(LEVELS)):
                    act.wait_ge(s["arg_ready"], l * len(LEVELS) + n + 1)
                    nc.scalar.activation(lev_e[n % 2][:, :, 0:SEQ], lev_e[n % 2][:, :, 0:SEQ], ACT.Exp).then_inc(s["e_ready"], 1)
                act.wait_ge(s["eb_ready"], 2 * l + 1)
                nc.scalar.activation(b_t1[:, :, 0:SEQ], b_b[:, :, 0:SEQ], ACT.Exp)
                nc.scalar.activation(bl[:], b_b[:, :, CHUNK_B - 1:SEQ:CHUNK_B], ACT.Exp)
                nc.scalar.activation(b_t2[:, :, 0:SEQ], b_t2[:, :, 0:SEQ], ACT.Exp)
                act.drain()
                act.sem_inc(s["eb_ready"], 1)
                turns[0] += len(LEVELS) + 1

                def keep(place):
                    b, q4 = part()
                    nc.scalar.activation(quad4(place), q4, ACT.Copy)
                    act.drain()
                    act.sem_inc(s["kept_sb"], 1)
                    act.sem_inc(quad_free[b // 4], 1)

                def swap(src, dst):
                    for lo in (0, 64):
                        nc.scalar.activation(quad4(dst)[64 - lo:128 - lo], src[lo:lo + 64], ACT.Copy)
                    act.drain()
                    act.sem_inc(s["rot_swapped"], 1)
                keep(kept[0])
                b = turn()
                act.wait_ge(s["tr_ps"], l + 1)
                nc.scalar.activation(ksT[:], ps[0:DEC_BATCH, b + 2, 0:256], ACT.Copy)
                act.wait_ge(s["states_t"], (l + 1) * 64)
                nc.scalar.activation(b_kT, ps[:, b:b + 2, :].rearrange("p b (t c) -> p (b t) c", t=2), ACT.Copy)
                act.drain()
                act.sem_inc(s["ks_sb"], 1)
                act.sem_inc(s["kT_sb"], 1)
                act.sem_inc(quad_free[b // 4], 1)
                turn()
                turn()
                keep(kept[1])
                b = turn()
                act.wait_ge(s["o_ps"], l + 1)
                nc.scalar.activation(b_t1[:, :, 0:SEQ], ps[:, b:b + 2, :], ACT.Copy)
                nc.scalar.activation(b_t1[:, :, SEQ:TOK], ps[:, b + 2, 0:16].rearrange("p (c n) -> p c n", c=2), ACT.Copy)
                nc.scalar.activation(b_t2[:, :, 0:SEQ], ps[:, b:b + 2, :], ACT.Square)
                nc.scalar.activation(b_t2[:, :, SEQ:TOK], ps[:, b + 2, 0:16].rearrange("p (c n) -> p c n", c=2), ACT.Square)
                act.drain()
                act.sem_inc(s["sq_sb"], 1)
                act.sem_inc(quad_free[b // 4], 1)
                for i in range(2):
                    swap(quad4(kept[i]), c_swapped[i])
                for hh in range(2):
                    pr = slice(64 * hh, 64 * hh + 64)
                    act.dma_start(o_gp[l, 0].rearrange("(c hh) k v -> hh k c v", hh=2)[hh], b_S[pr, CHUNKS_B, :, 64 * hh:64 * hh + 64])\
                       .then_inc(s["hg_out"], 16)
                for h in range(4):
                    act.dma_start(o_gs[l, :, h].rearrange("n k v -> k n v"), b_S0[64 * (h % 2):64 * (h % 2) + 64, h // 2])\
                       .then_inc(s["hg_out"], 16)
                b = turn()
                act.wait_ge(s["ms_ps"], l + 1)
                nc.scalar.activation(quad4(b_b), ps[:, b:b + 4, 0:HALF], ACT.Sqrt, bias=eps[:, 1:2])
                act.drain()
                act.sem_inc(s["ms_sqrt"], 1)
                act.sem_inc(quad_free[b // 4], 1)

                for j in range(2):
                    n2 = l * 2 + j + 1
                    if j == 0:
                        act.wait_ge(s["y_b"], l + 1)
                        act.wait_ge(s["hg_out"], (l + 1) * 96)
                    else:
                        act.wait_ge(s["y_c"], l * 4 + 2)
                        act.wait_ge(s["cs_out"], (l * 2 + 1) * 64)
                    for h in range(2):
                        act.dma_start(c_S0[:, h], A["state_ret"][l, :, 2 * j + h].rearrange("n k v -> k n v")).then_inc(s["cs_in"], 16)
                    if j == 1:
                        for i in range(2):
                            b, src = part()
                            swap(src, c_swapped[i])
                    b, q4 = part()
                    nc.scalar.activation(c_v[:, 0:4, :], ps[:, b:b + 4, 0:256], ACT.Copy)
                    nc.scalar.activation(c_v[0:DEC_BATCH, 4, :], ps[0:DEC_BATCH, b, 256:512], ACT.Copy)
                    act.drain()
                    act.sem_inc(s["v_c"], 1)
                    act.sem_inc(quad_free[b // 4], 1)
                    b, q4 = part()
                    nc.scalar.activation(quad4(c_g), q4, ACT.Silu)
                    act.drain()
                    act.sem_inc(s["g_c"], 1)
                    act.sem_inc(quad_free[b // 4], 1)
                    turn()
                    b = turn()
                    act.wait_ge(s["ctr_ps"], n2)
                    nc.scalar.activation(ksT[:], ps[0:DEC_BATCH, b + 2, 0:256], ACT.Copy, scale=float(DK_C ** -0.5))
                    act.drain()
                    act.sem_inc(s["cks_sb"], 1)
                    for h in range(2):
                        nc.scalar.activation(c_kT[:, :, h, :], ps[:, b:b + 2, :].rearrange("p b (t h c) -> p (b t) h c", t=2, h=2)[:, :, h, :],
                                             ACT.Copy, scale=table("kdec")[:, 2 * j + h:2 * j + h + 1])
                    act.drain()
                    act.sem_inc(s["ckT_sb"], 1)
                    act.sem_inc(quad_free[b // 4], 1)
                    if j == 1:
                        for k in range(0, KC - 2, 2):
                            nc.scalar.activation(ysT[:, 0, k:k + 2, :], y32[:, k:k + 2, :], ACT.Copy).then_inc(s["y_high"], 1)
                    turn()
                    turn()
                    b = turn()
                    act.wait_ge(s["co_ps"], n2)
                    nc.scalar.activation(c_t1[:, :, 0:SEQ], ps[:, b:b + 2, :], ACT.Copy)
                    nc.scalar.activation(c_t1[:, :, SEQ:TOK], ps[:, b + 2, 0:16].rearrange("p (c n) -> p c n", c=2), ACT.Copy)
                    act.drain()
                    act.sem_inc(s["co_sb"], 1)
                    act.sem_inc(quad_free[b // 4], 1)
                    for h in range(2):
                        act.dma_start(o_rp[l, 0, 2 * j + h], c_S[:, 4, h, :]).then_inc(s["cs_out"], 16)
                        act.dma_start(o_rs[l, :, 2 * j + h].rearrange("n k v -> k n v"), c_S0[:, h]).then_inc(s["cs_out"], 16)
                    turn()
                    act.wait_ge(s["cd_ready"], n2)
                    nc.scalar.activation(c_sw[:], c_t1[:], ACT.Square).then_inc(s["csq_sb"], 1)
                    b = turn()
                    act.wait_ge(s["cvar_ps"], n2)
                    nc.scalar.activation(quad4(c_sw), ps[:, b:b + 4, 0:HALF], ACT.Sqrt, bias=eps[:, 2:3])
                    act.drain()
                    act.sem_inc(s["cvar_sqrt"], 1)
                    act.sem_inc(quad_free[b // 4], 1)

                for k in (KC - 2, KC - 1):
                    act.wait_ge(s["y_c"], 4 * l + k - KC + 5)
                    nc.scalar.activation(ysT[:, 0, k, :], y32[:, k, :], ACT.Copy).then_inc(s["y_high"], 1)
                turns[0] += 4
                act.wait_ge(s["y_low"], (l + 1) * 5)
                act.wait_ge(s["cs_out"], (l + 1) * 128)
                for n, nm in enumerate(("ln1_g", "ln1_b")):
                    act.dma_start(lngb1[:, n, :], A[nm][bass.ds(l, 1), :].to_broadcast([P, D_MODEL])).then_inc(s["ln_loaded"], 16)
                act.wait_ge(s["mv_ready"], 2 * l + 1)
                nc.scalar.activation(lnrs[:, :, 0], mv[:, :, 1], ACT.Sqrt, bias=eps[:, 0:1]).then_inc(s["std_ready"], 1)
                act.wait_ge(s["lnrs_ready"], 2 * l + 1)
                for t in range(TILES):
                    r = rows_of(t)
                    nc.scalar.activation(x[0:r, t, :], x[0:r, t, :], ACT.Identity, bias=lnrs[0:r, t, 1:2],
                                         scale=lnrs[0:r, t, 0:1]).then_inc(s["ln_scaled"], 1)
                for t in range(TILES):
                    r = rows_of(t)
                    b = turn()
                    act.wait_ge(s["ln1_done"], l * TILES + t + 1)
                    nc.scalar.activation(xsM[0:r, 0, t, :], x[0:r, t, :], ACT.Copy).then_inc(s["xm_high"], 1)
                    act.wait_ge(s["x1T_ps"], l * TILES + t + 1)
                    src = ps[:, b:b + 2, :].rearrange("p b (k c) -> p (b k) c", c=P)[:, :, 0:r]
                    nc.scalar.activation(x1T[:, :, t * P:t * P + r], src, ACT.Copy)
                    act.drain()
                    act.sem_inc(s["x1T_sb"], 1)
                    if t == TILES - 1:
                        act.wait_ge(s["lgT_ps"], 2 * l + 1)
                        nc.scalar.activation(lgT[:, 0:HALF], ps[0:N_EXPERTS, b + 2, 0:HALF], ACT.Identity, bias=rb[:, 0:1])
                        act.drain()
                    act.sem_inc(quad_free[b // 4], 1)
                b = turn()
                act.wait_ge(s["lgT_ps"], 2 * l + 2)
                nc.scalar.activation(lgT[:, HALF:TOK], ps[0:N_EXPERTS, b, 0:HALF], ACT.Identity, bias=rb[:, 0:1])
                act.drain()
                act.sem_inc(s["lgT_sb"], 1)
                act.sem_inc(quad_free[b // 4], 1)
                act.wait_ge(s["lg_shifted"], l + 1)
                nc.scalar.activation(rt[:, 0], rt[:, 0], ACT.Exp).then_inc(s["prob_exp"], 1)
                act.wait_ge(s["xm_low"], (l + 1) * TILES)
                for t in range(TILES):
                    r = rows_of(t)
                    nc.scalar.activation(x[0:r, t, :], x[0:r, t, :], ACT.Copy, scale=float(ALPHA)).then_inc(s["x_scaled"], 1)

                act.wait_ge(s["routed"], l + 1)
                after = act.value_load(passes_i[0:1, bass.ds(l + 1, 1)], min_val=0, max_val=DEPTH * PASSES)
                most = act.value_load(cnt_i[0:1, bass.ds(l, 1)], min_val=0, max_val=TOK)
                with act.Fori(0, PASSES) as rnd:
                    with act.If(most > rnd * SLOTS):
                        def gathered(n, ks):
                            for k in ks:
                                act.wait_ge(s["gath_ps"], n * (KC // 2) + k + 1)
                                nc.scalar.activation(XeT[:, 0, 2 * k:2 * k + 2, :].rearrange("p k c -> p (k c)"), ps[:, k, :], ACT.Copy)\
                                    .then_inc(s["gath_high"], 1)

                        def experts(g, last):
                            n = act.snap((before + rnd) * PAIRS + g)
                            first = act.snap(base + MIX_UNITS + rnd * PASS_UNITS + g * PAIR_UNITS + SPLIT_SLOTS)

                            def silu(e):
                                act.wait_ge(s["w_used"], first + GATE_DONE[e])
                                act.wait_ge(s["h_done"], n * 2 + e + 1)
                                nc.scalar.activation(act_g[:], ps[:, 2 * e, :], ACT.Silu)
                                act.drain()
                                act.sem_inc(s["silu_done"], 1)
                                act.sem_inc(bank_free[2 * e], 1)

                            def ht(e):
                                act.wait_ge(s["ht_ps"], n * 2 + e + 1)
                                nc.scalar.activation(hT[:, 0].rearrange("p q c -> p (q c)"), ps[:, 4, :], ACT.Copy).then_inc(s["ht_high"], 1)

                            def out(e):
                                for half in range(2):
                                    act.wait_ge(s["w_used"], first + DOWN_FROM[e] + 2 * half + 2)
                                    nc.scalar.activation(ye[:, e, 0, half * 512:half * 512 + 512], ps[:, 5 + half, :], ACT.Copy)\
                                        .then_inc(s["ye_high"], 1)
                            silu(0)
                            for e in range(2):
                                act.wait_ge(s["pt_ps"], n * 2 + e + 1)
                                nc.scalar.activation(PT[:, e, :], ps[:, 4 + e, :].bitcast(bf16)[:, 0:TOK], ACT.Copy)
                                act.drain()
                                act.sem_inc(s["pt_sb"], 1)
                                act.sem_inc(bank_free[4 + e], 1)
                            silu(1)
                            ht(0)
                            out(0)
                            ht(1)
                            if not last:
                                gathered(n + 1, (0, 1))
                            out(1)
                            if not last:
                                gathered(n + 1, (2, 3))
                        gathered(act.snap((before + rnd) * PAIRS), range(KC // 2))
                        with act.Fori(0, PAIRS - 1) as g:
                            experts(g, False)
                        experts(PAIRS - 1, True)
                act.wait_ge(s["w_used"], l * MIX_UNITS + MIX_UNITS + after * PASS_UNITS + SPLIT_SLOTS)
                for n, nm in enumerate(("ln2_g", "ln2_b")):
                    act.dma_start(lngb2[:, n, :], A[nm][bass.ds(l, 1), :].to_broadcast([P, D_MODEL])).then_inc(s["ln_loaded"], 16)
                act.wait_ge(s["mv_ready"], 2 * l + 2)
                nc.scalar.activation(lnrs[:, :, 0], mv[:, :, 1], ACT.Sqrt, bias=eps[:, 0:1]).then_inc(s["std_ready"], 1)
                act.wait_ge(s["lnrs_ready"], 2 * l + 2)
                for t in range(TILES):
                    r = rows_of(t)
                    nc.scalar.activation(x[0:r, t, :], x[0:r, t, :], ACT.Identity, bias=lnrs[0:r, t, 1:2],
                                         scale=lnrs[0:r, t, 0:1]).then_inc(s["ln2_scaled"], 1)
            for t in range(4):
                act.wait_ge(s["x_tile_ready"], DEPTH * TILES + t + 1)
                act.dma_start(o_yp[0, t * P:(t + 1) * P, :], x[:, t, :]).then_inc(s["out_done"], 16)
            act.wait_ge(s["x_tile_ready"], (DEPTH + 1) * TILES)
            act.dma_start(o_ys.rearrange("b o d -> (b o) d"), x[0:DEC_BATCH, 4, :]).then_inc(s["out_done"], 16)
            act.wait_ge(s["out_done"], (DEPTH + TILES) * 16)
            act.wait_ge(s["states_t"], DEPTH * 64)
            act.wait_ge(s["hg_out"], DEPTH * 96)
            act.wait_ge(s["cs_out"], DEPTH * 2 * 64)

        @block.vector
        def _(dve):
            V = nc.vector
            TT, TS, STT = V.tensor_tensor, V.tensor_scalar, V.scalar_tensor_tensor
            dve.sem_inc(s["v_split"], LOW_CREDITS["V"])
            dve.sem_inc(s["g_split"], LOW_CREDITS["G"])
            dve.sem_inc(s["w_used"], SPLIT_SLOTS)
            dve.sem_inc(s["h_done"], 1)
            for q in quad_free + bank_free:
                dve.sem_inc(q, 1)
            V.memset(passes_i[:], 0)
            V.memset(passes_f[:], 0.0)
            V.memset(eps[:, 0:1], LN_EPS)
            V.memset(eps[:, 1:2], RMS_EPS)
            V.memset(eps[:, 2:3], GN_EPS)
            V.memset(ones_bf[:], 1.0)
            V.memset(lg[:], 0.0)
            V.memset(mv[:], 1.0)
            V.memset(posm[:], 0.0)
            dve.drain()
            dve.sem_inc(s["passes_known"], 1)
            dve.wait_ge(s["x_loaded"], TILES * 16)
            dve.sem_inc(s["x_tile_ready"], TILES)
            dve.wait_ge(s["ident_loaded"], 16)
            dve.wait_ge(s["tables_loaded"], 64)
            nc.vector.tensor_copy(lev[:], Z[:, 0:len(LEVELS) * P])
            V.tensor_copy(before_bf[:], table("before"))
            V.tensor_copy(ident_bf[:], ident)
            dve.drain()
            dve.sem_inc(s["tables_ready"], 1)

            with dve.Fori(0, DEPTH) as l:
                dve.wait_ge(s["passes_known"], l + 1)
                before = dve.value_load(passes_i[0:1, bass.ds(l, 1)], min_val=0, max_val=DEPTH * PASSES)
                base = dve.snap(l * MIX_UNITS + before * PASS_UNITS)
                turns = [0]
                lows = [0]
                parts = [0]

                def turn():
                    turns[0] += 1
                    return 4 * ((turns[0] - 1) % 2)

                def low(first, lows, k):
                    if lows[k] != "V":
                        return
                    dve.wait_ge(s["w_high"], first + k + 1)
                    experts = lows is PAIR_LOWS
                    TT(split_slot(k, 1, experts), raw[:, k % RAW_SLOTS, :], split_slot(k, 0, experts).bitcast(f32),
                       ALU.subtract).then_inc(s["v_split"], 1)

                def next_part(n=1):
                    for _ in range(2 * n):
                        low(base, MIX_LOWS, lows[0])
                        lows[0] += 1

                next_part(2)
                for t in range(TILES):
                    r = rows_of(t)
                    b = turn()
                    dve.wait_ge(s["xT_high"], l * TILES + t + 1)
                    src = ps[:, b:b + 2, :].rearrange("p b (k c) -> p (b k) c", c=P)[:, :, 0:r]
                    TT(xsT[:, 1, :, t * P:t * P + r], src, xsT[:, 0, :, t * P:t * P + r].bitcast(f32), ALU.subtract)
                    dve.drain()
                    dve.sem_inc(s["xT_low"], 1)
                    dve.sem_inc(quad_free[b // 4], 1)

                dve.wait_ge(s["params_loaded"], (l + 1) * (2 * 9 + 16 + 3) * 16 - 0)
                STT(lamt[:, 0, :], lam[:], -1.0, lam[:], ALU.mult, ALU.min)
                V.tensor_tensor(lbt[:, 0, :], lbl[:, 0, :], lbl[:, 1, :], ALU.max)
                dve.drain()
                TT(lbt[:, 1, :], lbl[:, 0, :], lbt[:, 0, :], ALU.subtract)
                TT(lbt[:, 2, :], lbl[:, 1, :], lbt[:, 0, :], ALU.subtract)
                dve.drain()
                dve.sem_inc(s["small_in"], 1)
                dve.wait_ge(s["small_exp"], l + 1)
                TS(lamt[:, 1, :], lamt[:, 0, :], 2.0, None, ALU.add)
                TT(lbt[:, 3, :], lbt[:, 1, :], lbt[:, 2, :], ALU.add)
                dve.drain()
                V.reciprocal(lamt[:, 2, :], lamt[:, 1, :])
                V.reciprocal(lbt[:, 4, :], lbt[:, 3, :])
                dve.drain()
                TT(lamt[:, 0, :], lamt[:, 0, :], lamt[:, 2, :], ALU.mult)
                STT(lb[:], lbt[:, 2, :], flag[:, 0:1], lbt[:, 4, :], ALU.mult, ALU.mult)
                dve.drain()
                TT(lamt[:, 1, :], lamt[:, 0, :], lamt[:, 0, :], ALU.mult)
                TS(oml[:], lb[:], -1.0, 1.0, ALU.mult, ALU.add)
                V.memset(lamt[:, 2, :], 1.0 / 17)
                dve.drain()
                for odd in (15, 13, 11, 9, 7, 5, 3, 1):
                    TT(lamt[:, 2, :], lamt[:, 2, :], lamt[:, 1, :], ALU.mult)
                    dve.drain()
                    TS(lamt[:, 2, :], lamt[:, 2, :], 1.0 / odd, None, ALU.add)
                    dve.drain()
                TT(lamt[:, 2, :], lamt[:, 2, :], lamt[:, 0, :], ALU.mult)
                TS(lamt[:, 1, :], lam[:], 0.0, RGLRU_C, ALU.min, ALU.mult)
                dve.drain()
                STT(c8[:], lamt[:, 2, :], -2.0 * RGLRU_C, lamt[:, 1, :], ALU.mult, ALU.add)
                V.memset(a_x[:, :, 0:3], 0.0)
                for c in range(2):
                    V.tensor_copy(a_xs[:, c, 0:3, :], csst[:, c])
                dve.drain()
                dve.sem_inc(s["params_ready"], 1)

                next_part()
                dve.wait_ge(s["xa_sb"], l + 1)
                for j in range(CONV_W):
                    for c in range(2):
                        taps = ((a_u[:, c, 0:SEQ], a_x[:, c, j:j + SEQ]), (a_u[:, c, SEQ:TOK], a_xs[:, c, j, :]))
                        for dst, src in taps:
                            if j == 0:
                                TS(dst, src, convw[:, c, 0:1], convb[:, c:c + 1], ALU.mult, ALU.add)
                            else:
                                STT(dst, src, convw[:, c, j:j + 1], dst, ALU.mult, ALU.add)
                    dve.drain()
                dve.sem_inc(s["u_ready"], 1)
                next_part()
                turns[0] += 4
                turns[0] += 2
                next_part()
                dve.wait_ge(s["tanh_a"], l + 1)
                TS(a_r[:], a_t[:], -1.0, 1.0, ALU.mult, ALU.add)
                TT(a_i[:], a_i[:], a_u[:], ALU.mult)
                dve.drain()
                V.reciprocal(a_r[:], a_r[:])
                dve.drain()
                TT(a_t[:], a_t[:], a_r[:], ALU.mult)
                dve.drain()
                TS(a_t[:], a_t[:], -2.0, 0.0, ALU.mult, ALU.max)
                dve.drain()
                dve.sem_inc(s["ratio_ready"], 1)
                next_part()
                dve.wait_ge(s["k_sig"], l + 1)
                for c in range(2):
                    TS(b_f[:, c, :], b_f[:, c, :], oml[:, c:c + 1], lb[:, c:c + 1], ALU.mult, ALU.add)
                    TS(b_k[:, c, :], b_k[:, c, :], oml[:, c:c + 1], None, ALU.mult)
                dve.drain()
                TS(b_f[:], b_f[:], F_TINY, None, ALU.max).then_inc(s["k_ready"], 1)
                dve.wait_ge(s["sqrt_a"], l + 1)
                TT(a_t[:], a_t[:], a_i[:], ALU.mult)
                dve.drain()
                for c in range(2):
                    V.tensor_tensor_scan(a_i[:, c, 0:SEQ], a_a[:, c, 0:SEQ], a_t[:, c, 0:SEQ], 0.0, ALU.mult, ALU.add)
                TT(a_i[:, :, SEQ:TOK], a_a[:, :, SEQ:TOK], h0[:], ALU.mult)
                dve.drain()
                TT(a_i[:, :, SEQ:TOK], a_i[:, :, SEQ:TOK], a_t[:, :, SEQ:TOK], ALU.add)
                dve.drain()
                V.tensor_copy(outst[:, :, 0:1], a_i[:, :, SEQ - 1:SEQ])
                V.tensor_copy(outst[:, :, 1:4], a_x[:, :, SEQ:SEQ + 3])
                V.tensor_copy(outst[:, :, 4:12], a_i[:, :, SEQ:TOK])
                V.tensor_copy(outst[:, :, 12:20], a_xs[:, :, 3, :])
                TT(y32[:, 0:2, :], a_i[:], a_g[:], ALU.mult)
                dve.drain()
                dve.sem_inc(s["states_sb"], 1)
                dve.sem_inc(s["y_a"], 1)
                turns[0] += 3

                TS(b_t1[:], b_f[:], F_SPLIT, None, ALU.max)
                TS(b_t2[:], b_f[:], 1.0 / F_SPLIT, 1.0, ALU.mult, ALU.min)
                dve.drain()
                dve.sem_inc(s["clamped"], 1)
                next_part(2)
                dve.wait_ge(s["v_b"], l + 1)
                for h in range(4):
                    TT(b_Vx[:, h], b_v[0:DEC_BATCH, 4, h * 64:(h + 1) * 64].unsqueeze(1).to_broadcast([DEC_BATCH, DEC_BATCH, 64]),
                       table("seqdelta", DEC_BATCH).unsqueeze(2).to_broadcast([DEC_BATCH, DEC_BATCH, 64]), ALU.mult)
                dve.drain()
                dve.sem_inc(s["vx_ready"], 1)
                b = turn()
                dve.wait_ge(s["lev_ps"], l * (len(LEVELS) + 1) + 1)
                acc16 = b_acc.rearrange("p h t c s -> p (h t c) s")
                TT(acc16, ps[:, b:b + 4, :].rearrange("p b (n s) -> p (b n) s", s=P), ident.unsqueeze(1).to_broadcast([P, 16, P]), ALU.mult)
                dve.drain()
                dve.sem_inc(s["lev_done"], 1)
                dve.sem_inc(quad_free[b // 4], 1)
                dve.wait_ge(s["log_ab"], l + 1)
                TT(b_t1[:], b_t1[:], b_t2[:], ALU.add)
                dve.drain()
                for c in range(2):
                    V.tensor_tensor_scan(b_b[:, c, 0:SEQ], table("reset"), b_t1[:, c, 0:SEQ], 0.0, ALU.mult, ALU.add)
                dve.drain()

                def level_done(n):
                    b = turn()
                    wait_apart(dve, s["lev_ps"], l * (len(LEVELS) + 1) + n + 2)
                    mask = lev[:, n * P:(n + 1) * P].unsqueeze(1).to_broadcast([P, 16, P])
                    V.copy_predicated(acc16, mask, ps[:, b:b + 4, :].rearrange("p b (n s) -> p (b n) s", s=P))
                    dve.drain()
                    dve.sem_inc(s["lev_done"], 1)
                    dve.sem_inc(quad_free[b // 4], 1)
                def exponents(n):
                    m = LEVELS[n]
                    for c in range(2):
                        bb = b_b[:, c, 0:SEQ].rearrange("p (n m) -> p n m", m=2 * m)
                        ee = lev_e[n % 2][:, c, 0:SEQ].rearrange("p (n m) -> p n m", m=2 * m)
                        mid = bb[:, :, m - 1:m].to_broadcast([P, SEQ // (2 * m), m])
                        TT(ee[:, :, m:2 * m], bb[:, :, m:2 * m], mid, ALU.subtract)
                        TT(ee[:, :, 0:m], mid, bb[:, :, 0:m], ALU.subtract)
                    dve.drain()
                    dve.sem_inc(s["arg_ready"], 1)

                exponents(0)
                for n, m in enumerate(LEVELS):
                    if n + 1 < len(LEVELS):
                        exponents(n + 1)
                    dve.wait_ge(s["e_ready"], l * len(LEVELS) + n + 1)
                    for c in range(2):
                        ee = lev_e[n % 2][:, c, 0:SEQ].rearrange("p (n m) -> p n m", m=2 * m)
                        oo = lev_qk[n % 2][:, c, 0:SEQ].rearrange("p (n m) -> p n m", m=2 * m)
                        qq = b_q[:, c, 0:SEQ].rearrange("p (n m) -> p n m", m=2 * m)
                        kk = b_k[:, c, 0:SEQ].rearrange("p (n m) -> p n m", m=2 * m)
                        TT(oo[:, :, m:2 * m], qq[:, :, m:2 * m], ee[:, :, m:2 * m], ALU.mult)
                        TT(oo[:, :, 0:m], kk[:, :, 0:m], ee[:, :, 0:m], ALU.mult)
                    dve.drain()
                    dve.sem_inc(s["qk_ready"], 1)
                    if n > 0:
                        level_done(n - 1)
                last = b_b[:, :, CHUNK_B - 1:SEQ:CHUNK_B].unsqueeze(3).to_broadcast([P, 2, CHUNKS_B, CHUNK_B])
                TT(b_t2[:, :, 0:SEQ].rearrange("p c (n m) -> p c n m", m=CHUNK_B), last,
                   b_b[:, :, 0:SEQ].rearrange("p c (n m) -> p c n m", m=CHUNK_B), ALU.subtract)
                dve.drain()
                dve.sem_inc(s["eb_ready"], 1)
                level_done(len(LEVELS) - 1)
                turn()
                dve.wait_ge(s["eb_ready"], 2 * l + 2)
                TT(b_q[:, :, 0:SEQ], b_q[:, :, 0:SEQ], b_t1[:, :, 0:SEQ], ALU.mult)
                TT(b_k[:, :, 0:SEQ], b_k[:, :, 0:SEQ], b_t2[:, :, 0:SEQ], ALU.mult)
                dve.drain()
                dve.sem_inc(s["p_ready"], 1)
                turn()
                b = turn()
                dve.wait_ge(s["hg_in"], (l + 1) * 64)
                TT(b_S0, b_S0, b_f[:, :, SEQ:TOK].unsqueeze(3).to_broadcast([P, 2, DEC_BATCH, DK_B]), ALU.mult)
                dve.drain()
                dve.wait_ge(s["kv_ps"], l + 1)
                TT(b_S0.rearrange("p c n v -> p c (n v)"), ps[:, b:b + 2, :], b_S0.rearrange("p c n v -> p c (n v)"), ALU.add)
                dve.drain()
                dve.sem_inc(s["s_new"], 1)
                dve.sem_inc(quad_free[b // 4], 1)
                b = turn()
                dve.wait_ge(s["ds_ps"], l + 1)
                V.memset(b_S[:, 0], 0.0)
                for odd in range(2):
                    TT(b_S[:, 1 + odd::2], ps[:, b + 2 * odd:b + 2 * odd + 2, :].rearrange("p b (n c k) -> p (b n) c k", c=2, k=P),
                       table("blockdiag").unsqueeze(1).unsqueeze(1).to_broadcast([P, 4, 2, P]), ALU.mult)
                dve.drain()
                dve.sem_inc(quad_free[b // 4], 1)
                for ch in range(1, CHUNKS_B):
                    for c in range(2):
                        STT(b_S[:, ch + 1, c, :], b_S[:, ch, c, :], bl[:, c, ch:ch + 1], b_S[:, ch + 1, c, :], ALU.mult, ALU.add)
                    dve.drain()
                dve.sem_inc(s["s_ready"], 1)
                turn()
                for i, dst in enumerate((c_k, c_q)):
                    dve.wait_ge(s["kept_sb"], 2 * l + i + 1)
                    TT(dst, kept[i], table("cos").unsqueeze(1).to_broadcast([P, 2, TOK]), ALU.mult)
                turn()
                turn()
                dve.wait_ge(s["ms_sqrt"], l + 1)
                V.reciprocal(b_b[:], b_b[:])
                dve.drain()
                STT(b_t1[:], b_t1[:], ng[:, 0:1], b_b[:], ALU.mult, ALU.mult)
                dve.drain()
                dve.wait_ge(s["g_b"], l + 1)
                TT(y32[:, 2:4, :], b_t1[:], b_g[:], ALU.mult)
                dve.drain()
                dve.sem_inc(s["y_b"], 1)

                cosb = table("cos").rearrange("p (h t) -> p h t", h=2)
                for j in range(2):
                    n2 = l * 2 + j + 1
                    for i, (dst, name) in enumerate(((c_k, "rot_k"), (c_q, "rot_q"))):
                        if j == 1:
                            b = turn()
                            dve.wait_ge(s["rot_swapped"], l * 4 + 2 * j + i + 1)
                            pv = ps[:, b:b + 4, 0:HALF].rearrange("p (c h) t -> p c h t", c=2)
                            for c in range(2):
                                TT(dst[:, c, :].rearrange("p (h t) -> p h t", h=2), pv[:, c], cosb, ALU.mult)
                            dve.drain()
                            dve.sem_inc(quad_free[b // 4], 1)
                        next_part()
                        dve.wait_ge(s["rot_sin"], l * 4 + 2 * j + i + 1)
                        TT(dst[:], dst[:], c_swapped[i], ALU.add)
                        dve.drain()
                        dve.sem_inc(s[name], 1)
                    turn()
                    turn()
                    next_part(2)
                    dve.wait_ge(s["v_c"], n2)
                    for h in range(2):
                        TT(c_Vx[:, h], c_v[0:DEC_BATCH, 4, h * P:(h + 1) * P].unsqueeze(1).to_broadcast([DEC_BATCH, DEC_BATCH, P]),
                           table("seqdelta", DEC_BATCH).unsqueeze(2).to_broadcast([DEC_BATCH, DEC_BATCH, P]), ALU.mult)
                    dve.drain()
                    dve.sem_inc(s["cvx_ready"], 1)
                    b = turn()
                    dve.wait_ge(s["sc_ps"], n2)
                    dm = table("dret").rearrange("p (h c) -> p h c", h=4)[:, 2 * j:2 * j + 2].unsqueeze(1).to_broadcast([P, 4, 2, P])
                    TT(c_sc, ps[:, b:b + 2, :].rearrange("p b (t h c) -> p (b t) h c", t=2, h=2), dm, ALU.mult)
                    qdt = table("qdec").rearrange("p (h c) -> p h c", h=4)[:, 2 * j:2 * j + 2].unsqueeze(2).to_broadcast([P, 2, 4, P])
                    TT(c_qd, c_q[:, :, 0:SEQ].rearrange("p h (t c) -> p h t c", t=4), qdt, ALU.mult)
                    dve.drain()
                    dve.sem_inc(s["sc_ready"], 1)
                    dve.sem_inc(s["qd_ready"], 1)
                    dve.sem_inc(quad_free[b // 4], 1)
                    turn()
                    b = turn()
                    dve.wait_ge(s["cs_in"], n2 * 32)
                    dve.wait_ge(s["ckv_ps"], n2)
                    for h in range(2):
                        v0 = c_S0[:, h].rearrange("p n v -> p (n v)").rearrange("p (b c) -> p b c", b=2)
                        STT(v0, v0, GAMMA[2 * j + h], ps[:, b + 2 * h:b + 2 * h + 2, :], ALU.mult, ALU.add)
                    dve.drain()
                    dve.sem_inc(s["cs_new"], 1)
                    dve.sem_inc(quad_free[b // 4], 1)
                    b = turn()
                    dve.wait_ge(s["cds_ps"], n2)
                    V.tensor_copy(c_S[:, 1:].rearrange("p t h c -> p (t h c)"), ps[:, b:b + 2, :].rearrange("p b c -> p (b c)"))
                    dve.drain()
                    dve.sem_inc(quad_free[b // 4], 1)
                    for t in range(1, 4):
                        for h in range(2):
                            STT(c_S[:, t + 1, h, :], c_S[:, t, h, :], GAMMA_CHUNK[2 * j + h], c_S[:, t + 1, h, :], ALU.mult, ALU.add)
                        dve.drain()
                    dve.sem_inc(s["cs_ready"], 1)
                    if j == 1:
                        for k in range(0, KC - 2, 2):
                            dve.wait_ge(s["y_high"], l * 5 + k // 2 + 1)
                            TT(ysT[:, 1, k:k + 2, :], y32[:, k:k + 2, :], ysT[:, 0, k:k + 2, :].bitcast(f32), ALU.subtract)\
                                .then_inc(s["y_low"], 1)
                    turn()
                    b = turn()
                    dve.wait_ge(s["cmean_ps"], n2)
                    o4 = c_t1.rearrange("p c (h t) -> p (c h) t", h=2)
                    TT(o4, o4, ps[:, b:b + 4, 0:HALF], ALU.subtract)
                    dve.drain()
                    dve.sem_inc(s["cd_ready"], 1)
                    dve.sem_inc(quad_free[b // 4], 1)
                    turn()
                    dve.wait_ge(s["g_c"], n2)
                    dve.wait_ge(s["csq_sb"], n2)
                    TT(c_t1[:], c_t1[:], c_g[:], ALU.mult)
                    dve.wait_ge(s["cvar_sqrt"], n2)
                    for h in range(2):
                        V.reciprocal(c_sw[:, h], c_sw[:, h])
                        dve.drain()
                        TT(y32[:, 4 + 2 * j + h, :], c_t1[:, h], c_sw[:, h], ALU.mult).then_inc(s["y_c"], 1)

                for k in (KC - 2, KC - 1):
                    dve.wait_ge(s["y_high"], l * 5 + k - KC + 6)
                    TT(ysT[:, 1, k, :], y32[:, k, :], ysT[:, 0, k, :].bitcast(f32), ALU.subtract).then_inc(s["y_low"], 1)
                def column_stats(i, chunks, tiles=range(TILES)):
                    w = D_MODEL // chunks
                    for t in tiles:
                        r = rows_of(t)
                        V.bn_stats(stats[0:r, t, 6 * i:6 * i + 6], x[0:r, t, i * w:(i + 1) * w])

                for cc in range(4):
                    b = turn()
                    if cc < 2:
                        next_part()
                    cols = slice(cc * 256, cc * 256 + 256)
                    dve.wait_ge(s["w_used"], base + 2 * len(IN_PARTS) + 2 * cc + 2 + SPLIT_SLOTS)
                    STT(x[:, 0:4, cols], x[:, 0:4, cols], float(ALPHA), ps[:, b:b + 4, 0:256], ALU.mult, ALU.add)
                    STT(x[0:DEC_BATCH, 4, cols], x[0:DEC_BATCH, 4, cols], float(ALPHA), ps[0:DEC_BATCH, b, 256:512], ALU.mult, ALU.add)
                    dve.drain()
                    dve.sem_inc(quad_free[b // 4], 1)
                    column_stats(cc, 4)
                assert lows[0] == MIX_UNITS, lows

                def norm_stats(which, chunks):
                    dve.drain()
                    for t in range(TILES):
                        r = rows_of(t)
                        V.bn_aggr(mv[0:r, t, :], stats[0:r, t, 0:6 * chunks])
                    dve.drain()
                    dve.sem_inc(s["mv_ready"], 1)
                    dve.wait_ge(s["std_ready"], 2 * l + which)
                    V.reciprocal(lnrs[:, :, 0], lnrs[:, :, 0])
                    dve.drain()
                    STT(lnrs[:, :, 1], mv[:, :, 0], -1.0, lnrs[:, :, 0], ALU.mult, ALU.mult)
                    dve.drain()
                    dve.sem_inc(s["lnrs_ready"], 1)

                def gain(t, gb):
                    r = rows_of(t)
                    TT(x[0:r, t, :], x[0:r, t, :], gb[0:r, 0, :], ALU.mult)
                    dve.drain()
                    TT(x[0:r, t, :], x[0:r, t, :], gb[0:r, 1, :], ALU.add)
                    dve.drain()

                norm_stats(1, 4)
                dve.wait_ge(s["ln_loaded"], l * 64 + 32)
                for t in range(TILES):
                    dve.wait_ge(s["ln_scaled"], l * TILES + t + 1)
                    gain(t, lngb1)
                    dve.sem_inc(s["ln1_done"], 1)
                for t in range(TILES):
                    r = rows_of(t)
                    dve.wait_ge(s["xm_high"], l * TILES + t + 1)
                    TT(xsM[0:r, 1, t, :], x[0:r, t, :], xsM[0:r, 0, t, :].bitcast(f32), ALU.subtract).then_inc(s["xm_low"], 1)
                turns[0] += TILES + 1

                b = turn()
                dve.wait_ge(s["lg_ps"], l + 1)
                V.tensor_copy(lg[:, 0:4, :], ps[:, b, 0:64].rearrange("p (t e) -> p t e", t=4))
                V.tensor_copy(lg[0:DEC_BATCH, 4, :], ps[0:DEC_BATCH, b, 64:80])
                dve.drain()
                dve.sem_inc(quad_free[b // 4], 1)

                def top(out, src):
                    V.tensor_reduce(out, src, AX.X, ALU.max)
                    dve.drain()

                def wide(v):
                    return v.to_broadcast([P, TILES, N_EXPERTS])
                mx, sm = rg[:, 0, :, 0:1], rg[:, 0, :, 1:2]
                v1, v2, k1 = rg[:, 0, :, 2:3], rg[:, 0, :, 3:4], rg[:, 7, :, 0:1]
                top(mx, lg[:])
                TT(rt[:, 0], lg[:], wide(mx), ALU.subtract)
                dve.drain()
                dve.sem_inc(s["lg_shifted"], 1)
                dve.wait_ge(s["prob_exp"], l + 1)
                V.tensor_reduce(sm, rt[:, 0], AX.X, ALU.add)
                dve.drain()
                V.reciprocal(sm, sm)
                dve.drain()
                pr = rt[:, 0]
                TT(pr, pr, wide(sm), ALU.mult)
                dve.drain()
                p4 = pr.rearrange("p t (g e) -> p t g e", g=4)
                TT(rg[:, 1], p4[:, :, :, 0], p4[:, :, :, 1], ALU.max)
                TT(rg[:, 2], p4[:, :, :, 0], p4[:, :, :, 1], ALU.min)
                TT(rg[:, 3], p4[:, :, :, 2], p4[:, :, :, 3], ALU.max)
                TT(rg[:, 4], p4[:, :, :, 2], p4[:, :, :, 3], ALU.min)
                dve.drain()
                TT(rg[:, 5], rg[:, 1], rg[:, 3], ALU.max)
                TT(rg[:, 6], rg[:, 1], rg[:, 3], ALU.min)
                TT(rg[:, 2], rg[:, 2], rg[:, 4], ALU.max)
                dve.drain()
                TT(rg[:, 6], rg[:, 6], rg[:, 2], ALU.max)
                dve.drain()
                TT(rg[:, 5], rg[:, 5], rg[:, 6], ALU.add)
                dve.drain()

                def first_of(dst, src, best, key, scratch, n):
                    top(best, src)
                    TT(dst, src, best.to_broadcast([P, TILES, n]), ALU.is_equal)
                    dve.drain()
                    TT(dst, dst, key.unsqueeze(1).to_broadcast([P, TILES, n]), ALU.mult)
                    dve.drain()
                    top(scratch, dst)
                    TT(dst, dst, scratch.to_broadcast([P, TILES, n]), ALU.is_equal)
                    dve.drain()
                first_of(rg[:, 1], rg[:, 5], mx, table("key4"), k1, 4)
                selb = rg[:, 1].unsqueeze(3).to_broadcast([P, TILES, 4, 4])
                pm = rt[:, 1]
                pm4 = pm.rearrange("p t (g e) -> p t g e", g=4)
                TS(rg[:, 2], rg[:, 1], 1.0, None, ALU.subtract)
                for t in range(TILES):
                    TT(pm4[:, t], p4[:, t], selb[:, t], ALU.mult)
                dve.drain()
                for t in range(TILES):
                    TT(pm4[:, t], pm4[:, t], rg[:, 2].unsqueeze(3).to_broadcast([P, TILES, 4, 4])[:, t], ALU.add)
                dve.drain()
                first_of(rt[:, 2], pm, v1, table("key16"), k1, N_EXPERTS)
                STT(rt[:, 3], rt[:, 2], -4.0, pm, ALU.mult, ALU.add)
                dve.drain()
                first_of(rt[:, 4], rt[:, 3], v2, table("key16"), k1, N_EXPERTS)
                TT(rt[:, 5], rt[:, 2], rt[:, 4], ALU.add)
                TT(sm, v1, v2, ALU.add)
                dve.drain()
                V.tensor_copy(mask_bf[:], rt[:, 5])
                V.reciprocal(sm, sm)
                dve.drain()
                dve.sem_inc(s["mask_ready"], 1)
                TT(v1, v1, sm, ALU.mult)
                TT(v2, v2, sm, ALU.mult)
                dve.drain()
                TT(rt[:, 2], rt[:, 2], wide(v1), ALU.mult)
                TT(rt[:, 4], rt[:, 4], wide(v2), ALU.mult)
                dve.drain()
                TT(comb[:], rt[:, 2], rt[:, 4], ALU.add)
                b = turn()
                dve.wait_ge(s["pos_ps"], l + 1)
                TS(posm[:, 0:4, :], ps[:, b, 0:64].rearrange("p (t e) -> p t e", t=4), 1.0, None, ALU.add)
                TS(posm[0:DEC_BATCH, 4, :], ps[0:DEC_BATCH, b, 64:80], 1.0, None, ALU.add)
                V.tensor_reduce(cnt[:, 0:1], ps[:, b, 80:96], AX.X, ALU.max)
                dve.drain()
                dve.sem_inc(quad_free[b // 4], 1)
                TT(posm[:], posm[:], rt[:, 5], ALU.mult)
                V.tensor_copy(cnt_i[:, bass.ds(l, 1)], cnt[:, 0:1])
                for r in range(PASSES):
                    TS(cnt[:, 1 + r:2 + r], cnt[:, 0:1], float(r * SLOTS), None, ALU.is_gt)
                dve.drain()
                TS(posm[:], posm[:], -1.0, None, ALU.add)
                V.tensor_reduce(cnt[:, 6:7], cnt[:, 1:6], AX.X, ALU.add)
                dve.drain()
                TT(passes_f[:], passes_f[:], cnt[:, 6:7], ALU.add)
                dve.drain()
                V.tensor_copy(passes_i[:, bass.ds(l + 1, 1)], passes_f[:])
                dve.drain()
                dve.sem_inc(s["routed"], 1)
                dve.sem_inc(s["passes_known"], 1)

                most = dve.value_load(cnt_i[0:1, bass.ds(l, 1)], min_val=0, max_val=TOK)
                wait_apart(dve, s["x_scaled"], (l + 1) * TILES)
                with dve.Fori(0, PASSES) as rnd:
                    with dve.If(most > rnd * SLOTS):
                        def build(n, g):
                            cols = bass.ds(g * 2, 2)
                            V.tensor_copy(pg[:], posm[:, :, cols])
                            V.tensor_copy(pc[:, 0], comb[:, :, cols])
                            dve.drain()
                            iota = table("slot").unsqueeze(1).to_broadcast([P, 2, SLOTS])
                            for t in range(TILES):
                                r = rows_of(t)
                                TT(Pm[0:r, t], iota[0:r], pg[0:r, t].unsqueeze(2).to_broadcast([r, 2, SLOTS]), ALU.is_equal)
                            dve.drain()
                            dve.sem_inc(s["p_built"], 1)
                            for i in range(3):
                                V.tensor_copy(cb3[:, :, :, i], pc[:, i % 2])
                                dve.drain()
                                if i < 2:
                                    TT(pc[:, (i + 1) % 2], pc[:, i % 2], cb3[:, :, :, i], ALU.subtract)
                                    dve.drain()
                            dve.sem_inc(s["cb_ready"], 1)

                        def gathered(n, ks):
                            for k in ks:
                                dve.wait_ge(s["gath_high"], n * (KC // 2) + k + 1)
                                TT(XeT[:, 1, 2 * k:2 * k + 2, :].rearrange("p k c -> p (k c)"), ps[:, k, :],
                                   XeT[:, 0, 2 * k:2 * k + 2, :].rearrange("p k c -> p (k c)").bitcast(f32), ALU.subtract)
                                dve.drain()
                                dve.sem_inc(s["gath_low"], 1)
                                dve.sem_inc(bank_free[k], 1)

                        def experts(g, last):
                            n = dve.snap((before + rnd) * PAIRS + g)
                            first = dve.snap(base + MIX_UNITS + rnd * PASS_UNITS + g * PAIR_UNITS)

                            def weights(k0, k1):
                                for k in range(k0, k1):
                                    low(first, PAIR_LOWS, k)

                            def gated(e):
                                dve.wait_ge(s["silu_done"], n * 2 + e + 1)
                                dve.wait_ge(s["w_used"], first + SPLIT_SLOTS + UP_DONE[e])
                                if e > 0:
                                    dve.wait_ge(s["ht_ps"], n * 2 + e)
                                STT(act_h[:], act_g[:], gsl[:, e:e + 1], ps[:, 2 * e + 1, :], ALU.mult, ALU.mult)
                                dve.drain()
                                dve.sem_inc(s["h_done"], 1)
                                dve.sem_inc(bank_free[2 * e + 1], 1)

                            def ht(e):
                                dve.wait_ge(s["ht_high"], n * 2 + e + 1)
                                TT(hT[:, 1].rearrange("p q c -> p (q c)"), ps[:, 4, :], hT[:, 0].rearrange("p q c -> p (q c)").bitcast(f32),
                                   ALU.subtract)
                                dve.drain()
                                dve.sem_inc(s["ht_low"], 1)
                                dve.sem_inc(bank_free[4], 1)

                            def out(e, half):
                                dve.wait_ge(s["ye_high"], n * 4 + 2 * e + half + 1)
                                hs = slice(half * 512, half * 512 + 512)
                                TT(ye[:, e, 1, hs], ps[:, 5 + half, :], ye[:, e, 0, hs].bitcast(f32), ALU.subtract)
                                dve.drain()
                                dve.sem_inc(s["ye_low"], 1)
                                dve.sem_inc(bank_free[5 + half], 1)

                            def next_weights(k0, k1):
                                for k in range(k0, k1):
                                    if not last:
                                        low(after_pair, PAIR_LOWS, k)

                            weights(6, 12)
                            dve.wait_ge(s["gs_ps"], n + 1)
                            V.tensor_reduce(gsl[:], ps[:, 6, 0:8].rearrange("p (e i) -> p e i", i=4)[:, :, 0:3], AX.X, ALU.add)
                            dve.drain()
                            dve.sem_inc(bank_free[6], 1)
                            gated(0)
                            weights(12, 14)
                            if not last:
                                build(n + 1, g + 1)
                            weights(14, 16)
                            ht(0)
                            weights(16, 20)
                            gated(1)
                            weights(20, 22)
                            out(0, 0)
                            weights(22, 24)
                            out(0, 1)
                            ht(1)
                            after_pair = dve.snap(first + PAIR_UNITS)
                            next_weights(0, 2)
                            if not last:
                                gathered(n + 1, (0, 1))
                            out(1, 0)
                            out(1, 1)
                            next_weights(2, 4)
                            if not last:
                                gathered(n + 1, (2, 3))
                            for i in range(2 * TILES):
                                if i in (2, 5):
                                    next_weights(4 + i // 4, 5 + i // 4)
                                t, hs = i // 2, slice((i % 2) * 512, (i % 2) * 512 + 512)
                                r = rows_of(t)
                                b = SCATTER_BANKS[i % 4]
                                dve.wait_ge(s["scat_ps"], n * 2 * TILES + i + 1)
                                TT(x[0:r, t, hs], ps[0:r, b, :], x[0:r, t, hs], ALU.add)
                                dve.drain()
                                dve.sem_inc(bank_free[b], 1)
                        n0 = dve.snap((before + rnd) * PAIRS)
                        build(n0, 0)
                        for k in range(EXPERT_SPLIT_SLOTS):
                            low(dve.snap(base + MIX_UNITS + rnd * PASS_UNITS), PAIR_LOWS, k)
                        gathered(n0, range(KC // 2))
                        with dve.Fori(0, PAIRS - 1) as g:
                            experts(g, False)
                        experts(PAIRS - 1, True)
                        TS(posm[:], posm[:], -float(SLOTS), None, ALU.add)
                        dve.drain()
                for i in range(2):
                    column_stats(i, 2)
                norm_stats(2, 2)
                dve.wait_ge(s["ln_loaded"], l * 64 + 64)
                for t in range(TILES):
                    dve.wait_ge(s["ln2_scaled"], l * TILES + t + 1)
                    gain(t, lngb2)
                    dve.sem_inc(s["x_tile_ready"], 1)


_IN = ["x_prompt", "x_sample", "state_rglru_h", "state_conv", "state_hgrn", "state_ret", "w_in", "conv_w", "conv_b",
       "w_rgate", "b_rgate", "w_igate", "b_igate", "rglru_lambda", "hgrn_lb_logits", "hgrn_norm_g", "w_out", "ln1_g",
       "ln1_b", "router_w", "router_b", "exp_w_gate", "exp_w_up", "exp_w_down", "ln2_g", "ln2_b"]
_OUT = [("y_prompt", (1, SEQ, D_MODEL)), ("y_sample", (DEC_BATCH, 1, D_MODEL)),
        ("h_prompt", (DEPTH, 1, D_A)), ("h_sample", (DEPTH, DEC_BATCH, D_A)),
        ("conv_prompt", (DEPTH, 1, CONV_W - 1, D_A)), ("conv_sample", (DEPTH, DEC_BATCH, CONV_W - 1, D_A)),
        ("hgrn_prompt", (DEPTH, 1, 4, DK_B, DK_B)), ("hgrn_sample", (DEPTH, DEC_BATCH, 4, DK_B, DK_B)),
        ("ret_prompt", (DEPTH, 1, C_HEADS, DK_C, DK_C)), ("ret_sample", (DEPTH, DEC_BATCH, C_HEADS, DK_C, DK_C))]


def kernel(**inputs):
    import concourse.bacc as bacc
    from concourse.bass_utils import run_bass_kernel_spmd
    nc = bacc.Bacc("TRN2", target_bir_lowering=False, num_devices=1)
    tables, levels, layer_flag = shape_tables()
    arrays = {n: np.ascontiguousarray(inputs[n]) for n in _IN}
    arrays.update(tables=tables, levels=levels, layer_flag=layer_flag)
    aps = {n: nc.dram_tensor(f"in_{n}", a.shape, mybir.dt.from_np(a.dtype), kind="ExternalInput").ap() for n, a in arrays.items()}
    outs = [nc.dram_tensor(f"out_{n}", shape, mybir.dt.float32, kind="ExternalOutput").ap() for n, shape in _OUT]
    build_program(nc, aps, outs)
    r = run_bass_kernel_spmd(nc, [{f"in_{n}": a for n, a in arrays.items()}], core_ids=[0])
    return tuple(r.results[0][f"out_{n}"] for n, _ in _OUT)
```
